# Optimizing a Trainium2 kernel written in Bass

```python
import math
import jax, jax.numpy as jnp
from jax import lax
import numpy as np

D_MODEL = 1024
BATCH = 1
SEQ = 512
DEPTH = 1

HEAD_DIM = 64
A_HEADS = 6
A_BRANCHES = ((128, 1), (512, 4), (2048, 16))
B_HEADS = 4
B_KEY_DIM = 32
B_VAL_DIM = 64
B_GATE_RANK = 16
B_GATE_TAU = 16.0
B_CHUNK = 16
C_HEADS = 6
C_BLOCK = 256
C_TOPK = 3
C_QCHUNK = 16
REL_BUCKETS = 32
REL_MAX_DIST = 2048
D_FF = 4 * D_MODEL
EPS = 1e-6
NEG_INF = -1e30

A_WIDTH = A_HEADS * HEAD_DIM
B_QK = B_HEADS * B_KEY_DIM
B_WIDTH = B_HEADS * B_VAL_DIM
C_WIDTH = C_HEADS * HEAD_DIM
MIX_WIDTH = A_WIDTH + B_WIDTH + C_WIDTH
IN_SIZES = (A_WIDTH, A_WIDTH, A_WIDTH, B_QK, B_QK, B_WIDTH, B_WIDTH, B_GATE_RANK, C_WIDTH, C_WIDTH, C_WIDTH)
IN_WIDTH = sum(IN_SIZES)


def rmsnorm(x, w):
    xf = x.astype(jnp.float32)
    y = xf * lax.rsqrt(jnp.mean(xf * xf, axis=-1, keepdims=True) + EPS)
    return (y * w.astype(jnp.float32)).astype(x.dtype)

def rel_bucket(dist):
    n = jnp.maximum(dist, 0)
    exact = REL_BUCKETS // 2
    logv = jnp.log(jnp.maximum(n, 1).astype(jnp.float32) / exact) / math.log(REL_MAX_DIST / exact)
    large = jnp.minimum(exact + (logv * (REL_BUCKETS - exact)).astype(jnp.int32), REL_BUCKETS - 1)
    return jnp.where(n < exact, n, large)

def dilated_branch(q, k, v, bias_a, window, dilation):
    Bsz, S, H, Dh = q.shape
    L = S // dilation
    span = window // dilation
    blk = min(span, L)
    nb = -(-L // blk)
    Lp = nb * blk

    def sub(t):
        t = t.reshape(Bsz, L, dilation, H, Dh).transpose(0, 2, 1, 3, 4)
        t = jnp.pad(t, ((0, 0), (0, 0), (0, Lp - L), (0, 0), (0, 0)))
        return t.reshape(Bsz, dilation, nb, blk, H, Dh)

    def with_prev(t):
        prev = jnp.pad(t, ((0, 0), (0, 0), (1, 0), (0, 0), (0, 0), (0, 0)))[:, :, :-1]
        return jnp.concatenate([prev, t], axis=3)

    qb = sub(q)
    kc = with_prev(sub(k))
    vc = with_prev(sub(v))
    logits = jnp.einsum('brnqhe,brnkhe->brnhqk', qb, kc, preferred_element_type=jnp.float32) * (Dh ** -0.5)

    steps = jnp.arange(blk)[:, None] + blk - jnp.arange(2 * blk)[None, :]
    band = (steps >= 0) & (steps <= span)
    key_ok = (jnp.arange(nb)[:, None] * blk + jnp.arange(2 * blk)[None, :] - blk) >= 0
    mask = band[None] & key_ok[:, None, :]
    bias = bias_a[:, rel_bucket(steps * dilation)].astype(jnp.float32)
    logits = jnp.where(mask[None, None, :, None], logits + bias[None, None, None], NEG_INF)

    lse = jax.nn.logsumexp(logits, axis=-1)
    p = jnp.exp(logits - lse[..., None])
    out = jnp.einsum('brnhqk,brnkhe->brnqhe', p.astype(v.dtype), vc)
    out = out.reshape(Bsz, dilation, Lp, H, Dh)[:, :, :L].transpose(0, 2, 1, 3, 4).reshape(Bsz, S, H, Dh)
    lse = lse.transpose(0, 1, 2, 4, 3).reshape(Bsz, dilation, Lp, H)[:, :, :L].transpose(0, 2, 1, 3).reshape(Bsz, S, H)
    return out.astype(jnp.float32), lse

def dilated_attention(q, k, v, bias_a):
    outs, lses = [], []
    for window, dilation in A_BRANCHES:
        o, l = dilated_branch(q, k, v, bias_a, window, dilation)
        outs.append(o)
        lses.append(l)
    wts = jax.nn.softmax(jnp.stack(lses), axis=0)
    out = jnp.einsum('gbsh,gbshe->bshe', wts, jnp.stack(outs))
    return out.astype(q.dtype)

def gla(q, k, v, r, a_lr, w_a2, b_a, norm_w):
    f32 = jnp.float32
    Bsz, S, H, dk = q.shape
    dv = v.shape[-1]
    C = B_CHUNK
    N = S // C
    log_a = jax.nn.log_sigmoid((a_lr @ w_a2 + b_a).astype(f32)) / B_GATE_TAU

    def chunks(t):
        return t.astype(f32).reshape(Bsz, N, C, H, -1).transpose(0, 3, 1, 2, 4)

    qc = chunks(q) * (dk ** -0.5)
    kc = chunks(k)
    vc = chunks(v)
    b = jnp.cumsum(chunks(log_a.reshape(Bsz, S, H, dk)), axis=3)

    causal = jnp.tril(jnp.ones((C, C), dtype=bool))
    diff = b[..., :, None, :] - b[..., None, :, :]
    decay = jnp.exp(jnp.where(causal[:, :, None], diff, NEG_INF))
    attn = jnp.einsum('bhnic,bhnjc,bhnijc->bhnij', qc, kc, decay)
    o_intra = jnp.einsum('bhnij,bhnjv->bhniv', attn, vc)

    b_last = b[..., -1, :]
    u = jnp.einsum('bhnjc,bhnjv->bhncv', kc * jnp.exp(b_last[..., None, :] - b), vc)

    def step(state, inp):
        dec, uu = inp
        return dec[..., None] * state + uu, state

    _, s_prev = lax.scan(step, jnp.zeros((Bsz, H, dk, dv), f32),
                         (jnp.moveaxis(jnp.exp(b_last), 2, 0), jnp.moveaxis(u, 2, 0)))
    s_prev = jnp.moveaxis(s_prev, 0, 2)
    o_inter = jnp.einsum('bhnic,bhncv->bhniv', qc * jnp.exp(b), s_prev)

    o = (o_intra + o_inter).transpose(0, 2, 3, 1, 4).reshape(Bsz, S, H, dv)
    o = o * lax.rsqrt(jnp.mean(o * o, axis=-1, keepdims=True) + EPS)
    o = o.reshape(Bsz, S, H * dv) * norm_w.astype(f32) * jax.nn.silu(r.astype(f32))
    return o.astype(q.dtype)

def moba_attention(q, k, v, bias_c):
    f32 = jnp.float32
    Bsz, S, H, Dh = q.shape
    nblk = -(-S // C_BLOCK)
    Sp = nblk * C_BLOCK

    def pad(t):
        return jnp.pad(t, ((0, 0), (0, Sp - S), (0, 0), (0, 0))).transpose(0, 2, 1, 3)

    qp, kp, vp = pad(q), pad(k), pad(v)
    kb = kp.reshape(Bsz, H, nblk, C_BLOCK, Dh)
    vb = vp.reshape(Bsz, H, nblk, C_BLOCK, Dh)
    k_mean = jnp.mean(kb.astype(f32), axis=3)

    qblk = jnp.arange(Sp) // C_BLOCK
    past = jnp.arange(nblk)[None, :] < qblk[:, None]
    gate = jnp.where(past, jnp.einsum('bhsd,bhnd->bhsn', qp.astype(f32), k_mean), NEG_INF)
    topk = min(C_TOPK, nblk)
    _, idx = lax.top_k(gate, topk)
    valid = idx < qblk[None, None, :, None]

    n_q = Sp // C_QCHUNK
    qch = qp.reshape(Bsz, H, n_q, C_QCHUNK, Dh).transpose(2, 0, 1, 3, 4)
    idxch = idx.reshape(Bsz, H, n_q, C_QCHUNK, topk).transpose(2, 0, 1, 3, 4)
    valch = valid.reshape(Bsz, H, n_q, C_QCHUNK, topk).transpose(2, 0, 1, 3, 4)
    b_ix = jnp.arange(Bsz)[:, None, None, None]
    h_ix = jnp.arange(H)[None, :, None, None]
    scale = Dh ** -0.5
    nsel = topk * C_BLOCK

    def one_chunk(args):
        ci, qc_, idx_, val_ = args
        qpos = ci * C_QCHUNK + jnp.arange(C_QCHUNK)
        ksel = kb[b_ix, h_ix, idx_].reshape(Bsz, H, C_QCHUNK, nsel, Dh)
        vsel = vb[b_ix, h_ix, idx_].reshape(Bsz, H, C_QCHUNK, nsel, Dh)
        kpos = (idx_[..., None] * C_BLOCK + jnp.arange(C_BLOCK)).reshape(Bsz, H, C_QCHUNK, nsel)
        l_sel = jnp.einsum('bhqd,bhqkd->bhqk', qc_, ksel, preferred_element_type=f32) * scale
        l_sel = l_sel + bias_c[h_ix, rel_bucket(qpos[None, None, :, None] - kpos)].astype(f32)
        l_sel = jnp.where(jnp.repeat(val_, C_BLOCK, axis=-1), l_sel, NEG_INF)
        own = (ci * C_QCHUNK) // C_BLOCK
        kown = lax.dynamic_slice_in_dim(kp, own * C_BLOCK, C_BLOCK, axis=2)
        vown = lax.dynamic_slice_in_dim(vp, own * C_BLOCK, C_BLOCK, axis=2)
        d_own = qpos[:, None] - (own * C_BLOCK + jnp.arange(C_BLOCK))[None, :]
        l_own = jnp.einsum('bhqd,bhkd->bhqk', qc_, kown, preferred_element_type=f32) * scale
        l_own = jnp.where(d_own[None, None] >= 0, l_own + bias_c[:, rel_bucket(d_own)].astype(f32)[None], NEG_INF)
        p = jax.nn.softmax(jnp.concatenate([l_sel, l_own], axis=-1), axis=-1)
        out = (jnp.einsum('bhqk,bhqkd->bhqd', p[..., :nsel].astype(vsel.dtype), vsel)
               + jnp.einsum('bhqk,bhkd->bhqd', p[..., nsel:].astype(vown.dtype), vown))
        return out

    outs = lax.map(one_chunk, (jnp.arange(n_q), qch, idxch, valch))
    return outs.transpose(1, 0, 3, 2, 4).reshape(Bsz, Sp, H, Dh)[:, :S]

def hybrid_layer(x, norm1_w, w_in, w_a2, b_a, gla_norm_w, w_out, norm2_w, w_ff1, w_ff2, rel_bias):
    Bsz, S, _ = x.shape
    h = rmsnorm(x, norm1_w)
    proj = h @ w_in
    aq, ak, av, bq, bk, bv, br, ba, cq, ck, cv = jnp.split(proj, list(np.cumsum(IN_SIZES)[:-1]), axis=-1)

    def heads(t, n):
        return t.reshape(Bsz, S, n, -1)

    bias_a = rel_bias[:, :A_HEADS].T
    bias_c = rel_bias[:, A_HEADS:].T
    y_a = dilated_attention(heads(aq, A_HEADS), heads(ak, A_HEADS), heads(av, A_HEADS), bias_a)
    y_b = gla(heads(bq, B_HEADS), heads(bk, B_HEADS), heads(bv, B_HEADS), br, ba, w_a2, b_a, gla_norm_w)
    y_c = moba_attention(heads(cq, C_HEADS), heads(ck, C_HEADS), heads(cv, C_HEADS), bias_c)
    mix = jnp.concatenate([y_a.reshape(Bsz, S, A_WIDTH), y_b, y_c.reshape(Bsz, S, C_WIDTH)], axis=-1)
    x = x + mix @ w_out

    h2 = rmsnorm(x, norm2_w)
    x = x + jnp.square(jax.nn.relu(h2 @ w_ff1)) @ w_ff2
    return x

def first_inputs(seed: int = 0) -> dict:
    key = jax.random.key(seed)
    ks = jax.random.split(key, 14)
    f32 = jnp.float32
    nrm = lambda k, shape, s: (jax.random.normal(k, shape, f32) * s)
    return {
        "x": nrm(ks[0], (BATCH, SEQ, D_MODEL), 1.0),
        "norm1_w": 1.0 + nrm(ks[1], (DEPTH, D_MODEL), 0.02),
        "w_in": nrm(ks[2], (DEPTH, D_MODEL, IN_WIDTH), D_MODEL ** -0.5),
        "gla_w_a2": nrm(ks[3], (DEPTH, B_GATE_RANK, B_QK), B_GATE_RANK ** -0.5),
        "gla_b_a": nrm(ks[4], (DEPTH, B_QK), 0.1),
        "gla_norm_w": 1.0 + nrm(ks[5], (DEPTH, B_WIDTH), 0.02),
        "w_out": nrm(ks[6], (DEPTH, MIX_WIDTH, D_MODEL), MIX_WIDTH ** -0.5),
        "norm2_w": 1.0 + nrm(ks[7], (DEPTH, D_MODEL), 0.02),
        "w_ff1": nrm(ks[8], (DEPTH, D_MODEL, D_FF), D_MODEL ** -0.5),
        "w_ff2": nrm(ks[9], (DEPTH, D_FF, D_MODEL), D_FF ** -0.5),
        "rel_bias": nrm(ks[10], (REL_BUCKETS, A_HEADS + C_HEADS), 0.2),
        "final_norm_w": 1.0 + nrm(ks[11], (D_MODEL,), 0.02),
    }

def first_block(x, norm1_w, w_in, gla_w_a2, gla_b_a, gla_norm_w, w_out, norm2_w, w_ff1, w_ff2, rel_bias, final_norm_w):
    for i in range(DEPTH):
        x = hybrid_layer(x, norm1_w[i], w_in[i], gla_w_a2[i], gla_b_a[i], gla_norm_w[i], w_out[i],
                         norm2_w[i], w_ff1[i], w_ff2[i], rel_bias)
    return rmsnorm(x, final_norm_w)


D_RNN = 1280
RNN_BLOCK = 64
N_RNN_BLOCKS = D_RNN // RNN_BLOCK
CONV_WIDTH = 4
LRU_C = 8.0
N_HEADS_MLA = 16
QK_NOPE = 64
QK_ROPE = 32
V_HEAD = 64
Q_LORA = 384
KV_LORA = 256
ROPE_THETA = 10000.0
Q_BLOCK = 128
D_FF_2 = 2816
FFN_CONV = 3
D_IN = D_RNN + Q_LORA + KV_LORA + QK_ROPE + 2 * D_MODEL


def rmsnorm_2(x, g):
    xf = x.astype(jnp.float32)
    y = xf * lax.rsqrt(jnp.mean(xf * xf, axis=-1, keepdims=True) + EPS)
    return (y * g.astype(jnp.float32)).astype(x.dtype)

def causal_dwconv(x, w, b):
    K = w.shape[0]
    S = x.shape[1]
    xp = jnp.pad(x, ((0, 0), (K - 1, 0), (0, 0)))
    y = xp[:, 0:S] * w[0]
    for k in range(1, K):
        y = y + xp[:, k:k + S] * w[k]
    return y + b

def rotary(x, positions):
    half = QK_ROPE // 2
    inv_freq = ROPE_THETA ** (-jnp.arange(half, dtype=jnp.float32) / half)
    ang = positions.astype(jnp.float32)[..., None] * inv_freq
    ang = ang.reshape(ang.shape[:2] + (1,) * (x.ndim - 3) + (half,))
    cos, sin = jnp.cos(ang), jnp.sin(ang)
    xf = x.astype(jnp.float32)
    x1, x2 = xf[..., :half], xf[..., half:]
    out = jnp.concatenate([x1 * cos - x2 * sin, x2 * cos + x1 * sin], axis=-1)
    return out.astype(x.dtype)

def rg_lru(xc, positions, w_a, b_a, w_x, b_x, lru_param):
    B, S, W = xc.shape
    xb = xc.reshape(B, S, N_RNN_BLOCKS, RNN_BLOCK)
    r = jax.nn.sigmoid(jnp.einsum('bsnd,nde->bsne', xb, w_a).reshape(B, S, W) + b_a)
    i = jax.nn.sigmoid(jnp.einsum('bsnd,nde->bsne', xb, w_x).reshape(B, S, W) + b_x)
    log_a = -LRU_C * r.astype(jnp.float32) * jax.nn.softplus(-lru_param.astype(jnp.float32))
    a = jnp.exp(log_a)
    mult = jnp.sqrt(-jnp.expm1(2.0 * log_a))
    reset = (positions == 0)[..., None]
    a = jnp.where(reset, 0.0, a)
    mult = jnp.where(reset, 1.0, mult)
    bterm = mult * (i * xc).astype(jnp.float32)

    def combine(lhs, rhs):
        a1, b1 = lhs
        a2, b2 = rhs
        return a1 * a2, a2 * b1 + b2

    _, h = lax.associative_scan(combine, (a, bterm), axis=1)
    return h.astype(xc.dtype)

def causal_block_attention(q, k, v):
    B, S, H, Dk = q.shape
    Dv = v.shape[-1]
    nb = S // Q_BLOCK
    scale = 1.0 / math.sqrt(Dk)
    qb = q.reshape(B, nb, Q_BLOCK, H, Dk).transpose(1, 0, 2, 3, 4)
    kpos = jnp.arange(S)

    def one_block(args):
        qi, blk = args
        s = jnp.einsum('bqhd,bkhd->bhqk', qi, k).astype(jnp.float32) * scale
        qpos = blk * Q_BLOCK + jnp.arange(Q_BLOCK)
        mask = kpos[None, :] <= qpos[:, None]
        s = jnp.where(mask[None, None], s, -jnp.inf)
        p = jax.nn.softmax(s, axis=-1).astype(v.dtype)
        return jnp.einsum('bhqk,bkhd->bqhd', p, v)

    o = lax.map(one_block, (qb, jnp.arange(nb)))
    return o.transpose(1, 0, 2, 3, 4).reshape(B, S, H * Dv)

def second_inputs(seed: int = 0) -> dict:
    key = jax.random.key(seed)
    ks = jax.random.split(key, 32)

    def nrm(k, shape, fan_in, mult=1.0):
        return jax.random.normal(k, shape, jnp.float32) * (mult * fan_in ** -0.5)

    def gain(k, shape):
        return 1.0 + 0.02 * jax.random.normal(k, shape, jnp.float32)

    def bias(k, shape):
        return 0.01 * jax.random.normal(k, shape, jnp.float32)

    L = DEPTH
    a0 = jax.random.uniform(ks[10], (L, D_RNN), jnp.float32, 0.9, 0.999)
    s0 = a0 ** (1.0 / LRU_C)
    lru_param = jnp.log(s0) - jnp.log1p(-s0)
    positions = (jnp.arange(SEQ, dtype=jnp.int32)[None, :]
                 + jax.random.randint(ks[31], (BATCH, 1), 0, SEQ, dtype=jnp.int32))
    return {
        "x": jax.random.normal(ks[0], (BATCH, SEQ, D_MODEL), jnp.float32),
        "c": jax.random.normal(ks[1], (BATCH, D_MODEL), jnp.float32),
        "positions": positions,
        "w_ada": nrm(ks[2], (L, D_MODEL, 6 * D_MODEL), D_MODEL, 0.5),
        "b_ada": bias(ks[3], (L, 6 * D_MODEL)),
        "norm1_g": gain(ks[4], (L, D_MODEL)),
        "w_in": nrm(ks[5], (L, D_MODEL, D_IN), D_MODEL),
        "conv_w": nrm(ks[6], (L, CONV_WIDTH, D_RNN), CONV_WIDTH),
        "conv_b": bias(ks[7], (L, D_RNN)),
        "w_gate_a": nrm(ks[8], (L, N_RNN_BLOCKS, RNN_BLOCK, RNN_BLOCK), RNN_BLOCK),
        "b_gate_a": bias(ks[9], (L, D_RNN)),
        "w_gate_x": nrm(ks[11], (L, N_RNN_BLOCKS, RNN_BLOCK, RNN_BLOCK), RNN_BLOCK),
        "b_gate_x": bias(ks[12], (L, D_RNN)),
        "lru_param": lru_param,
        "q_norm_g": gain(ks[13], (L, Q_LORA)),
        "w_uq": nrm(ks[14], (L, Q_LORA, N_HEADS_MLA * (QK_NOPE + QK_ROPE)), Q_LORA),
        "kv_norm_g": gain(ks[15], (L, KV_LORA)),
        "w_ukv": nrm(ks[16], (L, KV_LORA, N_HEADS_MLA * (QK_NOPE + V_HEAD)), KV_LORA),
        "w_proj_rnn": nrm(ks[17], (L, D_RNN, D_MODEL), D_RNN),
        "w_proj_mla": nrm(ks[18], (L, N_HEADS_MLA * V_HEAD, D_MODEL), N_HEADS_MLA * V_HEAD),
        "w_out": nrm(ks[19], (L, D_MODEL, D_MODEL), D_MODEL),
        "norm2_g": gain(ks[20], (L, D_MODEL)),
        "w_up": nrm(ks[21], (L, D_MODEL, 2 * D_FF_2), D_MODEL),
        "ffn_conv_w": nrm(ks[22], (L, FFN_CONV, 2 * D_FF_2), FFN_CONV),
        "ffn_conv_b": bias(ks[23], (L, 2 * D_FF_2)),
        "w_down": nrm(ks[24], (L, D_FF_2, D_MODEL), D_FF_2),
        "final_g": gain(ks[25], (D_MODEL,)),
    }

def second_block(x, c, positions, w_ada, b_ada, norm1_g, w_in, conv_w, conv_b,
              w_gate_a, b_gate_a, w_gate_x, b_gate_x, lru_param, q_norm_g, w_uq,
              kv_norm_g, w_ukv, w_proj_rnn, w_proj_mla, w_out, norm2_g, w_up,
              ffn_conv_w, ffn_conv_b, w_down, final_g):
    B, S, D = x.shape
    H = N_HEADS_MLA
    c_act = jax.nn.silu(c)
    for l in range(DEPTH):
        mod = c_act @ w_ada[l] + b_ada[l]
        shift1, scale1, gate1, shift2, scale2, gate2 = [m[:, None, :] for m in jnp.split(mod, 6, axis=-1)]

        h = rmsnorm_2(x, norm1_g[l]) * (1.0 + scale1) + shift1
        proj = h @ w_in[l]
        o0 = D_RNN
        o1 = o0 + Q_LORA
        o2 = o1 + KV_LORA
        o3 = o2 + QK_ROPE
        o4 = o3 + D_MODEL
        x_rnn, q_lat, kv_lat, k_rope, g_rnn, g_mla = (
            proj[..., :o0], proj[..., o0:o1], proj[..., o1:o2],
            proj[..., o2:o3], proj[..., o3:o4], proj[..., o4:])

        xc = causal_dwconv(x_rnn, conv_w[l], conv_b[l])
        y_rnn = rg_lru(xc, positions, w_gate_a[l], b_gate_a[l], w_gate_x[l], b_gate_x[l], lru_param[l])

        q = (rmsnorm_2(q_lat, q_norm_g[l]) @ w_uq[l]).reshape(B, S, H, QK_NOPE + QK_ROPE)
        q_rope = rotary(q[..., QK_NOPE:], positions)
        q = jnp.concatenate([q[..., :QK_NOPE], q_rope], axis=-1)
        kv = (rmsnorm_2(kv_lat, kv_norm_g[l]) @ w_ukv[l]).reshape(B, S, H, QK_NOPE + V_HEAD)
        k_nope, v = kv[..., :QK_NOPE], kv[..., QK_NOPE:]
        k_r = jnp.broadcast_to(rotary(k_rope, positions)[:, :, None, :], (B, S, H, QK_ROPE))
        k = jnp.concatenate([k_nope, k_r], axis=-1)
        y_mla = causal_block_attention(q, k, v)

        merged = (jax.nn.sigmoid(g_rnn) * (y_rnn @ w_proj_rnn[l])
                  + jax.nn.sigmoid(g_mla) * (y_mla @ w_proj_mla[l]))
        x = x + gate1 * (merged @ w_out[l])

        h2 = rmsnorm_2(x, norm2_g[l]) * (1.0 + scale2) + shift2
        u = causal_dwconv(h2 @ w_up[l], ffn_conv_w[l], ffn_conv_b[l])
        u_gate, u_val = u[..., :D_FF_2], u[..., D_FF_2:]
        x = x + gate2 * ((jax.nn.silu(u_gate) * u_val) @ w_down[l])

    return rmsnorm_2(x, final_g)


def setup_inputs(seed=0):
    out = dict(first_inputs(seed))
    for name, value in second_inputs(seed + 1).items():
        if name != "x":
            out[name + "_2"] = value
    return out


def reference(
    x, norm1_w, w_in, gla_w_a2, gla_b_a, gla_norm_w, w_out, norm2_w, w_ff1, w_ff2, rel_bias,
    final_norm_w, c_2, positions_2, w_ada_2, b_ada_2, norm1_g_2, w_in_2, conv_w_2, conv_b_2,
    w_gate_a_2, b_gate_a_2, w_gate_x_2, b_gate_x_2, lru_param_2, q_norm_g_2, w_uq_2,
    kv_norm_g_2, w_ukv_2, w_proj_rnn_2, w_proj_mla_2, w_out_2, norm2_g_2, w_up_2, ffn_conv_w_2,
    ffn_conv_b_2, w_down_2, final_g_2,
):
    x = first_block(
        x, norm1_w, w_in, gla_w_a2, gla_b_a, gla_norm_w, w_out, norm2_w, w_ff1, w_ff2, rel_bias,
        final_norm_w,
    )
    return second_block(
        x, c_2, positions_2, w_ada_2, b_ada_2, norm1_g_2, w_in_2, conv_w_2, conv_b_2,
        w_gate_a_2, b_gate_a_2, w_gate_x_2, b_gate_x_2, lru_param_2, q_norm_g_2, w_uq_2,
        kv_norm_g_2, w_ukv_2, w_proj_rnn_2, w_proj_mla_2, w_out_2, norm2_g_2, w_up_2,
        ffn_conv_w_2, ffn_conv_b_2, w_down_2, final_g_2,
    )


_drawn_inputs = setup_inputs


def setup_inputs(seed=0):
    import zlib

    import numpy as np

    out = dict(_drawn_inputs(seed))
    spreads = {}
    factors = {'norm1_w': 3.622,
     'gla_b_a': 4.137,
     'gla_norm_w': 8.0,
     'norm2_w': 3.366,
     'final_norm_w': 2.829,
     'b_ada_2': 3.409,
     'norm1_g_2': 8.0,
     'conv_b_2': 7.486,
     'b_gate_a_2': 64.0,
     'b_gate_x_2': 64.0,
     'q_norm_g_2': 8.0,
     'w_uq_2': 3.319,
     'kv_norm_g_2': 8.0,
     'norm2_g_2': 8.0,
     'ffn_conv_b_2': 33.593,
     'final_g_2': 7.708}
    for name, (base, spread) in spreads.items():
        noise = np.random.default_rng([zlib.crc32(name.encode()), seed]).standard_normal(out[name].shape)
        drawn = base * np.exp(spread * noise) if base else spread * noise
        out[name] = __import__('jax').numpy.asarray(drawn.astype(out[name].dtype))
    for name, factor in factors.items():
        out[name] = (out[name] * factor).astype(out[name].dtype)
    return out
```

```python
import math
from contextlib import ExitStack

import numpy as np

import concourse.bass as bass
from concourse import mybir

F32 = mybir.dt.float32
F32R = mybir.dt.float32r
I32 = mybir.dt.int32
ACT = mybir.ActivationFunctionType
ALU = mybir.AluOpType
AX_X = mybir.AxisListType.X
ds = bass.ds

P = 128
SEQ = 512
D_MODEL = 1024
KT = D_MODEL // P
TB = SEQ // P
EPS = 1e-6
NEG = -1e30
BIG = 3e38

HEAD_DIM = 64
A_HEADS = C_HEADS = 6
A_BRANCHES = ((128, 1), (512, 4), (2048, 16))
B_HEADS, B_KEY, B_VAL, B_RANK, B_TAU = 4, 32, 64, 16, 16.0
REL_BUCKETS, REL_MAX_DIST = 32, 2048
A_W, C_W, B_QK, B_W = A_HEADS * HEAD_DIM, C_HEADS * HEAD_DIM, B_HEADS * B_KEY, B_HEADS * B_VAL
COL_AQ, COL_AK, COL_AV = 0, A_W, 2 * A_W
COL_B = 3 * A_W
COL_CQ = COL_B + 2 * B_QK + 2 * B_W + B_RANK
COL_CK, COL_CV = COL_CQ + C_W, COL_CQ + 2 * C_W
NB_B = 7
PAIRS = (A_HEADS + C_HEADS) // 2
TAB = SEQ + P
GLA_GROUP = 4
GLA_GROUPS = B_VAL // GLA_GROUP
FF_GROUPS = 4 * D_MODEL // D_MODEL
ADA_COLS = 6 * D_MODEL // KT

D_RNN, RNN_BLOCK, CONV_W, LRU_C = 1280, 64, 4, 8.0
RT = D_RNN // P
N_MLA, NOPE, ROPE, VH, Q_LORA, KV_LORA = 16, 64, 32, 64, 384, 256
QKD = NOPE + ROPE
QT, KVT = Q_LORA // P, KV_LORA // P
ROPE_THETA = 10000.0
D_FF2, FFN_CONV = 2816, 3
FT = D_FF2 // P
COL_LAT, COL_ROPE, COL_GATE = D_RNN, D_RNN + Q_LORA + KV_LORA, D_RNN + Q_LORA + KV_LORA + ROPE
DOWN_KS = (8, 7, 7)
RNN_KS = (5, 5)

VEC_GROUPS = [
    [("norm1_w", 8), ("norm2_w", 8), ("final_norm_w", 8), ("gla_norm_w", 2), ("gla_b_a", 1), ("norm1_g_2", 8),
     ("q_norm_g_2", 3), ("kv_norm_g_2", 2), ("norm2_g_2", 8), ("final_g_2", 8), ("c_2", 8),
     ("conv_b_2", 10), ("b_gate_a_2", 10), ("b_gate_x_2", 10), ("lru_param_2", 10)],
    [("conv_w_2", 40), ("b_ada_2", 48)],
    [("ffn_conv_w0", 44), ("ffn_conv_w1", 44)],
    [("ffn_conv_w2", 44), ("ffn_conv_b_2", 44)],
]
VEC = {}
VEC_ROWS = []
_at = 0
for _g in VEC_GROUPS:
    VEC_ROWS.append((_at, sum(n for _, n in _g)))
    for _name, _n in _g:
        VEC[_name] = _at
        _at += _n
N_VEC = _at

C_IDENT, C_STRIP = 0, P
C_HEADSUM = C_STRIP + SEQ
C_INVF = C_HEADSUM + B_HEADS
C_PHASE, C_TURN, C_EPS = C_INVF + 1, C_INVF + 2, C_INVF + 3
N_CONST = C_INVF + 4


def shape_constants():
    f32 = np.float32
    j = np.arange(TAB)
    dist = SEQ - 1 - j
    n = np.maximum(dist, 0)
    exact = REL_BUCKETS // 2
    logv = np.log(np.maximum(n, 1).astype(f32) / f32(exact)) / f32(math.log(REL_MAX_DIST / exact))
    large = np.minimum(exact + (logv * f32(REL_BUCKETS - exact)).astype(np.int32), REL_BUCKETS - 1)
    bucket = np.where(n < exact, n, large)
    onehot = (bucket[None, :] == np.arange(REL_BUCKETS)[:, None]).astype(f32)
    visits = np.zeros(TAB)
    for window, dilation in A_BRANCHES:
        visits += (dist >= 0) & (dist <= window) & (dist % dilation == 0)
    scale = math.sqrt(HEAD_DIM)
    mask_a = np.where(visits > 0, scale * np.log(np.maximum(visits, 1)), NEG)
    mask_c = np.where(dist >= 0, 0.0, NEG)
    mask = np.concatenate([np.tile(mask_a, (A_HEADS, 1)), np.tile(mask_c, (C_HEADS, 1))]).astype(f32)
    c = np.zeros((P, N_CONST), f32)
    p = np.arange(P)
    c[:, C_IDENT:C_IDENT + P] = np.eye(P)
    d = (SEQ - P) + p[:, None] - np.arange(SEQ)[None, :]
    c[:, C_STRIP:C_STRIP + SEQ] = np.where(d >= 0, 0.0, NEG)
    c[p, C_HEADSUM + p // B_KEY] = 1.0
    half = ROPE // 2
    rate = ROPE_THETA ** (-np.arange(half) / half)
    c[NOPE:, C_INVF] = np.concatenate([rate, rate, -rate, rate])
    c[:NOPE + ROPE, C_PHASE] = math.pi / 2
    c[:NOPE + ROPE, C_TURN] = 0.25
    c[:, C_EPS] = EPS
    return {"const_tile": c, "const_onehot": onehot, "const_mask": mask}


def repeat(eng, n, body):
    if n == 1:
        body(0)
    elif n > 1:
        with eng.Fori(0, n) as i:
            body(i)


def peeled(eng, n, body):
    body(0)
    repeat(eng, n - 1, lambda i: body(i + 1))


class Steps:

    def __init__(self, eng, sem):
        self.eng, self.sem, self.before, self.k, self.at, self.inside = eng, sem, 0, 0, 0, False

    def enter(self, i, per):
        if not self.inside:
            self.before += self.k
        self.k, self.at, self.per, self.inside = 0, per * i, per, True

    def leave(self, rounds):
        assert self.k == self.per, (self.k, self.per)
        self.before, self.k, self.at, self.inside = self.before + self.per * rounds, 0, 0, False

    def done(self, ins):
        self.k += 1
        ins.then_inc(self.sem, 1)
        self.eng.wait_ge(self.sem, self.at + (self.before + self.k))


class Phase:

    slots = 0
    blocks = 0

    def __init__(self, nb, ks=(KT,), counted=True):
        assert counted or nb % 2 == 0
        self.n0, self.b0, self.nb, self.ks = Phase.slots, Phase.blocks, nb, ks
        Phase.slots += nb * len(ks)
        Phase.blocks += nb * counted

    def slot(self, n):
        return (self.n0 + n) % 2

    def bank(self, b):
        return (self.b0 + b) % 2


def hybrid_stack(nc, io, out):
    Phase.slots = Phase.blocks = 0
    ctx = ExitStack()
    with ctx:
        sems = {}

        def S(name):
            if name not in sems:
                sems[name] = ctx.enter_context(nc.semaphore(name))
            return sems[name]

        top = [-(-nc.sbuf_base // 64) * 64]

        def place(name, shape, offset, dt=F32):
            return nc.alloc_sbuf_tensor_at(name, shape, dt, offset=offset)

        def size(shape):
            return 4 * int(np.prod(shape[1:]))

        def keep(name, shape, dt=F32):
            t = place(name, shape, top[0], dt)
            top[0] += -(-size(shape) // 64) * 64
            return t

        xT = keep("xT", [P, KT, SEQ])
        actH = keep("actH", [P, KT, SEQ], F32R)
        actL = keep("actL", [P, KT, SEQ], F32R)
        Wraw = [keep(f"Wraw{i}", [P, KT, P]) for i in range(2)]
        WH = [keep(f"WH{i}", [P, KT, P], F32R) for i in range(2)]
        WL = [keep(f"WL{i}", [P, KT, P], F32R) for i in range(2)]
        const = keep("const", [P, N_CONST])
        ones = keep("ones", [P, P])
        vec = keep("vec", [P, N_VEC])
        cact = keep("cact", [P, KT])
        mod = keep("mod", [P, 6 * KT])
        gainA = keep("gainA", [P, 2, KT])
        nsp = keep("nsp", [P, 2, RT])
        stat = keep("stat", [P, 4, 2, TB])
        rstd = keep("rstd", [P, SEQ])
        T = [keep(f"T{i}", [P, SEQ]) for i in range(6)]
        R = top[0]
        END = nc.sbuf_usable_end

        ident = const[:, C_IDENT:C_IDENT + P]
        strip = const[:, C_STRIP:C_STRIP + SEQ]
        headsum = const[:, C_HEADSUM:C_HEADSUM + B_HEADS]
        epsc = const[:, C_EPS:C_EPS + 1]

        def region(specs, start=R):
            made, at = [], start
            for name, shape, dt in specs:
                made.append(place(name, shape, at, dt))
                at += -(-size(shape) // 64) * 64
            assert at <= END, (at, END)
            return made

        bT, qT, kT, Vt, alpha, oTok, oSq, Z, Qs, Ks, Vs, vb, kvp, scanned, qs = region([
            ("bT", [P, NB_B, SEQ], F32), ("qT", [P, PAIRS, SEQ], F32), ("kT", [P, PAIRS, SEQ], F32),
            ("Vt", [P, PAIRS, TB, P], F32), ("alpha", [P, SEQ], F32), ("oTok", [P, TB, B_W], F32),
            ("oSq", [P, TB, B_W], F32), ("Z", [P, 2, SEQ], F32),
            ("Qs", [P, SEQ], F32), ("Ks", [P, SEQ], F32), ("Vs", [P, TB, P], F32),
            ("vb", [P, 2, GLA_GROUP, SEQ], F32), ("kvp", [P, 2, SEQ], F32), ("scanned", [P, 2, SEQ], F32),
            ("qs", [P, GLA_GROUP, SEQ], F32)])
        vb0 = R + sum(size(t.shape) for t in (bT, qT, kT, Vt, alpha, oTok, oSq, Z, Qs, Ks, Vs))
        (LP,) = region([("LP", [P, 2, TB * (TB + 1) // 2 * P], F32)], vb0)
        (PT,) = region([("PT", [P, TB, SEQ], F32)], vb0 + size(vb.shape) + size(kvp.shape) + size(scanned.shape))
        xn, vrows, onehot, maskt, relb, tabs, wa2 = region([
            ("xn", [P, TB, D_MODEL], F32), ("vrows", [P, len(VEC_GROUPS), P], F32), ("onehot", [REL_BUCKETS, TAB], F32),
            ("maskt", [2 * PAIRS, TAB], F32), ("relb", [REL_BUCKETS, 2 * PAIRS], F32), ("tabs", [2 * PAIRS, TAB], F32),
            ("wa2", [B_RANK, B_QK], F32)], R + size(bT.shape))
        UH, UL, adaacc = region([
            ("UH", [P, FT, SEQ], F32R), ("UL", [P, FT, SEQ], F32R), ("adaacc", [P, 6 * D_MODEL], F32)])
        (wada,) = region([("wada", [P, 2, ADA_COLS], F32)], R + size([P, 2 * KT, SEQ]))
        tailH, tailL, rest = R + size([P, RT, SEQ]), R + size(UH.shape) + size([P, RT, SEQ]), R + 2 * size(UH.shape)
        gR, PT2 = region([("gR", [P, KT, SEQ], F32), ("PT2", [P, TB, SEQ], F32)], tailH)
        posr, BDa, BDx = region([("posr", [P, SEQ], I32), ("BDa", [P, 2, P], F32), ("BDx", [P, 2, P], F32)],
                                tailH + size(gR.shape))
        gM, Qp, Kp = region([("gM", [P, KT, SEQ], F32), ("Qp", [P, 2, SEQ], F32), ("Kp", [P, 2, SEQ], F32)], tailL)
        xc, rA, rTh = region([("xc", [P, RT, SEQ], F32), ("rA", [P, 2, SEQ], F32), ("rTh", [P, 2, SEQ], F32)], rest)
        LP2, lat, Vp, CS = region([
            ("LP2", [P, 2, TB * (TB + 1) // 2 * P], F32), ("lat", [P, QT + KVT, SEQ], F32),
            ("Vp", [P, 2, TB, VH], F32), ("CS", [P, SEQ], F32)], rest)
        posb, rotk, rott = region([("posb", [P, SEQ], I32), ("rotk", [P, SEQ], F32), ("rott", [P, SEQ], F32)], rest)
        cg, cv, act2 = region([("cg", [P, 2, SEQ], F32), ("cv", [P, 2, SEQ], F32), ("act2", [P, 2, SEQ], F32)], rest)
        yout, yrow = region([("yout", [P, KT, SEQ], F32), ("yrow", [P, TB, D_MODEL], F32)])

        ps = ctx.enter_context(nc.psum_tensor("ps", [P, 8, SEQ], F32))
        tab_dram = nc.dram_tensor("tab_dram", [2 * PAIRS, TAB], F32, kind="Internal").ap()
        strip_dram = nc.dram_tensor("strip_dram", [2 * PAIRS, P, SEQ], F32, kind="Internal").ap()
        bv_dram = nc.dram_tensor("bv_dram", [B_W, SEQ], F32, kind="Internal").ap()

        gB = Phase(NB_B)
        gQK = Phase(4 * PAIRS // 2)
        gV = Phase(PAIRS)
        gOut = Phase(KT)
        gFF = [(Phase(KT, counted=False), Phase(KT, counted=False)) for _ in range(FF_GROUPS)]
        gX = Phase(RT)
        gGate = Phase(2 * KT, counted=False)
        gPR = Phase(KT, RNN_KS)
        gLat = Phase(QT + KVT)
        gRope = Phase(1)
        gHead = Phase(N_MLA, counted=False)
        gPM = Phase(KT)
        gOut2 = Phase(KT)
        gUp = Phase(2 * FT, counted=False)
        gDown = Phase(KT, DOWN_KS)

        s_raw = [S("raw0_loaded"), S("raw1_loaded")]
        s_hi, s_lo = S("weights_high"), S("weights_low")
        s_mm = S("block_multiplied")
        s_ev = S("block_evacuated")
        def wcols(name, rows0, kts):
            return io[name][rows0:rows0 + kts * P, :].rearrange("(k p) c -> p k c", p=P)

        loads = {}
        slot_base = {}
        total = [0, 0]
        for ph, dmas in ([(gB, 1), (gQK, 1), (gV, 1), (gOut, 3)] + [(g, 1) for pair in gFF for g in pair]
                         + [(gX, 1), (gGate, 1), (gPR, 1), (gLat, 1), (gRope, 3), (gHead, 4), (gPM, 1), (gOut2, 1),
                            (gUp, 1), (gDown, 1)]):
            loads[ph] = dmas
            slot_base[ph] = list(total)
            for n in range(ph.nb * len(ph.ks)):
                total[ph.slot(n)] += 16 * dmas

        def landed(ph, j, i=0, per=2):
            slot = ph.slot(j)
            k = len([x for x in range(j + 1) if ph.slot(x) == slot])
            return s_raw[slot], i * (16 * loads[ph] * (per // 2)) + (slot_base[ph][slot] + 16 * loads[ph] * k)

        FF_SLOTS = 2 * KT

        block = ctx.enter_context(nc.Block())

        @block.sync
        def _(sp):
            def load(n, slot, pieces):
                if not isinstance(n, int) or n >= 2:
                    sp.wait_ge(s_lo, n - 1)
                for dst, src in pieces:
                    sp.dma_start(dst, src).then_inc(s_raw[slot], 16)

            def stream(ph, per, rounds, piece, first=0):
                def body(i):
                    for j in range(per):
                        slot = ph.slot(first + j)
                        load(per * i + (ph.n0 + first + j), slot, piece(i, j, slot))
                (repeat if ph.n0 else peeled)(sp, rounds, body)

            def cols(view, kts, at):
                return lambda i, j, slot: [(Wraw[slot][:, 0:kts, :], view[:, :, ds(at(i, j), P)])]

            sp.dma_start(xn[:], io["x"][0].rearrange("(t p) d -> p t d", p=P)).then_inc(S("x_loaded"), 16)
            sp.dma_start(const[:], io["const_tile"]).then_inc(S("const_loaded"), 16)
            for g, names in enumerate(VEC_GROUPS):
                r = 0
                for name, n in names:
                    if name.startswith("ffn_conv_w"):
                        src = io["ffn_conv_w_2"][int(name[-1])]
                    elif name == "conv_w_2":
                        src = io[name].rearrange("k c -> (k c)")
                    else:
                        src = io[name]
                    sp.dma_start(vrows[r:r + n, g, :], src.rearrange("(r c) -> r c", c=P)).then_inc(S("vec_loaded"), 16)
                    r += n
            for dst, src in ((onehot, io["const_onehot"]), (maskt, io["const_mask"]), (relb, io["rel_bias"]),
                             (wa2, io["gla_w_a2"])):
                sp.dma_start(dst[:], src).then_inc(S("tables_loaded"), 16)
            w_in = wcols("w_in", 0, KT)
            stream(gB, 2, NB_B // 2, cols(w_in, KT, lambda i, j: 2 * P * i + (COL_B + P * j)))
            stream(gB, 1, 1, cols(w_in, KT, lambda i, j: COL_B + P * (NB_B - 1)), first=NB_B - 1)
            sp.wait_ge(S("tabs_ready"), 2)
            sp.dma_start(tab_dram, tabs[:]).then_inc(S("tab_stored"), 16)
            sp.wait_ge(S("tab_stored"), 16)
            sp.dma_start(strip_dram, bass.AP(tab_dram.tensor, P - 1, [[TAB, 2 * PAIRS], [-1, P], [1, SEQ]])
                         ).then_inc(S("strips_stored"), 16)
            sp.wait_ge(S("strips_stored"), 16)

            def strip(s, par):
                if not isinstance(s, int) or s >= 2:
                    sp.wait_ge(S("a_logits"), 4 * s - 4)
                sp.dma_start(Z[:, par, :], strip_dram[ds(s, 1), :, :].rearrange("h p j -> (h p) j")
                             ).then_inc(S(f"strip_loaded{par}"), 16)
            strip(0, 0)
            strip(1, 1)
            sp.wait_ge(s_ev, gB.b0 + 4)
            sp.dma_start(bv_dram.rearrange("(k p) t -> p k t", p=P), bT[:, 2:4, :]).then_inc(S("bv_stored"), 16)
            sp.wait_ge(S("bv_stored"), 16)

            def gla_values(g, par):
                if not isinstance(g, int) or g >= 2:
                    sp.wait_ge(S("gla_kv"), GLA_GROUP * g - GLA_GROUP)
                for h in range(B_HEADS):
                    src = bv_dram[ds(h * B_VAL + GLA_GROUP * g, GLA_GROUP), :].rearrange("v t -> (v t)")
                    sp.dma_start(vb[h * B_KEY:(h + 1) * B_KEY, par, :, :].rearrange("p v t -> p (v t)"),
                                 src.unsqueeze(0).to_broadcast([B_KEY, GLA_GROUP * SEQ])
                                 ).then_inc(S(f"gla_values{par}"), 16)

            bases = (COL_AQ, COL_AK, COL_CQ, COL_CK)
            gla_values(0, 0)
            gla_values(1, 1)
            stream(gQK, 4, 1, lambda i, j, slot: [(Wraw[slot][:], w_in[:, :, bases[j]:bases[j] + P])])
            for g in (2, 3):
                gla_values(g, g % 2)

            def qk_round(i):
                for j in range(4):
                    slot = gQK.slot(j)
                    load(4 * i + (gQK.n0 + 4 + j), slot, [(Wraw[slot][:], w_in[:, :, ds(P * i + (bases[j] + P), P)])])
                    gla_values(4 * i + (4 + j), j % 2)
            repeat(sp, 2, qk_round)

            def v_round(i):
                for j, base in enumerate((COL_AV, COL_CV)):
                    slot = gV.slot(j)
                    load(2 * i + (gV.n0 + j), slot, [(Wraw[slot][:], w_in[:, :, ds(P * i + base, P)])])
            repeat(sp, PAIRS // 2, v_round)
            for g in range(4 * PAIRS // 2, GLA_GROUPS):
                gla_values(g, g % 2)
            w_out = wcols("w_out", 0, KT)
            a, b = A_W // P, (A_W + B_W) // P

            def out_blocks(i0):
                return lambda i, j, slot: [
                    (Wraw[slot][:, 0:a, :], w_out[:, 0:a, ds(2 * P * i + P * (2 * i0 + j), P)]),
                    (Wraw[slot][:, a:2 * a, :], w_out[:, b:KT, ds(2 * P * i + P * (2 * i0 + j), P)]),
                    (Wraw[slot][:, 2 * a:KT, :], w_out[:, a:b, ds(2 * P * i + P * (2 * i0 + j), P)])]
            stream(gOut, 2, 2, out_blocks(0))

            def strip_pair(p):
                for par in range(2):
                    strip(2 * p + (2 + par), par)
            repeat(sp, PAIRS - 1, strip_pair)
            stream(gOut, 2, KT // 2 - 2, out_blocks(2), first=4)
            ff1 = wcols("w_ff1", 0, KT)
            ff2 = io["w_ff2"].rearrange("(g k p) c -> g p k c", k=KT, p=P)
            ada = io["w_ada_2"].rearrange("(k p) (m c) -> k p m c", p=P, c=ADA_COLS)
            sp.wait_ge(S("a_low"), PAIRS)

            def ff_group(o):
                for gi in range(2):
                    for half in range(2):
                        ph = gFF[gi][half]

                        def body(p, gi=gi, half=half, ph=ph):
                            for j in range(2):
                                slot = ph.slot(j)
                                if half == 0:
                                    src = ff1[:, :, ds(2 * KT * P * o + 2 * P * p + (KT * P * gi + P * j), P)]
                                else:
                                    src = ff2[ds(2 * o + gi, 1), :, :, ds(2 * P * p + P * j, P)].rearrange(
                                        "g p k c -> (g p) k c")
                                load(2 * FF_SLOTS * o + 2 * p + (ph.n0 + j), slot, [(Wraw[slot][:], src)])
                            for j in range(2):
                                c = 4 * KT * o + 2 * p + (2 * KT * gi + KT * half + j)
                                sp.wait_ge(S("ada_used"), c)
                                sp.dma_start(wada[:, j, :], ada[ds(4 * o + (2 * gi + half), 1), :, ds(2 * p + j, 1), :]
                                             .rearrange("k p m c -> (k p) (m c)")).then_inc(S(f"ada_loaded{j}"), 16)
                        repeat(sp, KT // 2, body)
            repeat(sp, FF_GROUPS // 2, ff_group)
            w_in2 = wcols("w_in_2", 0, KT)
            wga = io["w_gate_a_2"].rearrange("(t b) d e -> t b d e", b=2)
            wgx = io["w_gate_x_2"].rearrange("(t b) d e -> t b d e", b=2)

            def rnn_gates(t, par):
                if not isinstance(t, int) or t >= 2:
                    sp.wait_ge(S("rnn_gated"), t - 1)
                for w, bd in ((wga, BDa), (wgx, BDx)):
                    for b in range(2):
                        q = slice(b * RNN_BLOCK, (b + 1) * RNN_BLOCK)
                        sp.dma_start(bd[q, par, q], w[ds(t, 1), b, :, :].rearrange("t d e -> (t d) e")
                                     ).then_inc(S(f"rnn_weights{par}"), 16)

            stream(gX, 2, 1, cols(w_in2, KT, lambda i, j: P * j))
            sp.wait_ge(S("bd_cleared"), 2)
            sp.dma_start(posr[:], io["positions_2"].to_broadcast([P, SEQ])).then_inc(S("reset_loaded"), 16)
            rnn_gates(0, 0)
            rnn_gates(1, 1)

            def x_round(p):
                for j in range(2):
                    slot = gX.slot(j)
                    load(2 * p + (gX.n0 + 2 + j), slot, [(Wraw[slot][:], w_in2[:, :, ds(2 * P * p + (2 + j) * P, P)])])
                for j in range(2):
                    rnn_gates(2 * p + (2 + j), j)
            repeat(sp, RT // 2 - 1, x_round)
            stream(gGate, 2, KT, cols(w_in2, KT, lambda i, j: 2 * P * i + (COL_GATE + P * j)))
            sp.wait_ge(S("rnn_low"), RT)
            sp.dma_start(posb[:], io["positions_2"].to_broadcast([P, SEQ])).then_inc(S("pos_loaded"), 16)
            wpr = io["w_proj_rnn_2"].rearrange("(q k p) c -> q p k c", k=RNN_KS[0], p=P)
            stream(gPR, 4, KT // 2, lambda i, j, slot: [
                (Wraw[slot][:, 0:RNN_KS[0], :], wpr[j % 2][:, :, ds(2 * P * i + P * (j // 2), P)])])
            stream(gLat, 2, (QT + KVT) // 2, cols(w_in2, KT, lambda i, j: 2 * P * i + (COL_LAT + P * j)))
            stream(gLat, 1, 1, cols(w_in2, KT, lambda i, j: COL_LAT + P * (QT + KVT - 1)), first=QT + KVT - 1)
            half = ROPE // 2
            stream(gRope, 1, 1, lambda i, j, slot: [
                (Wraw[slot][:, :, 0:QKD], w_in2[:, :, COL_ROPE - NOPE:COL_ROPE + ROPE]),
                (Wraw[slot][:, :, QKD:QKD + half], w_in2[:, :, COL_ROPE + half:COL_ROPE + ROPE]),
                (Wraw[slot][:, :, QKD + half:P], w_in2[:, :, COL_ROPE:COL_ROPE + half])])
            wuq, wukv = wcols("w_uq_2", 0, QT), wcols("w_ukv_2", 0, KVT)
            stream(gHead, 2, N_MLA // 2, lambda i, j, slot: [
                (Wraw[slot][:, 0:QT, 0:QKD], wuq[:, :, ds(2 * QKD * i + QKD * j, QKD)]),
                (Wraw[slot][:, 0:QT, QKD:QKD + half], wuq[:, :, ds(2 * QKD * i + (QKD * j + NOPE + half), half)]),
                (Wraw[slot][:, 0:QT, QKD + half:P], wuq[:, :, ds(2 * QKD * i + (QKD * j + NOPE), half)]),
                (Wraw[slot][:, QT:QT + KVT, :], wukv[:, :, ds(2 * P * i + P * j, P)])])
            stream(gPM, 2, KT // 2, cols(wcols("w_proj_mla_2", 0, KT), KT, lambda i, j: 2 * P * i + P * j))
            stream(gOut2, 2, KT // 2, cols(wcols("w_out_2", 0, KT), KT, lambda i, j: 2 * P * i + P * j))
            stream(gUp, 2, FT, cols(wcols("w_up_2", 0, KT), KT, lambda i, j: P * i + D_FF2 * j))
            downs, r = [], 0
            for k in DOWN_KS:
                downs.append(wcols("w_down_2", r * P, k))
                r += k
            stream(gDown, 2 * len(DOWN_KS), KT // 2, lambda i, j, slot: [
                (Wraw[slot][:, 0:DOWN_KS[j % 3], :], downs[j % 3][:, :, ds(2 * P * i + P * (j // 3), P)])])
            sp.wait_ge(S("rows_ready"), KT)
            sp.dma_start(out[0].rearrange("(t p) d -> p t d", p=P), yrow[:]).then_inc(S("stored"), 16)
            sp.wait_ge(S("stored"), 16)

        @block.gpsimd
        def _(pool):
            def low(n, slot, kts=KT):
                pool.wait_ge(s_hi, n + 1)
                nc.gpsimd.tensor_tensor(WL[slot][:, 0:kts, :], Wraw[slot][:, 0:kts, :],
                                        WH[slot][:, 0:kts, :].bitcast(F32), ALU.subtract).then_inc(s_lo, 1)

            def lows(ph, per, rounds, first=0, extra=0):
                def body(i):
                    for j in range(per):
                        low((per + extra) * i + (ph.n0 + first + j), ph.slot(first + j), ph.ks[(first + j) % len(ph.ks)])
                repeat(pool, rounds, body)

            nc.gpsimd.memset(ones[:], 1.0).then_inc(S("ones_set"), 1)
            lows(gB, 2, NB_B // 2)
            lows(gB, 1, 1, first=NB_B - 1)

            def gla_products(g, par):
                pool.wait_ge(S(f"gla_values{par}"), (g // 2 + 1) * 64 if isinstance(g, int) else (g - par) * 32 + 64)
                for j in range(GLA_GROUP):
                    if not isinstance(g, int) or g > 0 or j >= 2:
                        pool.wait_ge(S("gla_scanned"), GLA_GROUP * g + (j - 1))
                    nc.gpsimd.tensor_tensor(kvp[:, j % 2, :], bT[:, 1, :], vb[:, par, j, :],
                                            ALU.mult).then_inc(S("gla_kv"), 1)

            for j in range(4):
                low(gQK.n0 + j, gQK.slot(j))
                gla_products(j, j % 2)

            def qk_round(i):
                for j in range(4):
                    low(4 * i + (gQK.n0 + 4 + j), gQK.slot(j))
                    gla_products(4 * i + (4 + j), j % 2)
            repeat(pool, 2, qk_round)
            lows(gV, 2, PAIRS // 2)
            for g in range(4 * PAIRS // 2, GLA_GROUPS):
                gla_products(g, g % 2)
            pool.wait_ge(s_ev, gV.b0 + PAIRS)

            def stage(t, par):
                q = slice(HEAD_DIM * par, HEAD_DIM * (par + 1))
                if not isinstance(t, int) or t > 0 or par:
                    pool.wait_ge(S("a_v_staged"), 2 * t + par)
                if not isinstance(t, int) or t > 0:
                    pool.wait_ge(S("a_scored"), 8 * t - 8 + 4 * par + 4)
                for staged, src in ((Qs, qT), (Ks, kT)):
                    nc.gpsimd.tensor_copy(staged[q, :], src[q, ds(t, 1), :].rearrange("p a t -> p (a t)")
                                          ).then_inc(S("a_qk_staged"), 1)
                pool.wait_ge(S("a_qk_staged"), 4 * t + (2 * par + 2))
                if not isinstance(t, int) or t > 0:
                    pool.wait_ge(S("a_weighted"), 2 * t - 1 + par)
                nc.gpsimd.tensor_copy(Vs[:, :, q], Vt[:, ds(t, 1), :, q].rearrange("p a t d -> p (a t) d")
                                      ).then_inc(S("a_v_staged"), 1)

            stage(0, 0)
            stage(0, 1)

            def stage_pair(p):
                stage(p + 1, 0)
                stage(p + 1, 1)
            lows(gOut, 2, 1)
            repeat(pool, PAIRS - 1, stage_pair)
            pool.wait_ge(S("a_low"), PAIRS)
            nc.gpsimd.memset(adaacc[:], 0.0).then_inc(S("ada_used"), 1)
            lows(gOut, 2, KT // 2 - 1, first=2)

            def ff_group(o):
                for gi in range(2):
                    for half in range(2):
                        ph = gFF[gi][half]

                        def body(p, ph=ph):
                            for j in range(2):
                                low(2 * FF_SLOTS * o + 2 * p + (ph.n0 + j), ph.slot(j))
                        repeat(pool, KT // 2, body)
            repeat(pool, FF_GROUPS // 2, ff_group)
            lows(gX, 2, 1)
            pool.wait_ge(S("ada_done"), 1)
            nc.gpsimd.memset(BDa[:], 0.0).then_inc(S("bd_cleared"), 1)
            nc.gpsimd.memset(BDx[:], 0.0).then_inc(S("bd_cleared"), 1)
            lows(gX, 2, RT // 2 - 1, first=2)
            lows(gGate, 2, KT)
            lows(gPR, 4, KT // 2)
            lows(gLat, 2, (QT + KVT) // 2)
            lows(gLat, 1, 1, first=QT + KVT - 1)
            lows(gRope, 1, 1)

            def heads(i):
                for j in range(2):
                    low(2 * i + (gHead.n0 + j), gHead.slot(j), QT + KVT)
            repeat(pool, N_MLA // 2, heads)
            for ph in (gPM, gOut2):
                lows(ph, 2, KT // 2)
            lows(gUp, 2, FT)
            lows(gDown, 2 * len(DOWN_KS), KT // 2)

        @block.scalar
        def _(act):
            own = Steps(act, S("scalar_steps"))
            A = nc.scalar.activation

            def high(ph, j, n, loaded, kts=KT):
                act.wait_ge(*loaded)
                if not isinstance(n, int) or n >= 2:
                    act.wait_ge(s_mm, n - 1)
                slot = ph.slot(j)
                A(WH[slot][:, 0:kts, :], Wraw[slot][:, 0:kts, :], ACT.Copy).then_inc(s_hi, 1)

            def highs(ph, per, rounds, first=0):
                def body(i):
                    for j in range(per):
                        high(ph, first + j, per * i + (ph.n0 + first + j), landed(ph, first + j, i, per),
                             ph.ks[(first + j) % len(ph.ks)])
                repeat(act, rounds, body)

            def ff_high(ph, j, o, p, at=0):
                per = FF_SLOTS
                sem, v = landed(ph, j)
                high(ph, j, 2 * FF_SLOTS * o + 2 * p + (ph.n0 + j), (sem, 16 * per * o + 16 * p + v))

            def norm_parts(name, tiles, src, dim, dsts, shift=None, base=0):
                for k in range(tiles):
                    if k >= 2:
                        act.wait_ge(S(name + "_summed"), k - 1)
                    A(T[k % 2][:], src(k), ACT.Square).then_inc(S(name + "_squared"), 1)
                act.wait_ge(S(name + "_summed"), tiles)
                A(rstd[:], ps[:, 2, :], ACT.Sqrt, bias=epsc, scale=1.0 / dim).then_inc(S(name + "_root"), 1)
                if dsts is not None:
                    for k in range(tiles):
                        act.wait_ge(S(name + "_scaled"), k + 1)
                        A(dsts(k), T[2 + k % 4][:], ACT.Copy if shift is None else ACT.Identity,
                          **({} if shift is None else {"bias": shift(k)})).then_inc(S(name + "_high"), 1)

            highs(gB, 2, 1)
            act.wait_ge(S("vecs_turned"), len(VEC_GROUPS))
            act.wait_ge(S("x_turned"), KT)
            act.wait_ge(S("const_loaded"), 16)
            norm_parts("n1", KT, lambda k: xT[:, k, :], D_MODEL, lambda k: actH[:, k, :])
            highs(gB, 2, NB_B // 2 - 1, first=2)
            highs(gB, 1, 1, first=NB_B - 1)
            highs(gQK, 2, 1)
            act.wait_ge(s_ev, gB.b0 + NB_B)
            A(bT[:, 4:6, :], bT[:, 4:6, :], ACT.Silu).then_inc(S("gla_silu"), 1)
            act.wait_ge(S("gla_zmin"), 1)
            own.done(A(T[1][:], ps[:, 2, :], ACT.Abs, bias=vec[:, VEC["gla_b_a"]:VEC["gla_b_a"] + 1]))
            own.done(A(T[1][:], T[1][:], ACT.Exp, scale=-1.0))
            A(T[1][:], T[1][:], ACT.Ln, bias=ones[:, 0:1]).then_inc(S("gla_log"), 1)
            act.wait_ge(S("gla_logsig"), 1)
            A(alpha[:], T[0][:], ACT.Exp, scale=1.0 / B_TAU).then_inc(S("gla_alpha"), 1)
            highs(gQK, 2, 1, first=2)
            def qk_round(i):
                for j in range(4):
                    high(gQK, j, 4 * i + (gQK.n0 + 4 + j), landed(gQK, 4 + j, i, 4))
            repeat(act, 2, qk_round)
            highs(gV, 2, PAIRS // 2)
            act.wait_ge(S("gla_ms"), 1)
            A(T[0][:, 0:16], T[0][:, 0:16], ACT.Sqrt, bias=epsc, scale=1.0 / B_VAL).then_inc(S("gla_root"), 1)
            highs(gOut, 2, 1)
            for e in range(2):
                act.wait_ge(S("gla_out"), e + 1)
                A(actH[:, 2 * A_W // P + e, :], T[2 + e][:], ACT.Copy).then_inc(S("gla_high"), 1)

            def exps(pre, lp, s, par, i):
                off = i * (i + 1) // 2 * P
                act.wait_ge(S(pre + "_logits"), 4 * s + (i + 1))
                A(lp[:, par, off:off + (i + 1) * P], lp[:, par, off:off + (i + 1) * P], ACT.Exp,
                  bias=stat[:, 0, par, i:i + 1], scale=-1.0, accum_out=stat[:, 1, par, i:i + 1]
                  ).then_inc(S(pre + "_exp"), 1)

            def turned(pre, pt, s, i):
                act.wait_ge(S(pre + "_turned"), 4 * s + (i + 1))
                A(pt[:, 0:i + 1, i * P:(i + 1) * P], ps[:, 5 + i % 2, 0:(i + 1) * P].rearrange("p (k q) -> p k q", q=P),
                  ACT.Copy).then_inc(S(pre + "_pt"), 1)

            def pair_high(pre, p):
                act.wait_ge(S(pre + "_weighted"), 2 * p + 2)
                A(actH[:, ds(p, 1), :].rearrange("p a t -> p (a t)"), ps[:, 7, :], ACT.Copy
                  ).then_inc(S(pre + "_high"), 1)

            for i in range(TB):
                exps("a", LP, 0, 0, i)

            def pair(p):
                for i in range(TB):
                    exps("a", LP, 2 * p + 1, 1, i)
                    turned("a", PT, 2 * p, i)
                for i in range(TB):
                    exps("a", LP, 2 * p + 2, 0, i)
                    turned("a", PT, 2 * p + 1, i)
                pair_high("a", p)
            repeat(act, PAIRS - 1, pair)
            for i in range(TB):
                exps("a", LP, 2 * PAIRS - 1, 1, i)
                turned("a", PT, 2 * PAIRS - 2, i)
            for i in range(TB):
                turned("a", PT, 2 * PAIRS - 1, i)
            pair_high("a", PAIRS - 1)
            highs(gOut, 2, KT // 2 - 1, first=2)
            ff_high(gFF[0][0], 0, 0, 0)
            ff_high(gFF[0][0], 1, 0, 0)
            act.wait_ge(s_ev, gOut.b0 + KT)
            norm_parts("n2", KT, lambda k: xT[:, k, :], D_MODEL, lambda k: actH[:, k, :])
            A(cact[:], vec[:, VEC["c_2"]:VEC["c_2"] + KT], ACT.Silu).then_inc(S("c_ready"), 1)

            def relu(ph, o, gi, p, j):
                b = 2 * FF_SLOTS * o + 2 * p + (ph.b0 + j)
                f = 2 * KT * o + 2 * p + (KT * gi + j)
                act.wait_ge(s_mm, 2 * FF_SLOTS * o + 2 * p + (ph.n0 + j + 1))
                if not isinstance(f, int) or f >= 2:
                    act.wait_ge(S("hid_squared"), f - 1)
                A(T[j][:], ps[:, ph.bank(j), :], ACT.Relu).then_inc(s_ev_act, 1)

            def square_high(o, gi, p, j):
                f = 2 * KT * o + 2 * p + (KT * gi + j)
                act.wait_ge(S("hid_squared"), f + 1)
                A(UH[:, ds(2 * p + (KT * gi + j), 1), :].rearrange("p a t -> p (a t)"), T[2 + j][:], ACT.Copy
                  ).then_inc(S("hid_high"), 1)

            s_ev_act = S("hid_relu")

            def ff_group(o):
                for gi in range(2):
                    one, two = gFF[gi]
                    nxt = gFF[gi + 1][0] if gi == 0 else None

                    def first(p, one=one, gi=gi):
                        for j in range(2):
                            ff_high(one, j, o, p + 1)
                            relu(one, o, gi, p, j)
                        for j in range(2):
                            square_high(o, gi, p, j)
                    (repeat if o or gi else peeled)(act, KT // 2 - 1, first)
                    for j in range(2):
                        ff_high(two, j, o, 0)
                        relu(one, o, gi, KT // 2 - 1, j)
                    for j in range(2):
                        square_high(o, gi, KT // 2 - 1, j)

                    def second(p, two=two):
                        for j in range(2):
                            ff_high(two, j, o, p + 1)
                    repeat(act, KT // 2 - 1, second)
                    if gi == 0:
                        for j in range(2):
                            ff_high(nxt, j, o, 0)
            ff_group(0)
            for j in range(2):
                ff_high(gFF[0][0], j, 1, 0)
            ff_group(1)
            highs(gX, 2, 1)
            act.wait_ge(s_ev, gX.b0)
            norm_parts("n3", KT, lambda k: xT[:, k, :], D_MODEL, None)
            act.wait_ge(S("n3_done"), KT)
            act.wait_ge(S("ada_done"), 1)
            norm_parts("n4", KT, lambda k: xT[:, k, :], D_MODEL, lambda k: actH[:, k, :],
                       shift=lambda k: mod[:, k:k + 1])
            own.done(A(nsp[:, 1, :], vec[:, VEC["lru_param_2"]:VEC["lru_param_2"] + RT], ACT.Abs))
            own.done(A(nsp[:, 1, :], nsp[:, 1, :], ACT.Exp, scale=-1.0))
            A(nsp[:, 1, :], nsp[:, 1, :], ACT.Ln, bias=ones[:, 0:1]).then_inc(S("lru_log"), 1)

            def bias_at(name, t, j):
                return vec[:, ds(t + (VEC[name] + j), 1)]

            def rnn_sigmoids(t, j):
                act.wait_ge(S("rnn_gated"), t + (j + 1))
                if not isinstance(t, int) or t > 0:
                    act.wait_ge(S("rnn_low"), t + (j - 1))
                A(T[j][:], ps[:, 2 + 2 * j, :], ACT.Sigmoid, bias=bias_at("b_gate_a_2", t, j)).then_inc(S("rnn_sig"), 1)
                A(T[2 + j][:], ps[:, 3 + 2 * j, :], ACT.Sigmoid, bias=bias_at("b_gate_x_2", t, j)).then_inc(S("rnn_sig"), 1)

            def rnn_rest(t):
                marks = []
                for j in range(2):
                    act.wait_ge(S("rnn_loga"), t + (j + 1))
                    A(rA[:, j, :], T[j][:], ACT.Exp).then_inc(S("rnn_a"), 1)
                    A(rTh[:, j, :], T[j][:], ACT.Tanh, scale=-1.0).then_inc(S("rnn_tanh"), 1)
                for j in range(2):
                    act.wait_ge(S("rnn_m2"), t + (j + 1))
                    A(rTh[:, j, :], rTh[:, j, :], ACT.Sqrt).then_inc(S("rnn_mult"), 1)
                for j in range(2):
                    act.wait_ge(S("rnn_state"), t + (j + 1))
                    A(UH[:, ds(t + j, 1), :].rearrange("p a t -> p (a t)"), T[j][:], ACT.Copy).then_inc(S("rnn_high"), 1)

            highs(gX, 2, 1, first=2)

            def x_round(p):
                for j in range(2):
                    sem, v = landed(gX, 4 + j)
                    high(gX, j, 2 * p + (gX.n0 + 4 + j), (sem, 16 * p + v))
                    rnn_sigmoids(2 * p, j)
                rnn_rest(2 * p)
            peeled(act, RT // 2 - 2, x_round)
            for j in range(2):
                sem, v = landed(gGate, j)
                high(gGate, j, gGate.n0 + j, (sem, v))
                rnn_sigmoids(RT - 4, j)
            rnn_rest(RT - 4)
            for j in range(2):
                rnn_sigmoids(RT - 2, j)
            rnn_rest(RT - 2)

            def gate_evac(dst, p, j, at):
                act.wait_ge(s_mm, 2 * p + (gGate.n0 + at + j + 1))
                A(dst[:, ds(2 * p + j, 1), :].rearrange("p a t -> p (a t)"), ps[:, gGate.bank(j), :], ACT.Sigmoid
                  ).then_inc(S("gate_evacuated"), 1)

            def gate_round(dst, at):
                def body(p):
                    for j in range(2):
                        sem, v = landed(gGate, at + 2 + j)
                        high(gGate, j, 2 * p + (gGate.n0 + at + 2 + j), (sem, 16 * p + v))
                        gate_evac(dst, p, j, at)
                return body
            repeat(act, KT // 2, gate_round(gR, 0))
            repeat(act, KT // 2 - 1, gate_round(gM, KT))
            for j in range(2):
                high(gPR, j, gPR.n0 + j, landed(gPR, j), RNN_KS[j])
                gate_evac(gM, KT // 2 - 1, j, KT)
            highs(gPR, 2, 1, first=2)
            def pr_round(i):
                for j in range(4):
                    high(gPR, j, 4 * i + (gPR.n0 + 4 + j), landed(gPR, 4 + j, i, 4), RNN_KS[j % 2])
            repeat(act, KT // 2 - 1, pr_round)
            act.wait_ge(S("rot_angle"), 1)
            A(CS[NOPE:P, :], rott[NOPE:P, :], ACT.Sin).then_inc(S("rot_ready"), 1)
            highs(gLat, 2, (QT + KVT) // 2)
            highs(gLat, 1, 1, first=QT + KVT - 1)
            highs(gRope, 1, 1)
            act.wait_ge(s_ev, gLat.b0 + QT + KVT)
            norm_parts("nq", QT, lambda k: lat[:, k, :], Q_LORA, lambda k: UH[:, k, :])
            act.wait_ge(S("nq_low"), QT)
            norm_parts("nkv", KVT, lambda k: lat[:, QT + k, :], KV_LORA, lambda k: UH[:, QT + k, :])

            def head_high(s, par):
                sem, v = landed(gHead, par)
                p = (s - par) // 2 if isinstance(s, int) else None
                high(gHead, par, s + gHead.n0, (sem, 64 * p + v) if p is not None else (sem, (s - par) * 32 + v),
                     QT + KVT)

            def key_evac(s, par):
                act.wait_ge(S("m_k_made"), s + 1)
                A(Kp[0:NOPE, par, :], ps[0:NOPE, 1, :], ACT.Copy).then_inc(S("m_k_ready"), 1)

            def value_evac(s, par):
                act.wait_ge(s_mm, s + (gHead.n0 + 1))
                if not isinstance(s, int) or s >= 2:
                    act.wait_ge(S("m_weighted"), s - 1)
                A(Vp[:, par, :, :], ps[:, 1, 0:TB * VH].rearrange("p (t d) -> p t d", d=VH), ACT.Copy
                  ).then_inc(S("m_v_ready"), 1)

            head_high(0, 0)
            head_high(1, 1)
            key_evac(0, 0)
            value_evac(0, 0)

            def head(s, par, more, ahead):
                for i in range(TB):
                    exps("m", LP2, s, par, i)
                    if i == 0 and ahead:
                        head_high(s + 2, par)
                    if i == 0 and more:
                        key_evac(s + 1, 1 - par)
                    if not (isinstance(s, int) and s == 0):
                        turned("m", PT2, s - 1, i)
                if more:
                    value_evac(s + 1, 1 - par)

            head(0, 0, True, True)

            def head_pair(p):
                head(2 * p + 1, 1, True, True)
                head(2 * p + 2, 0, True, True)
                pair_high("m", p)
            repeat(act, N_MLA // 2 - 2, head_pair)
            head(N_MLA - 3, 1, True, True)
            head(N_MLA - 2, 0, True, False)
            pair_high("m", N_MLA // 2 - 2)
            head(N_MLA - 1, 1, False, False)
            for i in range(TB):
                turned("m", PT2, N_MLA - 1, i)
            highs(gPM, 2, 1)
            pair_high("m", N_MLA // 2 - 1)

            def merged_high(p, j):
                act.wait_ge(S("merged"), 2 * p + (j + 1))
                A(UH[:, ds(2 * p + j, 1), :].rearrange("p a t -> p (a t)"), T[j][:], ACT.Copy).then_inc(S("merged_high"), 1)

            def pm_round(p):
                for j in range(2):
                    sem, v = landed(gPM, 2 + j)
                    high(gPM, j, 2 * p + (gPM.n0 + 2 + j), (sem, 16 * p + v))
                for j in range(2):
                    merged_high(p, j)
            repeat(act, KT // 2 - 1, pm_round)
            highs(gOut2, 2, 1)
            for j in range(2):
                merged_high(KT // 2 - 1, j)
            highs(gOut2, 2, KT // 2 - 1, first=2)
            highs(gUp, 2, 1)
            act.wait_ge(s_ev, gOut2.b0 + KT)
            norm_parts("n5", KT, lambda k: xT[:, k, :], D_MODEL, lambda k: actH[:, k, :],
                       shift=lambda k: mod[:, 3 * KT + k:3 * KT + k + 1])

            def up_parts(t, j):
                act.wait_ge(S("up_gate"), t + 1)
                if not isinstance(t, int) or t >= 2:
                    act.wait_ge(S("up_low"), t - 1)
                A(act2[:, j, :], cg[:, j, :], ACT.Silu).then_inc(S("up_silu"), 1)

            def up_high(t, j):
                act.wait_ge(S("up_product"), t + 1)
                A(UH[:, ds(t, 1), :].rearrange("p a t -> p (a t)"), act2[:, j, :], ACT.Copy).then_inc(S("up_high"), 1)

            def up_round(p):
                for j in range(2):
                    for h in range(2):
                        sem, v = landed(gUp, 2 * j + 2 + h)
                        high(gUp, h, 4 * p + (gUp.n0 + 2 * j + 2 + h), (sem, 32 * p + v))
                    up_parts(2 * p + j, j)
                    up_high(2 * p + j, j)
            peeled(act, FT // 2 - 1, up_round)
            for h in range(2):
                high(gUp, h, gUp.n0 + 2 * FT - 2 + h, landed(gUp, 2 * FT - 2 + h))
            up_parts(FT - 2, 0)
            up_high(FT - 2, 0)
            for h in range(2):
                high(gDown, h, gDown.n0 + h, landed(gDown, h), DOWN_KS[h])
            up_parts(FT - 1, 1)
            up_high(FT - 1, 1)
            n = len(DOWN_KS)
            highs(gDown, 2 * n - 2, 1, first=2)

            def down_round(i):
                for j in range(2 * n):
                    high(gDown, j, 2 * n * i + (gDown.n0 + 2 * n + j), landed(gDown, 2 * n + j, i, 2 * n), DOWN_KS[j % n])
            repeat(act, KT // 2 - 1, down_round)
            act.wait_ge(s_ev, gDown.b0 + KT)
            norm_parts("n6", KT, lambda k: xT[:, k, :], D_MODEL, None)

        @block.vector
        def _(dve):
            own = Steps(dve, S("vector_steps"))
            V = nc.vector

            def vcol(name, k=0):
                return vec[:, VEC[name] + k:VEC[name] + k + 1]

            def copies(ph, per, rounds, dst, first=0, after=0):
                def body(i):
                    for j in range(per):
                        n = per * i + (ph.n0 + first + j)
                        dve.wait_ge(s_mm, n + 1)
                        V.tensor_copy(dst(i, j), ps[:, ph.bank(first + j), :]).then_inc(s_ev, 1)
                repeat(dve, rounds, body)

            def adds(ph, per=1):
                def body(i):
                    for j in range(2):
                        dve.wait_ge(s_mm, 2 * per * i + (ph.n0 + per * (j + 1)))
                        x = xT[:, ds(2 * i + j, 1), :].rearrange("p a t -> p (a t)")
                        V.tensor_tensor(x, ps[:, ph.bank(j), :], x, ALU.add).then_inc(s_ev, 1)
                return body

            def norm_parts(name, tiles, src, gain, dstL, dstH=None, shift=None, plain=None):
                dve.wait_ge(S(name + "_root"), 1)
                own.done(V.reciprocal(rstd[:], rstd[:]))
                for k in range(tiles):
                    if plain is not None:
                        V.scalar_tensor_tensor(plain(k), src(k), gain(k), rstd[:], ALU.mult, ALU.mult
                                               ).then_inc(S(name + "_done"), 1)
                        continue
                    if k >= 4:
                        low(name, k - 4, dstL, dstH, shift)
                        dve.wait_ge(S(name + "_low"), k - 3)
                    V.scalar_tensor_tensor(T[2 + k % 4][:], src(k), gain(k), rstd[:], ALU.mult, ALU.mult
                                           ).then_inc(S(name + "_scaled"), 1)
                if plain is None:
                    for k in range(max(0, tiles - 4), tiles):
                        low(name, k, dstL, dstH, shift)

            def low(name, k, dstL, dstH, shift):
                dve.wait_ge(S(name + "_high"), k + 1)
                t = T[2 + k % 4][:]
                if shift is None:
                    V.tensor_tensor(dstL(k), t, dstH(k).bitcast(F32), ALU.subtract).then_inc(S(name + "_low"), 1)
                else:
                    V.scalar_tensor_tensor(dstL(k), t, shift(k), dstH(k).bitcast(F32), ALU.add, ALU.subtract
                                           ).then_inc(S(name + "_low"), 1)

            for g, (at, n) in enumerate(VEC_ROWS):
                dve.wait_ge(S("vec_transposed"), g + 1)
                V.tensor_copy(vec[:, at:at + n], ps[:, 2 + g, 0:n]).then_inc(S("vecs_turned"), 1)
            for k in range(KT):
                dve.wait_ge(S("x_transposed"), k + 1)
                V.tensor_copy(xT[:, k, :], ps[:, 6 + k % 2, :]).then_inc(S("x_turned"), 1)
            dve.wait_ge(S("tabs_made"), 1)
            dve.wait_ge(S("tables_loaded"), 64)
            for h in range(2):
                q = slice(h * TAB // 2, (h + 1) * TAB // 2)
                V.scalar_tensor_tensor(tabs[:, q], ps[0:2 * PAIRS, 3 + h, 0:TAB // 2], math.sqrt(HEAD_DIM), maskt[:, q],
                                       ALU.mult, ALU.add).then_inc(S("tabs_ready"), 1)
            dve.wait_ge(S("vecs_turned"), len(VEC_GROUPS))
            dve.wait_ge(S("x_turned"), KT)
            norm_parts("n1", KT, lambda k: xT[:, k, :], lambda k: vcol("norm1_w", k), lambda k: actL[:, k, :],
                       lambda k: actH[:, k, :])
            copies(gB, 2, NB_B // 2, lambda i, j: bT[:, ds(2 * i + j, 1), :].rearrange("p a t -> p (a t)"))
            copies(gB, 1, 1, lambda i, j: bT[:, NB_B - 1, :], first=NB_B - 1)
            dve.wait_ge(s_ev, gB.b0 + NB_B)
            own.done(V.tensor_scalar(bT[:, 0, :], bT[:, 0, :], float(B_KEY ** -0.5), None, ALU.mult))
            dve.wait_ge(S("gla_z"), 1)
            V.tensor_scalar(T[0][:], ps[:, 2, :], vcol("gla_b_a"), 0.0, ALU.add, ALU.min).then_inc(S("gla_zmin"), 1)
            dve.wait_ge(S("gla_log"), 1)
            V.tensor_tensor(T[0][:], T[0][:], T[1][:], ALU.subtract).then_inc(S("gla_logsig"), 1)
            dve.wait_ge(S("gla_alpha"), 1)

            def gla_scan(g, j):
                dve.wait_ge(S("gla_kv"), GLA_GROUP * g + (j + 1))
                if not isinstance(g, int) or g > 0 or j >= 2:
                    dve.wait_ge(S("gla_read"), GLA_GROUP * g + (j - 1))
                V.tensor_tensor_scan(scanned[:, j % 2, :], alpha[:], kvp[:, j % 2, :], 0.0, ALU.mult, ALU.add
                                     ).then_inc(S("gla_scanned"), 1)

            def gla_read(g, j):
                dve.wait_ge(S("gla_scanned"), GLA_GROUP * g + (j + 1))
                if not isinstance(g, int) or g > 0:
                    dve.wait_ge(S("gla_summed"), GLA_GROUP * g + (j + 1 - GLA_GROUP))
                V.tensor_tensor(qs[:, j, :], scanned[:, j % 2, :], bT[:, 0, :], ALU.mult).then_inc(S("gla_read"), 1)

            def gla_group(g):
                gla_scan(g, 0)
                gla_scan(g, 1)
                gla_read(g, 0)
                gla_scan(g, 2)
                gla_read(g, 1)
                gla_scan(g, 3)
                gla_read(g, 2)
                gla_read(g, 3)

            def qk_dst(j, i):
                t = (qT, kT)[j % 2]
                return t[:, ds(i + (PAIRS // 2) * (j // 2), 1), :].rearrange("p a t -> p (a t)")

            dve.wait_ge(S("tab_stored"), 16)
            for j in range(4):
                copies(gQK, 1, 1, lambda i, _, j=j: qk_dst(j, 0), first=j)
                gla_group(j)

            def qk_round(i):
                for j in range(4):
                    dve.wait_ge(s_mm, 4 * i + (gQK.n0 + 4 + j + 1))
                    V.tensor_copy(qk_dst(j, i + 1), ps[:, gQK.bank(j), :]).then_inc(s_ev, 1)
                    gla_group(4 * i + (4 + j))
            repeat(dve, 2, qk_round)
            copies(gV, 2, PAIRS // 2, lambda i, j: Vt[:, ds(i + PAIRS // 2 * j, 1), :, :].rearrange("p a t d -> p (a t d)"))
            for g in range(4 * PAIRS // 2, GLA_GROUPS):
                gla_group(g)
            dve.wait_ge(S("gla_summed"), B_VAL)
            own.done(V.tensor_copy(oTok[:].rearrange("p t f -> p (t f)"), ps[:, 2:4, :].rearrange("p b f -> p (b f)")))
            own.done(V.tensor_tensor(oSq[:], oTok[:], oTok[:], ALU.mult))
            V.tensor_reduce(T[0][:, 0:TB * B_HEADS], oSq[:].rearrange("p t (h v) -> p (t h) v", v=B_VAL), AX_X, ALU.add
                            ).then_inc(S("gla_ms"), 1)
            dve.wait_ge(S("gla_root"), 1)
            own.done(V.reciprocal(T[0][:, 0:TB * B_HEADS], T[0][:, 0:TB * B_HEADS]))
            V.tensor_tensor(oTok[:].rearrange("p t (h v) -> p (t h) v", v=B_VAL),
                            oTok[:].rearrange("p t (h v) -> p (t h) v", v=B_VAL),
                            T[0][:, 0:TB * B_HEADS].unsqueeze(2).to_broadcast([P, TB * B_HEADS, B_VAL]), ALU.mult
                            ).then_inc(S("gla_normed"), 1)
            for e in range(2):
                dve.wait_ge(S("gla_turned"), e + 1)
                dve.wait_ge(S("gla_silu"), 1)
                V.scalar_tensor_tensor(T[2 + e][:], ps[:, 5 + e, :], vcol("gla_norm_w", e), bT[:, 4 + e, :], ALU.mult, ALU.mult
                                       ).then_inc(S("gla_out"), 1)
            for e in range(2):
                dve.wait_ge(S("gla_high"), e + 1)
                k = 2 * A_W // P + e
                V.tensor_tensor(actL[:, k, :], T[2 + e][:], actH[:, k, :].bitcast(F32), ALU.subtract
                                ).then_inc(S("gla_low"), 1)

            S_BANK = (3, 4, 2, 3)

            def logits(pre, lp, s, par, i, z, scale):
                n, off = (i + 1) * P, i * (i + 1) // 2 * P
                dve.wait_ge(S(pre + "_scored"), 4 * s + (i + 1))
                dve.sem_inc(S("scores_seen"), 1)
                V.tensor_tensor_reduce(lp[:, par, off:off + n], ps[:, S_BANK[i], 0:n], z((TB - 1 - i) * P), -scale, BIG,
                                       ALU.add, ALU.min, stat[:, 0, par, i:i + 1]).then_inc(S(pre + "_logits"), 1)

            def normed(pre, lp, s, par, i):
                n, off = (i + 1) * P, i * (i + 1) // 2 * P
                dve.wait_ge(S(pre + "_exp"), 4 * s + (i + 1))
                own.done(V.reciprocal(stat[:, 2, par, i:i + 1], stat[:, 1, par, i:i + 1]))
                V.tensor_scalar(lp[:, par, off:off + n], lp[:, par, off:off + n], stat[:, 2, par, i:i + 1], None, ALU.mult
                                ).then_inc(S(pre + "_normed"), 1)

            def head(pre, lp, s, par, z, scale, between=None):
                for i in range(TB):
                    logits(pre, lp, s, par, i, z, scale)
                    if i == 0 and between is not None:
                        between()
                    if i > 0:
                        normed(pre, lp, s, par, i - 1)
                normed(pre, lp, s, par, TB - 1)

            def pair_low(pre, p):
                dve.wait_ge(S(pre + "_high"), p + 1)
                q = lambda t: t[:, ds(p, 1), :].rearrange("p a t -> p (a t)")
                V.tensor_tensor(q(actL), ps[:, 7, :], q(actH).bitcast(F32), ALU.subtract).then_inc(S(pre + "_low"), 1)

            SC_A = HEAD_DIM ** -0.5

            def a_head(s, par, p):
                dve.wait_ge(S(f"strip_loaded{par}"), 16 * p + 16)
                head("a", LP, s, par, lambda at: Z[:, par, at:SEQ], SC_A)
            a_head(0, 0, 0)

            def pair(p):
                own.enter(p, 2 * TB)
                a_head(2 * p + 1, 1, p)
                a_head(2 * p + 2, 0, p + 1)
                pair_low("a", p)
            repeat(dve, PAIRS - 1, pair)
            own.leave(PAIRS - 1)
            a_head(2 * PAIRS - 1, 1, PAIRS - 1)
            pair_low("a", PAIRS - 1)
            repeat(dve, KT // 2, adds(gOut))
            dve.wait_ge(s_ev, gOut.b0 + KT)
            norm_parts("n2", KT, lambda k: xT[:, k, :], lambda k: vcol("norm2_w", k), lambda k: actL[:, k, :],
                       lambda k: actH[:, k, :])
            dve.wait_ge(S("c_ready"), 1)

            def ada_chunk(o, gi, half, p, j):
                c = 4 * KT * o + 2 * p + (2 * KT * gi + KT * half + j)
                dve.wait_ge(S(f"ada_loaded{j}"), 2 * KT * 16 * o + 16 * p + 16 * (KT * gi + KT // 2 * half + 1))
                dve.wait_ge(S("ada_used"), c + 1)
                q = adaacc[:, ds(2 * ADA_COLS * p + ADA_COLS * j, ADA_COLS)]
                V.scalar_tensor_tensor(q, wada[:, j, :], cact[:, ds(4 * o + (2 * gi + half), 1)], q, ALU.mult, ALU.add
                                       ).then_inc(S("ada_used"), 1)

            def ff_group(o):
                for gi in range(2):
                    one, two = gFF[gi]

                    def first(p, one=one, gi=gi):
                        for j in range(2):
                            f = 2 * KT * o + 2 * p + (KT * gi + j)
                            dve.wait_ge(S("hid_relu"), f + 1)
                            if not isinstance(f, int) or f >= 2:
                                dve.wait_ge(S("hid_low"), f - 1)
                            V.tensor_tensor(T[2 + j][:], T[j][:], T[j][:], ALU.mult).then_inc(S("hid_squared"), 1)
                        for j in range(2):
                            f = 2 * KT * o + 2 * p + (KT * gi + j)
                            ada_chunk(o, gi, 0, p, j)
                            dve.wait_ge(S("hid_high"), f + 1)
                            u = lambda t: t[:, ds(2 * p + (KT * gi + j), 1), :].rearrange("p a t -> p (a t)")
                            V.tensor_tensor(u(UL), T[2 + j][:], u(UH).bitcast(F32), ALU.subtract).then_inc(S("hid_low"), 1)
                    (repeat if o or gi else peeled)(dve, KT // 2, first)

                    def second(p, two=two, gi=gi):
                        for j in range(2):
                            ada_chunk(o, gi, 1, p, j)
                            dve.wait_ge(s_mm, 2 * FF_SLOTS * o + 2 * p + (two.n0 + j + 1))
                            x = xT[:, ds(2 * p + j, 1), :].rearrange("p a t -> p (a t)")
                            dve.wait_ge(S("x_added"), KT * (2 * o + gi)) if gi or not isinstance(o, int) or o else None
                            V.tensor_tensor(x, ps[:, two.bank(j), :], x, ALU.add).then_inc(S("x_added"), 1)
                    repeat(dve, KT // 2, second)
            ff_group(0)
            ff_group(1)
            dve.wait_ge(S("x_added"), KT * FF_GROUPS)
            norm_parts("n3", KT, lambda k: xT[:, k, :], lambda k: vcol("final_norm_w", k), None,
                       plain=lambda k: xT[:, k, :])
            dve.wait_ge(S("ada_summed"), 1)
            own.done(V.tensor_tensor(mod[:], ps[:, 3, 0:6 * KT], vec[:, VEC["b_ada_2"]:VEC["b_ada_2"] + 6 * KT], ALU.add))
            own.done(V.scalar_tensor_tensor(gainA[:, 0, :], mod[:, KT:2 * KT], 1.0,
                                            vec[:, VEC["norm1_g_2"]:VEC["norm1_g_2"] + KT], ALU.add, ALU.mult))
            V.scalar_tensor_tensor(gainA[:, 1, :], mod[:, 4 * KT:5 * KT], 1.0,
                                   vec[:, VEC["norm2_g_2"]:VEC["norm2_g_2"] + KT], ALU.add, ALU.mult
                                   ).then_inc(S("ada_done"), 1)
            dve.wait_ge(S("ada_done"), 1)
            norm_parts("n4", KT, lambda k: xT[:, k, :], lambda k: gainA[:, 0, k:k + 1], lambda k: actL[:, k, :],
                       lambda k: actH[:, k, :], shift=lambda k: mod[:, k:k + 1])
            own.done(V.tensor_scalar(nsp[:, 0, :], vec[:, VEC["lru_param_2"]:VEC["lru_param_2"] + RT], -1.0, 0.0,
                                     ALU.mult, ALU.max))
            dve.wait_ge(S("lru_log"), 1)
            own.done(V.tensor_tensor(nsp[:, 0, :], nsp[:, 0, :], nsp[:, 1, :], ALU.add))
            own.done(V.tensor_scalar(nsp[:, 0, :], nsp[:, 0, :], -LRU_C, None, ALU.mult))
            dve.wait_ge(S("reset_loaded"), 16)
            own.done(V.tensor_copy(T[4][:], posr[:]))
            own.done(V.tensor_scalar(T[4][:], T[4][:], 0.0, NEG, ALU.is_equal, ALU.mult))

            def conv(t, j):
                dve.wait_ge(s_mm, t + (gX.n0 + j + 1))
                y = lambda a: xc[:, ds(t + j, 1), a:SEQ].rearrange("p a t -> p (a t)")
                w = lambda k: vec[:, ds(t + (VEC["conv_w_2"] + RT * k + j), 1)]
                own.done(V.tensor_scalar(y(0), ps[:, gX.bank(j), :], w(CONV_W - 1),
                                         vec[:, ds(t + (VEC["conv_b_2"] + j), 1)], ALU.mult, ALU.add))
                for k in range(1, CONV_W):
                    ins = V.scalar_tensor_tensor(y(k), ps[:, gX.bank(j), 0:SEQ - k], w(CONV_W - 1 - k), y(k),
                                                 ALU.mult, ALU.add)
                    if k < CONV_W - 1:
                        own.done(ins)
                    else:
                        ins.then_inc(s_ev, 1)

            def rnn_loga(t, j):
                dve.wait_ge(S("rnn_sig"), 2 * t + (2 * j + 2))
                V.scalar_tensor_tensor(T[j][:], T[j][:], nsp[:, 0, ds(t + j, 1)], T[4][:], ALU.mult, ALU.add
                                       ).then_inc(S("rnn_loga"), 1)

            def rnn_tiles(t):
                for j in range(2):
                    x = xc[:, ds(t + j, 1), :].rearrange("p a t -> p (a t)")
                    own.done(V.tensor_tensor(T[2 + j][:], T[2 + j][:], x, ALU.mult))
                for j in range(2):
                    dve.wait_ge(S("rnn_tanh"), t + (j + 1))
                    own.done(V.tensor_tensor(T[5][:], rA[:, j, :], rA[:, j, :], ALU.mult))
                    V.scalar_tensor_tensor(rTh[:, j, :], T[5][:], 1.0, rTh[:, j, :], ALU.add, ALU.mult
                                           ).then_inc(S("rnn_m2"), 1)
                    dve.wait_ge(S("rnn_m2"), t + (j + 1))
                for j in range(2):
                    dve.wait_ge(S("rnn_mult"), t + (j + 1))
                    own.done(V.tensor_tensor(rTh[:, j, :], rTh[:, j, :], T[2 + j][:], ALU.mult))
                    V.tensor_tensor_scan(T[j][:], rA[:, j, :], rTh[:, j, :], 0.0, ALU.mult, ALU.add
                                         ).then_inc(S("rnn_state"), 1)
                for j in range(2):
                    dve.wait_ge(S("rnn_high"), t + (j + 1))
                    u = lambda b: b[:, ds(t + j, 1), :].rearrange("p a t -> p (a t)")
                    V.tensor_tensor(u(UL), T[j][:], u(UH).bitcast(F32), ALU.subtract).then_inc(S("rnn_low"), 1)

            conv(0, 0)
            conv(0, 1)

            def x_round(p):
                own.enter(p, 2 * (CONV_W - 1) + 6)
                for j in range(2):
                    conv(2 * p + 2, j)
                    rnn_loga(2 * p, j)
                rnn_tiles(2 * p)
            repeat(dve, RT // 2 - 1, x_round)
            own.leave(RT // 2 - 1)
            for j in range(2):
                rnn_loga(RT - 2, j)
            rnn_tiles(RT - 2)
            dve.wait_ge(S("rnn_low"), RT)
            dve.wait_ge(S("gate_evacuated"), 2 * KT)

            def pr_round(i):
                for j in range(2):
                    dve.wait_ge(s_mm, 4 * i + (gPR.n0 + 2 * j + 2))
                    g = gR[:, ds(2 * i + j, 1), :].rearrange("p a t -> p (a t)")
                    V.tensor_tensor(g, ps[:, gPR.bank(j), :], g, ALU.mult).then_inc(s_ev, 1)
            dve.wait_ge(S("pos_loaded"), 16)
            c1 = 6.28125
            c2 = float(np.float32(2 * math.pi - c1) - np.float32(2 * math.pi - c1) % np.float32(2.0 ** -20))
            c3 = float(2 * math.pi - c1 - c2)
            rnd = float(1.5 * 2 ** 23)
            own.done(V.tensor_copy(rott[:], posb[:]))
            own.done(V.tensor_scalar(rott[:], rott[:], const[:, C_INVF:C_INVF + 1], None, ALU.mult))
            own.done(V.tensor_scalar(rotk[:], rott[:], float(1 / (2 * math.pi)), const[:, C_TURN:C_TURN + 1], ALU.mult, ALU.add))
            own.done(V.tensor_scalar(rotk[:], rotk[:], rnd, None, ALU.add))
            own.done(V.tensor_scalar(rotk[:], rotk[:], -rnd, None, ALU.add))
            for c in (c1, c2, c3):
                own.done(V.scalar_tensor_tensor(rott[:], rotk[:], -c, rott[:], ALU.mult, ALU.add))
            own.done(V.tensor_scalar(rott[:], rott[:], const[:, C_PHASE:C_PHASE + 1], 3.1415925, ALU.add, ALU.min))
            own.done(V.memset(CS[0:NOPE, :], 1.0))
            V.tensor_scalar(rott[:], rott[:], -3.1415925, None, ALU.max).then_inc(S("rot_angle"), 1)
            repeat(dve, KT // 2, pr_round)
            dve.wait_ge(S("rot_ready"), 1)
            copies(gLat, 2, (QT + KVT) // 2, lambda i, j: lat[:, ds(2 * i + j, 1), :].rearrange("p a t -> p (a t)"))
            copies(gLat, 1, 1, lambda i, j: lat[:, QT + KVT - 1, :], first=QT + KVT - 1)
            dve.wait_ge(s_mm, gRope.n0 + 1)
            V.tensor_tensor(T[4][NOPE:P, :], ps[NOPE:P, gRope.bank(0), :], CS[NOPE:P, :], ALU.mult).then_inc(s_ev, 1)
            dve.wait_ge(s_ev, gRope.b0 + 1)
            own.done(V.tensor_copy(T[5][NOPE:QKD, :], T[4][QKD:P, :]))
            for par in range(2):
                own.done(V.tensor_tensor(Kp[NOPE:QKD, par, :], T[4][NOPE:QKD, :], T[5][NOPE:QKD, :], ALU.add))
                V.tensor_copy(Kp[QKD:P, par, :], Kp[NOPE:QKD, par, :]).then_inc(S("krot_ready"), 1)
            dve.wait_ge(S("krot_ready"), 2)
            norm_parts("nq", QT, lambda k: lat[:, k, :], lambda k: vcol("q_norm_g_2", k), lambda k: UL[:, k, :],
                       lambda k: UH[:, k, :])
            norm_parts("nkv", KVT, lambda k: lat[:, QT + k, :], lambda k: vcol("kv_norm_g_2", k),
                       lambda k: UL[:, QT + k, :], lambda k: UH[:, QT + k, :])

            def query_evac(s, par):
                dve.wait_ge(S("m_q_made"), s + 1)
                V.tensor_tensor(Qp[:, par, :], ps[:, 0, :], CS[:], ALU.mult).then_inc(S("m_q_ready"), 1)

            SC_M = QKD ** -0.5
            z_m = lambda at: strip[:, at:SEQ]
            query_evac(0, 0)
            head("m", LP2, 0, 0, z_m, SC_M, lambda: query_evac(1, 1))

            def head_pair(p):
                own.enter(p, 2 * TB)
                head("m", LP2, 2 * p + 1, 1, z_m, SC_M, lambda: query_evac(2 * p + 2, 0))
                head("m", LP2, 2 * p + 2, 0, z_m, SC_M, lambda: query_evac(2 * p + 3, 1))
                pair_low("m", p)
            repeat(dve, N_MLA // 2 - 1, head_pair)
            own.leave(N_MLA // 2 - 1)
            head("m", LP2, N_MLA - 1, 1, z_m, SC_M)
            pair_low("m", N_MLA // 2 - 1)

            def pm_round(i):
                for j in range(2):
                    dve.wait_ge(s_mm, 2 * i + (gPM.n0 + j + 1))
                    m = lambda t: t[:, ds(2 * i + j, 1), :].rearrange("p a t -> p (a t)")
                    if not isinstance(i, int) or i > 0:
                        dve.wait_ge(S("merged_low"), 2 * i + (j - 1))
                    V.tensor_tensor(T[j][:], ps[:, gPM.bank(j), :], m(gM), ALU.mult).then_inc(s_ev, 1)
                    dve.wait_ge(s_ev, 2 * i + (gPM.b0 + j + 1))
                    V.tensor_tensor(T[j][:], T[j][:], m(gR), ALU.add).then_inc(S("merged"), 1)
                for j in range(2):
                    m = lambda t: t[:, ds(2 * i + j, 1), :].rearrange("p a t -> p (a t)")
                    dve.wait_ge(S("merged_high"), 2 * i + (j + 1))
                    V.tensor_tensor(m(UL), T[j][:], m(UH).bitcast(F32), ALU.subtract).then_inc(S("merged_low"), 1)
            peeled(dve, KT // 2, pm_round)

            def gated_adds(ph, gate, per=1):
                def body(i):
                    for j in range(2):
                        dve.wait_ge(s_mm, 2 * per * i + (ph.n0 + per * (j + 1)))
                        x = xT[:, ds(2 * i + j, 1), :].rearrange("p a t -> p (a t)")
                        V.scalar_tensor_tensor(x, ps[:, ph.bank(j), :], mod[:, ds(2 * i + (gate + j), 1)], x,
                                               ALU.mult, ALU.add).then_inc(s_ev, 1)
                return body
            repeat(dve, KT // 2, gated_adds(gOut2, 2 * KT))
            dve.wait_ge(s_ev, gOut2.b0 + KT)
            norm_parts("n5", KT, lambda k: xT[:, k, :], lambda k: gainA[:, 1, k:k + 1], lambda k: actL[:, k, :],
                       lambda k: actH[:, k, :], shift=lambda k: mod[:, 3 * KT + k:3 * KT + k + 1])

            def ffn_conv(t, j, h, dst, sem):
                dve.wait_ge(s_mm, 2 * t + (gUp.n0 + h + 1))
                w = lambda k: vec[:, ds(t + (VEC[f"ffn_conv_w{k}"] + FT * h), 1)]
                own.done(V.tensor_scalar(dst[:, j, :], ps[:, gUp.bank(h), :], w(FFN_CONV - 1),
                                         vec[:, ds(t + (VEC["ffn_conv_b_2"] + FT * h), 1)], ALU.mult, ALU.add))
                own.done(V.scalar_tensor_tensor(dst[:, j, 1:SEQ], ps[:, gUp.bank(h), 0:SEQ - 1], w(FFN_CONV - 2),
                                                dst[:, j, 1:SEQ], ALU.mult, ALU.add))
                V.scalar_tensor_tensor(dst[:, j, 2:SEQ], ps[:, gUp.bank(h), 0:SEQ - 2], w(FFN_CONV - 3),
                                       dst[:, j, 2:SEQ], ALU.mult, ALU.add).then_inc(S(sem), 1)

            def up_pair(t, j):
                ffn_conv(t, j, 0, cg, "up_gate")
                ffn_conv(t, j, 1, cv, "up_value")
                dve.wait_ge(S("up_value"), t + 1)
                dve.wait_ge(S("up_silu"), t + 1)
                V.tensor_tensor(act2[:, j, :], act2[:, j, :], cv[:, j, :], ALU.mult).then_inc(S("up_product"), 1)
                dve.wait_ge(S("up_high"), t + 1)
                u = lambda b: b[:, ds(t, 1), :].rearrange("p a t -> p (a t)")
                V.tensor_tensor(u(UL), act2[:, j, :], u(UH).bitcast(F32), ALU.subtract).then_inc(S("up_low"), 1)

            def up_round(p):
                own.enter(p, 8)
                up_pair(2 * p, 0)
                up_pair(2 * p + 1, 1)
            repeat(dve, FT // 2, up_round)
            own.leave(FT // 2)
            repeat(dve, KT // 2, gated_adds(gDown, 5 * KT, len(DOWN_KS)))
            dve.wait_ge(s_ev, gDown.b0 + KT)
            norm_parts("n6", KT, lambda k: xT[:, k, :], lambda k: vcol("final_g_2", k), None, plain=lambda k: yout[:, k, :])
            for k in range(KT):
                dve.wait_ge(S("y_turned"), k + 1)
                V.tensor_copy(yrow[:, :, k * P:(k + 1) * P], ps[:, 4 + k % 2, :].rearrange("p (t f) -> p t f", f=P)
                              ).then_inc(S("rows_ready"), 1)

        @block.tensor
        def _(pe):
            MM = nc.tensor.matmul

            def three(o, wh, wl, ah, al, first, last):
                MM(o, wh, ah, start=first, stop=False)
                MM(o, wh, al, start=False, stop=False)
                return MM(o, wl, ah, start=False, stop=last)

            def block_product(ph, n, j, q, actin, k0, ready, evac):
                kts, last = ph.ks[q], q == len(ph.ks) - 1
                slot, bank = ph.slot(len(ph.ks) * j + q), ph.bank(j)
                pe.wait_ge(s_lo, n + 1)
                if q == 0:
                    for sem, v in evac:
                        pe.wait_ge(sem, v)
                for k in range(kts):
                    if ready is not None:
                        pe.wait_ge(*ready(k0 + k))
                    mm = three(ps[:, bank, :], WH[slot][:, k, :], WL[slot][:, k, :], actin(0, k0 + k), actin(1, k0 + k),
                               q == 0 and k == 0, last and k == kts - 1)
                mm.then_inc(s_mm, 1)

            def free(b):
                return [(s_ev, b - 1)] if not isinstance(b, int) or b >= 2 else []

            def products(ph, per, rounds, actin, ready=None, first=0, evac=free):
                nk = len(ph.ks)

                def body(i):
                    for j in range(per):
                        k0 = 0
                        for q in range(nk):
                            block_product(ph, per * nk * i + (ph.n0 + nk * (first + j) + q), first + j, q, actin, k0,
                                          ready if j == 0 else None, evac(per * i + (ph.b0 + first + j)))
                            k0 += ph.ks[q]
                (repeat if ph.b0 else peeled)(pe, rounds, body)

            x_in = lambda part, k: (actH, actL)[part][:, k, :]

            def mean_square(name, tiles):
                for k in range(tiles):
                    pe.wait_ge(S(name + "_squared"), k + 1)
                    MM(ps[:, 2, :], ones[:], T[k % 2][:], start=(k == 0), stop=(k == tiles - 1)
                       ).then_inc(S(name + "_summed"), 1)

            pe.wait_ge(S("const_loaded"), 16)
            pe.wait_ge(S("vec_loaded"), 16 * sum(len(g) for g in VEC_GROUPS))
            for g, (at, n) in enumerate(VEC_ROWS):
                nc.tensor.transpose(ps[:, 2 + g, 0:n], vrows[0:n, g, :], ident[0:n, 0:n]).then_inc(S("vec_transposed"), 1)
            pe.wait_ge(S("x_loaded"), 16)
            for k in range(KT):
                if k >= 2:
                    pe.wait_ge(S("x_turned"), k - 1)
                for t in range(TB):
                    mm = nc.tensor.transpose(ps[:, 6 + k % 2, t * P:(t + 1) * P], xn[:, t, k * P:(k + 1) * P], ident)
                mm.then_inc(S("x_transposed"), 1)
            pe.wait_ge(S("tables_loaded"), 64)
            pe.wait_ge(S("vecs_turned"), len(VEC_GROUPS))
            for h in range(2):
                mm = MM(ps[0:2 * PAIRS, 3 + h, 0:TAB // 2], relb[:], onehot[:, h * TAB // 2:(h + 1) * TAB // 2],
                        start=True, stop=True)
            mm.then_inc(S("tabs_made"), 1)
            pe.wait_ge(S("ones_set"), 1)
            mean_square("n1", KT)
            n1 = lambda k: (S("n1_low"), k + 1)
            products(gB, 2, NB_B // 2, x_in, n1)
            products(gB, 1, 1, x_in, first=NB_B - 1)
            pe.wait_ge(s_ev, gB.b0 + NB_B)
            MM(ps[:, 2, :], wa2[:], bT[0:B_RANK, NB_B - 1, :], start=True, stop=True).then_inc(S("gla_z"), 1)

            def gla_sums(g):
                for j in range(GLA_GROUP):
                    pe.wait_ge(S("gla_read"), GLA_GROUP * g + (j + 1))
                    for t in range(TB):
                        o = ps[:, 2 + t // 2, (t % 2) * B_W:(t % 2 + 1) * B_W].rearrange("p (h v) -> p h v", v=B_VAL)
                        mm = MM(o[:, :, ds(GLA_GROUP * g + j, 1)].rearrange("p h a -> p (h a)"),
                                qs[:, j, t * P:(t + 1) * P], headsum, start=True, stop=True)
                    mm.then_inc(S("gla_summed"), 1)

            for j in range(4):
                products(gQK, 1, 1, x_in, first=j)
                if j:
                    gla_sums(j - 1)

            def qk_round(i):
                for j in range(4):
                    block_product(gQK, 4 * i + (gQK.n0 + 4 + j), j, 0, x_in, 0, None, free(4 * i + (gQK.b0 + 4 + j)))
                    gla_sums(4 * i + (3 + j))
            repeat(pe, 2, qk_round)

            def v_round(i):
                for j in range(2):
                    slot, bank = gV.slot(j), gV.bank(j)
                    pe.wait_ge(s_lo, 2 * i + (gV.n0 + j + 1))
                    pe.wait_ge(s_ev, 2 * i + (gV.b0 + j - 1))
                    for t in range(TB):
                        q = slice(t * P, (t + 1) * P)
                        for k in range(KT):
                            mm = three(ps[:, bank, q], actH[:, k, q], actL[:, k, q], WH[slot][:, k, :], WL[slot][:, k, :],
                                       k == 0, k == KT - 1)
                    mm.then_inc(s_mm, 1)
            repeat(pe, PAIRS // 2, v_round)
            for g in range(4 * PAIRS // 2 - 1, GLA_GROUPS):
                gla_sums(g)
            pe.wait_ge(S("gla_normed"), 1)
            for e in range(2):
                for t in range(TB):
                    mm = nc.tensor.transpose(ps[:, 5 + e, t * P:(t + 1) * P], oTok[:, t, e * P:(e + 1) * P], ident)
                mm.then_inc(S("gla_turned"), 1)

            S_BANK = (3, 4, 2, 3)

            def scores(pre, s, i, q, k):
                n = (i + 1) * P
                if i == TB - 1:
                    pe.wait_ge(S(pre + "_logits"), 4 * s + 1)
                elif not isinstance(s, int) or s > 0:
                    pe.wait_ge(S(pre + "_logits"), 4 * s)
                MM(ps[:, S_BANK[i], 0:n], q(i), k(n), start=True, stop=True).then_inc(S(pre + "_scored"), 1)

            def turn(pre, lp, s, par, i):
                off = i * (i + 1) // 2 * P
                pe.wait_ge(S(pre + "_normed"), 4 * s + (i + 1))
                if i >= 2:
                    pe.wait_ge(S(pre + "_pt"), 4 * s + (i - 1))
                for k in range(i + 1):
                    mm = nc.tensor.transpose(ps[:, 5 + i % 2, k * P:(k + 1) * P],
                                             lp[:, par, off + k * P:off + (k + 1) * P], ident)
                mm.then_inc(S(pre + "_turned"), 1)

            def weigh(pre, pt, s, par, p, v):
                pe.wait_ge(S(pre + "_pt"), 4 * s + 4)
                if par == 0 and not (isinstance(p, int) and p == 0):
                    pe.wait_ge(S(pre + "_low"), p)
                for k in range(TB):
                    mm = MM(ps[HEAD_DIM * par:HEAD_DIM * (par + 1), 7, k * P:SEQ], v(k), pt[:, k, k * P:SEQ],
                            start=(k == 0), stop=(k == TB - 1))
                mm.then_inc(S(pre + "_weighted"), 1)

            def a_head(s, par):
                q = slice(HEAD_DIM * par, HEAD_DIM * (par + 1))
                pe.wait_ge(S("a_qk_staged"), 2 * s + 2)
                for i in range(TB):
                    scores("a", s, i, lambda i: Qs[q, i * P:(i + 1) * P], lambda n: Ks[q, 0:n])
                    if not (isinstance(s, int) and s == 0):
                        turn("a", LP, s - 1, 1 - par, i)

            def a_weigh(s, par, p):
                pe.wait_ge(S("a_v_staged"), s + 1)
                weigh("a", PT, s, par, p, lambda k: Vs[:, k, HEAD_DIM * par:HEAD_DIM * (par + 1)])

            a_head(0, 0)

            def a_pair(p):
                a_head(2 * p + 1, 1)
                a_weigh(2 * p, 0, p)
                a_head(2 * p + 2, 0)
                a_weigh(2 * p + 1, 1, p)
            repeat(pe, PAIRS - 1, a_pair)
            a_head(2 * PAIRS - 1, 1)
            a_weigh(2 * PAIRS - 2, 0, PAIRS - 1)
            for i in range(TB):
                turn("a", LP, 2 * PAIRS - 1, 1, i)
            a_weigh(2 * PAIRS - 1, 1, PAIRS - 1)
            pe.wait_ge(S("gla_low"), 2)
            pe.wait_ge(S("a_low"), PAIRS)
            products(gOut, 2, KT // 2, x_in)
            mean_square("n2", KT)
            n2 = lambda k: (S("n2_low"), k + 1)

            def ff_group(o):
                for gi in range(2):
                    one, two = gFF[gi]
                    hid = lambda part, k, gi=gi: (UH, UL)[part][:, KT * gi + k, :]

                    def first(p, one=one, gi=gi):
                        for j in range(2):
                            f = 2 * KT * o + 2 * p + (KT * gi + j)
                            prev = [(S("hid_relu"), f - 1)] if not isinstance(f, int) or f >= 2 else []
                            if gi or not isinstance(o, int) or o:
                                prev.append((S("x_added"), KT * (2 * o + gi)))
                            else:
                                prev.append((s_ev, gOut.b0 + KT))
                            block_product(one, 2 * FF_SLOTS * o + 2 * p + (one.n0 + j), j, 0, x_in, 0,
                                          n2 if j == 0 else None, prev)
                    (repeat if o or gi else peeled)(pe, KT // 2, first)

                    def second(p, two=two, gi=gi, hid=hid):
                        for j in range(2):
                            a = KT * (2 * o + gi) + 2 * p + j
                            prev = [(S("x_added"), a - 1)] if not isinstance(a, int) or a >= 2 else []
                            prev.append((S("hid_relu"), 2 * KT * o + KT * (gi + 1)))
                            block_product(two, 2 * FF_SLOTS * o + 2 * p + (two.n0 + j), j, 0, hid, 0,
                                          (lambda k: (S("hid_low"), 2 * KT * o + (KT * gi + k + 1))) if j == 0 else None,
                                          prev)
                    (repeat if o or gi else peeled)(pe, KT // 2, second)
            ff_group(0)
            ff_group(1)
            pe.wait_ge(S("ada_used"), 1 + 2 * KT * FF_GROUPS)
            for m in range(6 * KT):
                mm = MM(ps[:, 3, m:m + 1], adaacc[:, m * P:(m + 1) * P], ones[:, 0:1], start=True, stop=True)
            mm.then_inc(S("ada_summed"), 1)
            pe.wait_ge(S("x_added"), KT * FF_GROUPS)
            mean_square("n3", KT)
            mean_square("n4", KT)
            n4 = lambda k: (S("n4_low"), k + 1)
            x_free = lambda b: free(b) if not isinstance(b, int) or b >= gX.b0 + 2 else [(S("x_added"), KT * FF_GROUPS)]
            products(gX, 2, 1, x_in, n4, evac=x_free)

            def rnn_gate(t, j):
                pe.wait_ge(S(f"rnn_weights{j}"), t * 32 + 64)
                pe.wait_ge(s_ev, t + (gX.b0 + j + 1))
                if not isinstance(t, int) or t > 0:
                    pe.wait_ge(S("rnn_sig"), 2 * t + (2 * j - 2))
                x = xc[:, ds(t + j, 1), :].rearrange("p a t -> p (a t)")
                MM(ps[:, 2 + 2 * j, :], BDa[:, j, :], x, start=True, stop=True)
                MM(ps[:, 3 + 2 * j, :], BDx[:, j, :], x, start=True, stop=True).then_inc(S("rnn_gated"), 1)

            def x_round(p):
                for j in range(2):
                    block_product(gX, 2 * p + (gX.n0 + 2 + j), j, 0, x_in, 0, None, free(2 * p + (gX.b0 + 2 + j)))
                    rnn_gate(2 * p, j)
            peeled(pe, RT // 2 - 1, x_round)
            for j in range(2):
                rnn_gate(RT - 2, j)

            def gate_round(i):
                for j in range(2):
                    n = 2 * i + j
                    prev = [(s_ev, gX.b0 + RT)]
                    if not isinstance(i, int) or i > 0:
                        prev.append((S("gate_evacuated"), n - 1))
                    block_product(gGate, 2 * i + (gGate.n0 + j), j, 0, x_in, 0, None, prev)
            peeled(pe, KT, gate_round)
            y_in = lambda part, k: (UH, UL)[part][:, k, :]
            pe.wait_ge(S("rnn_low"), RT)
            pe.wait_ge(S("gate_evacuated"), 2 * KT)
            products(gPR, 2, KT // 2, y_in, evac=lambda b: [(s_ev, b - 1)])
            products(gLat, 2, (QT + KVT) // 2, x_in, evac=lambda b: [(s_ev, b - 1)])
            products(gLat, 1, 1, x_in, first=QT + KVT - 1, evac=lambda b: [(s_ev, b - 1)])
            products(gRope, 1, 1, x_in, evac=lambda b: [(s_ev, b - 1)])
            mean_square("nq", QT)
            pe.wait_ge(S("nq_root"), 1)
            mean_square("nkv", KVT)
            pe.wait_ge(S("nkv_low"), KVT)
            pe.wait_ge(s_ev, gRope.b0 + 1)

            def head_products(s, par):
                pe.wait_ge(s_lo, s + (gHead.n0 + 1))
                slot = gHead.slot(par)
                if not isinstance(s, int) or s > 0:
                    pe.wait_ge(S("m_q_ready"), s)
                for k in range(QT):
                    mm = three(ps[:, 0, :], WH[slot][:, k, :], WL[slot][:, k, :], UH[:, k, :], UL[:, k, :], k == 0, k == QT - 1)
                mm.then_inc(S("m_q_made"), 1)
                if not isinstance(s, int) or s > 0:
                    pe.wait_ge(S("m_v_ready"), s)
                for k in range(KVT):
                    mm = three(ps[:, 1, :], WH[slot][:, QT + k, :], WL[slot][:, QT + k, :], UH[:, QT + k, :], UL[:, QT + k, :],
                               k == 0, k == KVT - 1)
                mm.then_inc(S("m_k_made"), 1)

            def head_values(s, par):
                slot = gHead.slot(par)
                pe.wait_ge(S("m_k_ready"), s + 1)
                for t in range(TB):
                    q = slice(t * P, (t + 1) * P)
                    for k in range(KVT):
                        mm = three(ps[:, 1, t * VH:(t + 1) * VH], UH[:, QT + k, q], UL[:, QT + k, q],
                                   WH[slot][:, QT + k, NOPE:P], WL[slot][:, QT + k, NOPE:P], k == 0, k == KVT - 1)
                mm.then_inc(s_mm, 1)

            def m_head(s, par, more=True):
                pe.wait_ge(S("m_q_ready"), s + 1)
                pe.wait_ge(S("m_k_ready"), s + 1)
                if more:
                    head_products(s + 1, 1 - par)
                for i in range(TB):
                    scores("m", s, i, lambda i: Qp[:, par, i * P:(i + 1) * P], lambda n: Kp[:, par, 0:n])
                    if not (isinstance(s, int) and s == 0):
                        turn("m", LP2, s - 1, 1 - par, i)
                if more:
                    head_values(s + 1, 1 - par)

            def m_weigh(s, par, p):
                pe.wait_ge(S("m_v_ready"), s + 1)
                weigh("m", PT2, s, par, p, lambda k: Vp[:, par, k, :])

            pe.wait_ge(S("krot_ready"), 2)
            head_products(0, 0)
            head_values(0, 0)
            m_head(0, 0)

            def m_pair(p):
                m_head(2 * p + 1, 1)
                m_weigh(2 * p, 0, p)
                m_head(2 * p + 2, 0)
                m_weigh(2 * p + 1, 1, p)
            repeat(pe, N_MLA // 2 - 1, m_pair)
            m_head(N_MLA - 1, 1, more=False)
            m_weigh(N_MLA - 2, 0, N_MLA // 2 - 1)
            for i in range(TB):
                turn("m", LP2, N_MLA - 1, 1, i)
            m_weigh(N_MLA - 1, 1, N_MLA // 2 - 1)
            products(gPM, 2, KT // 2, x_in, lambda k: (S("m_low"), k + 1), evac=lambda b: [(s_ev, b - 1)])
            products(gOut2, 2, KT // 2, y_in, lambda k: (S("merged_low"), k + 1), evac=lambda b: [(s_ev, b - 1)])
            mean_square("n5", KT)

            def up_round(p):
                for h in range(2):
                    prev = [(s_ev, gOut2.b0 + KT)]
                    if not isinstance(p, int) or p > 0:
                        prev.append((S(("up_gate", "up_value")[h]), p))
                    block_product(gUp, 2 * p + (gUp.n0 + h), h, 0, x_in, 0,
                                  (lambda k: (S("n5_low"), k + 1)) if h == 0 else None, prev)
            peeled(pe, FT, up_round)
            products(gDown, 2, KT // 2, y_in, lambda k: (S("up_low"), k + 1),
                     evac=lambda b: [(s_ev, b - 1), (S("up_value"), FT)])
            mean_square("n6", KT)
            for k in range(KT):
                pe.wait_ge(S("n6_done"), k + 1)
                if k >= 2:
                    pe.wait_ge(S("rows_ready"), k - 1)
                for t in range(TB):
                    mm = nc.tensor.transpose(ps[:, 4 + k % 2, t * P:(t + 1) * P], yout[:, k, t * P:(t + 1) * P], ident)
                mm.then_inc(S("y_turned"), 1)


INPUTS = ["x", "norm1_w", "w_in", "gla_w_a2", "gla_b_a", "gla_norm_w", "w_out", "norm2_w", "w_ff1", "w_ff2", "rel_bias",
          "final_norm_w", "c_2", "positions_2", "w_ada_2", "b_ada_2", "norm1_g_2", "w_in_2", "conv_w_2", "conv_b_2",
          "w_gate_a_2", "b_gate_a_2", "w_gate_x_2", "b_gate_x_2", "lru_param_2", "q_norm_g_2", "w_uq_2", "kv_norm_g_2",
          "w_ukv_2", "w_proj_rnn_2", "w_proj_mla_2", "w_out_2", "norm2_g_2", "w_up_2", "ffn_conv_w_2", "ffn_conv_b_2",
          "w_down_2", "final_g_2"]
WITHOUT_LAYERS = {"x", "rel_bias", "final_norm_w", "positions_2", "final_g_2"}


def kernel(**inputs):
    import concourse.bacc as bacc
    from concourse.bass_utils import run_bass_kernel_spmd

    nc = bacc.Bacc("TRN2", target_bir_lowering=False, num_devices=1)
    arrays, io = {}, {}

    def give(name, a):
        a = np.ascontiguousarray(a)
        arrays[f"in_{name}"] = a
        ap = nc.dram_tensor(f"in_{name}", a.shape, mybir.dt.from_np(a.dtype), kind="ExternalInput").ap()
        io[name] = ap if name in WITHOUT_LAYERS or name.startswith("const") else ap[0]

    for name in INPUTS:
        give(name, inputs[name])
    for name, a in shape_constants().items():
        give(name, a)
    out = nc.dram_tensor("out", (1, SEQ, D_MODEL), F32, kind="ExternalOutput").ap()
    hybrid_stack(nc, io, out)
    r = run_bass_kernel_spmd(nc, [arrays], core_ids=[0])
    return r.results[0]["out"]
```

```python
import math
from contextlib import ExitStack

import numpy as np

import concourse.bass as bass
from concourse import mybir

F32 = mybir.dt.float32
F32R = mybir.dt.float32r
I32 = mybir.dt.int32
ACT = mybir.ActivationFunctionType
ALU = mybir.AluOpType
AX_X = mybir.AxisListType.X
ds = bass.ds

P = 128
SEQ = 512
D_MODEL = 1024
KT = D_MODEL // P
TB = SEQ // P
EPS = 1e-6
NEG = -1e30
BIG = 3e38

HEAD_DIM = 64
A_HEADS = C_HEADS = 6
A_BRANCHES = ((128, 1), (512, 4), (2048, 16))
B_HEADS, B_KEY, B_VAL, B_RANK, B_TAU = 4, 32, 64, 16, 16.0
REL_BUCKETS, REL_MAX_DIST = 32, 2048
A_W, C_W, B_QK, B_W = A_HEADS * HEAD_DIM, C_HEADS * HEAD_DIM, B_HEADS * B_KEY, B_HEADS * B_VAL
COL_AQ, COL_AK, COL_AV = 0, A_W, 2 * A_W
COL_B = 3 * A_W
COL_CQ = COL_B + 2 * B_QK + 2 * B_W + B_RANK
COL_CK, COL_CV = COL_CQ + C_W, COL_CQ + 2 * C_W
NB_B = 7
PAIRS = (A_HEADS + C_HEADS) // 2
TAB = SEQ + P
GLA_GROUP = 4
GLA_GROUPS = B_VAL // GLA_GROUP
FF_GROUPS = 4 * D_MODEL // D_MODEL
ADA_COLS = 6 * D_MODEL // KT

ADA_DEEP = 4

D_RNN, RNN_BLOCK, CONV_W, LRU_C = 1280, 64, 4, 8.0
RT = D_RNN // P
LOG_TERMS = tuple(range(17, 0, -2))
N_MLA, NOPE, ROPE, VH, Q_LORA, KV_LORA = 16, 64, 32, 64, 384, 256
QKD = NOPE + ROPE
QT, KVT = Q_LORA // P, KV_LORA // P
ROPE_THETA = 10000.0
D_FF2, FFN_CONV = 2816, 3
FT = D_FF2 // P
COL_LAT, COL_ROPE, COL_GATE = D_RNN, D_RNN + Q_LORA + KV_LORA, D_RNN + Q_LORA + KV_LORA + ROPE
LAG = 5
DOWN_KS = (8, 7, 7)
RNN_KS = (5, 5)

VEC_GROUPS = [
    [("norm1_w", 8), ("norm2_w", 8), ("final_norm_w", 8), ("gla_norm_w", 2), ("gla_b_a", 1), ("norm1_g_2", 8),
     ("q_norm_g_2", 3), ("kv_norm_g_2", 2), ("norm2_g_2", 8), ("final_g_2", 8), ("c_2", 8),
     ("conv_b_2", 10), ("b_gate_a_2", 10), ("b_gate_x_2", 10), ("lru_param_2", 10)],
    [("conv_w_2", 40), ("b_ada_2", 48)],
    [("ffn_conv_w0", 44), ("ffn_conv_w1", 44)],
    [("ffn_conv_w2", 44), ("ffn_conv_b_2", 44)],
]
VEC = {}
VEC_ROWS = []
_at = 0
for _g in VEC_GROUPS:
    VEC_ROWS.append((_at, sum(n for _, n in _g)))
    for _name, _n in _g:
        VEC[_name] = _at
        _at += _n
N_VEC = _at

C_IDENT, C_STRIP = 0, P
C_HEADSUM = C_STRIP + SEQ
C_INVF = C_HEADSUM + B_HEADS
C_PHASE, C_TURN, C_EPS = C_INVF + 1, C_INVF + 2, C_INVF + 3
N_CONST = C_INVF + 4


def shape_constants():
    f32 = np.float32
    j = np.arange(TAB)
    dist = SEQ - 1 - j
    n = np.maximum(dist, 0)
    exact = REL_BUCKETS // 2
    logv = np.log(np.maximum(n, 1).astype(f32) / f32(exact)) / f32(math.log(REL_MAX_DIST / exact))
    large = np.minimum(exact + (logv * f32(REL_BUCKETS - exact)).astype(np.int32), REL_BUCKETS - 1)
    bucket = np.where(n < exact, n, large)
    onehot = (bucket[None, :] == np.arange(REL_BUCKETS)[:, None]).astype(f32)
    visits = np.zeros(TAB)
    for window, dilation in A_BRANCHES:
        visits += (dist >= 0) & (dist <= window) & (dist % dilation == 0)
    scale = math.sqrt(HEAD_DIM)
    mask_a = np.where(visits > 0, scale * np.log(np.maximum(visits, 1)), NEG)
    mask_c = np.where(dist >= 0, 0.0, NEG)
    mask = np.concatenate([np.tile(mask_a, (A_HEADS, 1)), np.tile(mask_c, (C_HEADS, 1))]).astype(f32)
    c = np.zeros((P, N_CONST), f32)
    p = np.arange(P)
    c[:, C_IDENT:C_IDENT + P] = np.eye(P)
    d = (SEQ - P) + p[:, None] - np.arange(SEQ)[None, :]
    c[:, C_STRIP:C_STRIP + SEQ] = np.where(d >= 0, 0.0, NEG)
    c[p, C_HEADSUM + p // B_KEY] = 1.0
    half = ROPE // 2
    rate = ROPE_THETA ** (-np.arange(half) / half)
    c[NOPE:, C_INVF] = np.concatenate([rate, rate, -rate, rate])
    c[:NOPE + ROPE, C_PHASE] = math.pi / 2
    c[:NOPE + ROPE, C_TURN] = 0.25
    c[:, C_EPS] = EPS
    return {"const_tile": c, "const_onehot": onehot, "const_mask": mask}


def repeat(eng, n, body):
    if n == 1:
        body(0)
    elif n > 1:
        with eng.Fori(0, n) as i:
            body(i)


def peeled(eng, n, body):
    body(0)
    repeat(eng, n - 1, lambda i: body(i + 1))


class Steps:

    def __init__(self, eng, sem):
        self.eng, self.sem, self.before, self.k, self.at, self.inside = eng, sem, 0, 0, 0, False

    def enter(self, i, per):
        if not self.inside:
            self.before += self.k
        self.k, self.at, self.per, self.inside = 0, per * i, per, True

    def leave(self, rounds):
        assert self.k == self.per, (self.k, self.per)
        self.before, self.k, self.at, self.inside = self.before + self.per * rounds, 0, 0, False

    def done(self, ins):
        self.k += 1
        ins.then_inc(self.sem, 1)
        self.eng.wait_ge(self.sem, self.at + (self.before + self.k))


class Phase:

    slots = 0
    blocks = 0

    def __init__(self, nb, ks=(KT,), counted=True):
        assert counted or nb % 2 == 0
        self.n0, self.b0, self.nb, self.ks = Phase.slots, Phase.blocks, nb, ks
        Phase.slots += nb * len(ks)
        Phase.blocks += nb * counted

    def slot(self, n):
        return (self.n0 + n) % 2

    def bank(self, b):
        return (self.b0 + b) % 2


def hybrid_stack(nc, io, out):
    Phase.slots = Phase.blocks = 0
    ctx = ExitStack()
    with ctx:
        sems = {}

        def S(name):
            if name not in sems:
                sems[name] = ctx.enter_context(nc.semaphore(name))
            return sems[name]

        top = [-(-nc.sbuf_base // 64) * 64]

        def place(name, shape, offset, dt=F32):
            return nc.alloc_sbuf_tensor_at(name, shape, dt, offset=offset)

        def size(shape):
            return 4 * int(np.prod(shape[1:]))

        def keep(name, shape, dt=F32):
            t = place(name, shape, top[0], dt)
            top[0] += -(-size(shape) // 64) * 64
            return t

        xT = keep("xT", [P, KT, SEQ])
        actH = keep("actH", [P, KT, SEQ], F32R)
        actL = keep("actL", [P, KT, SEQ], F32R)
        Wraw = [keep(f"Wraw{i}", [P, KT, P]) for i in range(2)]
        WH = [keep(f"WH{i}", [P, KT, P], F32R) for i in range(2)]
        WL = [keep(f"WL{i}", [P, KT, P], F32R) for i in range(2)]
        const = keep("const", [P, N_CONST])
        ones = keep("ones", [P, P])
        vec = keep("vec", [P, N_VEC])
        cact = keep("cact", [P, KT])
        mod = keep("mod", [P, 6 * KT])
        gainA = keep("gainA", [P, 2, KT])
        nsp = keep("nsp", [P, 3, RT])
        stat = keep("stat", [P, 4, 2, TB])
        rstd = keep("rstd", [P, SEQ])
        T = [keep(f"T{i}", [P, SEQ]) for i in range(6)]
        R = top[0]
        END = nc.sbuf_usable_end

        ident = const[:, C_IDENT:C_IDENT + P]
        strip = const[:, C_STRIP:C_STRIP + SEQ]
        headsum = const[:, C_HEADSUM:C_HEADSUM + B_HEADS]
        epsc = const[:, C_EPS:C_EPS + 1]

        def region(specs, start=R):
            made, at = [], start
            for name, shape, dt in specs:
                made.append(place(name, shape, at, dt))
                at += -(-size(shape) // 64) * 64
            assert at <= END, (at, END)
            return made

        bT, qT, kT, Vt, alpha, oTok, oSq, Z, Qs, Ks, Vs, vb, kvp, scanned, qs = region([
            ("bT", [P, NB_B, SEQ], F32), ("qT", [P, PAIRS, SEQ], F32), ("kT", [P, PAIRS, SEQ], F32),
            ("Vt", [P, PAIRS, TB, P], F32), ("alpha", [P, SEQ], F32), ("oTok", [P, TB, B_W], F32),
            ("oSq", [P, TB, B_W], F32), ("Z", [P, 2, SEQ], F32),
            ("Qs", [P, SEQ], F32), ("Ks", [P, SEQ], F32), ("Vs", [P, TB, P], F32),
            ("vb", [P, 2, GLA_GROUP, SEQ], F32), ("kvp", [P, GLA_GROUP, SEQ], F32), ("scanned", [P, 2, SEQ], F32),
            ("qs", [P, 2, GLA_GROUP, SEQ], F32)])
        vb0 = R + sum(size(t.shape) for t in (bT, qT, kT, Vt, alpha, oTok, oSq, Z, Qs, Ks, Vs))
        (LP,) = region([("LP", [P, 2, TB * (TB + 1) // 2 * P], F32)], vb0)
        (PT,) = region([("PT", [P, 2, TB, SEQ], F32)], vb0 + size(vb.shape) + size(kvp.shape) + size(scanned.shape))
        xn, vrows, onehot, maskt, relb, tabs, wa2 = region([
            ("xn", [P, TB, D_MODEL], F32), ("vrows", [P, len(VEC_GROUPS), P], F32), ("onehot", [REL_BUCKETS, TAB], F32),
            ("maskt", [2 * PAIRS, TAB], F32), ("relb", [REL_BUCKETS, 2 * PAIRS], F32), ("tabs", [2 * PAIRS, TAB], F32),
            ("wa2", [B_RANK, B_QK], F32)], R + size(bT.shape))
        UH, UL, adaacc = region([
            ("UH", [P, FT, SEQ], F32R), ("UL", [P, FT, SEQ], F32R), ("adaacc", [P, 6 * D_MODEL], F32)])
        (wada,) = region([("wada", [P, ADA_DEEP, ADA_COLS], F32)], R + size([P, 2 * KT, SEQ]))
        tailH, tailL, rest = R + size([P, RT, SEQ]), R + size(UH.shape) + size([P, RT, SEQ]), R + 2 * size(UH.shape)
        gR, PT2 = region([("gR", [P, KT, SEQ], F32), ("PT2", [P, TB, SEQ], F32)], tailH)
        r2, r4 = region([("r2", [P, SEQ], F32), ("r4", [P, SEQ], F32)], tailH)
        posr, BDa, BDx = region([("posr", [P, SEQ], I32), ("BDa", [P, 2, P], F32), ("BDx", [P, 2, P], F32)],
                                tailH + size(gR.shape))
        gM, Qp, Kp = region([("gM", [P, KT, SEQ], F32), ("Qp", [P, 2, SEQ], F32), ("Kp", [P, 2, SEQ], F32)], tailL)
        xc, rA, rTh = region([("xc", [P, RT, SEQ], F32), ("rA", [P, 2, SEQ], F32), ("rTh", [P, 2, SEQ], F32)], rest)
        LP2, lat, Vp, CS, Vf = region([
            ("LP2", [P, 2, TB * (TB + 1) // 2 * P], F32), ("lat", [P, QT + KVT, SEQ], F32),
            ("Vp", [P, 2, TB, VH], F32), ("CS", [P, SEQ], F32), ("Vf", [P, SEQ], F32)], rest)
        posb, rotk, rott = region([("posb", [P, SEQ], I32), ("rotk", [P, SEQ], F32), ("rott", [P, SEQ], F32)], rest)
        cg, cv, act2 = region([("cg", [P, 2, SEQ], F32), ("cv", [P, 2, SEQ], F32), ("act2", [P, 2, SEQ], F32)], rest)
        yout, yrow = region([("yout", [P, KT, SEQ], F32), ("yrow", [P, TB, D_MODEL], F32)])

        ps = ctx.enter_context(nc.psum_tensor("ps", [P, 8, SEQ], F32))
        tab_dram = nc.dram_tensor("tab_dram", [2 * PAIRS, TAB], F32, kind="Internal").ap()
        strip_dram = nc.dram_tensor("strip_dram", [2 * PAIRS, P, SEQ], F32, kind="Internal").ap()
        bv_dram = nc.dram_tensor("bv_dram", [B_W, SEQ], F32, kind="Internal").ap()

        gB = Phase(NB_B)
        gQK = Phase(4 * PAIRS // 2)
        gV = Phase(PAIRS)
        gOut = Phase(KT)
        gFF = [(Phase(KT, counted=False), Phase(KT, counted=False)) for _ in range(FF_GROUPS)]
        gX = Phase(RT)
        gGate = Phase(2 * KT, counted=False)
        gLat = Phase(QT + KVT)
        gRope = Phase(1)
        gPR = Phase(KT, RNN_KS)
        gHead = Phase(N_MLA, counted=False)
        gPM = Phase(KT)
        gOut2 = Phase(KT)
        gUp = Phase(2 * FT, counted=False)
        gDown = Phase(KT, DOWN_KS)

        s_raw = [S("raw0_loaded"), S("raw1_loaded")]
        s_hi, s_lo = S("weights_high"), S("weights_low")
        s_mm = S("block_multiplied")
        s_ev = S("block_evacuated")
        def wcols(name, rows0, kts):
            return io[name][rows0:rows0 + kts * P, :].rearrange("(k p) c -> p k c", p=P)

        loads = {}
        slot_base = {}
        total = [0, 0]
        for ph, dmas in ([(gB, 1), (gQK, 1), (gV, 1), (gOut, 3)] + [(g, 1) for pair in gFF for g in pair]
                         + [(gX, 1), (gGate, 1), (gLat, 1), (gRope, 3), (gPR, 1), (gHead, 4), (gPM, 1), (gOut2, 1),
                            (gUp, 1), (gDown, 1)]):
            loads[ph] = dmas
            slot_base[ph] = list(total)
            for n in range(ph.nb * len(ph.ks)):
                total[ph.slot(n)] += 16 * dmas

        def landed(ph, j, i=0, per=2):
            slot = ph.slot(j)
            k = len([x for x in range(j + 1) if ph.slot(x) == slot])
            return s_raw[slot], i * (16 * loads[ph] * (per // 2)) + (slot_base[ph][slot] + 16 * loads[ph] * k)

        norms = [("n1", KT, 1, 0), ("n2", KT, 1, 1), ("n3", KT, 0, 1), ("n4", KT, 1, 1), ("nq", QT, 1, 0),
                 ("nkv", KVT, 1, 0), ("n5", KT, 1, 1), ("n6", KT, 0, 1)]

        def N(name, kind, v):
            apart = kind in ("squared", "added")
            if name == "n4" and apart:
                return S("n4_" + kind), v
            for other, tiles, split, running in norms:
                if other == name:
                    return S("norm_" + kind), v
                if other != "n4" or not apart:
                    v += {"root": 1, "squared": tiles, "added": (tiles - 1) * running, "summed": 1 if running else tiles,
                          "done": tiles * (1 - split)}.get(kind, tiles * split)

        FF_SLOTS = 2 * KT

        block = ctx.enter_context(nc.Block())

        @block.sync
        def _(sp):
            def load(n, slot, pieces):
                if not isinstance(n, int) or n >= 2:
                    sp.wait_ge(s_lo, n - 1)
                for dst, src in pieces:
                    sp.dma_start(dst, src).then_inc(s_raw[slot], 16)

            def stream(ph, per, rounds, piece, first=0):
                def body(i):
                    for j in range(per):
                        slot = ph.slot(first + j)
                        load(per * i + (ph.n0 + first + j), slot, piece(i, j, slot))
                repeat(sp, rounds, body)

            def cols(view, kts, at):
                return lambda i, j, slot: [(Wraw[slot][:, 0:kts, :], view[:, :, ds(at(i, j), P)])]

            sp.dma_start(const[:], io["const_tile"]).then_inc(S("const_loaded"), 16)
            x_rows = io["x"][0].rearrange("(t p) d -> p t d", p=P)
            for h in range(2):
                q = slice(h * D_MODEL // 2, (h + 1) * D_MODEL // 2)
                sp.dma_start(xn[:, :, q], x_rows[:, :, q]).then_inc(S(f"x_loaded{h}"), 16)
            w_in = wcols("w_in", 0, KT)
            b_cols = cols(w_in, KT, lambda i, j: 2 * P * i + (COL_B + P * j))
            stream(gB, 2, 1, b_cols)
            for g, names in enumerate(VEC_GROUPS):
                r = 0
                for name, n in names:
                    if name.startswith("ffn_conv_w"):
                        src = io["ffn_conv_w_2"][int(name[-1])]
                    elif name == "conv_w_2":
                        src = io[name].rearrange("k c -> (k c)")
                    else:
                        src = io[name]
                    sp.dma_start(vrows[r:r + n, g, :], src.rearrange("(r c) -> r c", c=P)).then_inc(S("vec_loaded"), 16)
                    r += n
            for dst, src in ((onehot, io["const_onehot"]), (maskt, io["const_mask"]), (relb, io["rel_bias"]),
                             (wa2, io["gla_w_a2"])):
                sp.dma_start(dst[:], src).then_inc(S("tables_loaded"), 16)
            stream(gB, 2, NB_B // 2 - 1, cols(w_in, KT, lambda i, j: 2 * P * i + (COL_B + 2 * P + P * j)), first=2)
            stream(gB, 1, 1, cols(w_in, KT, lambda i, j: COL_B + P * (NB_B - 1)), first=NB_B - 1)
            bases = (COL_AQ, COL_AK, COL_CQ, COL_CK)

            def qk_load(c, i, j):
                slot = gQK.slot(j)
                load(gQK.n0 + c, slot, [(Wraw[slot][:], w_in[:, :, ds(P * i + bases[j], P)])])

            def v_load(c, i, j):
                slot = gV.slot(j)
                load(gQK.n0 + c, slot, [(Wraw[slot][:], w_in[:, :, ds(P * i + (COL_AV, COL_CV)[j], P)])])

            qk_load(0, 0, 0)
            qk_load(1, 0, 1)
            sp.wait_ge(s_ev, gB.b0 + 4)
            sp.dma_start(bv_dram.rearrange("(k p) t -> p k t", p=P), bT[:, 2:4, :]).then_inc(S("bv_stored"), 16)
            sp.wait_ge(S("bv_stored"), 16)

            def gla_values(g, par):
                if not isinstance(g, int) or g >= 2:
                    sp.wait_ge(S("gla_scanned"), GLA_GROUP * g - GLA_GROUP)
                for h in range(B_HEADS):
                    src = bv_dram[ds(h * B_VAL + GLA_GROUP * g, GLA_GROUP), :].rearrange("v t -> (v t)")
                    sp.dma_start(vb[h * B_KEY:(h + 1) * B_KEY, par, :, :].rearrange("p v t -> p (v t)"),
                                 src.unsqueeze(0).to_broadcast([B_KEY, GLA_GROUP * SEQ])
                                 ).then_inc(S(f"gla_values{par}"), 16)

            gla_values(0, 0)
            gla_values(1, 1)
            qk_load(2, 0, 2)
            qk_load(3, 0, 3)
            gla_values(2, 0)
            sp.wait_ge(S("tabs_ready"), 2)
            sp.dma_start(tab_dram, tabs[:]).then_inc(S("tab_stored"), 16)

            def qk_round(i):
                for j in range(4):
                    qk_load(4 * i + (4 + j), i + 1, j)
                    gla_values(4 * i + (3 + j), (3 + j) % 2)
            repeat(sp, 2, qk_round)
            sp.wait_ge(S("tab_stored"), 16)
            sp.dma_start(strip_dram, bass.AP(tab_dram.tensor, P - 1, [[TAB, 2 * PAIRS], [-1, P], [1, SEQ]])
                         ).then_inc(S("strips_stored"), 16)
            qk_blocks = 4 * PAIRS // 2

            def v_round(i):
                for j in range(2):
                    v_load(2 * i + (qk_blocks + j), i, j)
                    gla_values(2 * i + (qk_blocks - 1 + j), (qk_blocks - 1 + j) % 2)
            repeat(sp, PAIRS // 2 - 1, v_round)
            v_load(qk_blocks + PAIRS - 2, PAIRS // 2 - 1, 0)
            gla_values(GLA_GROUPS - 1, (GLA_GROUPS - 1) % 2)
            v_load(qk_blocks + PAIRS - 1, PAIRS // 2 - 1, 1)
            sp.wait_ge(S("strips_stored"), 16)

            def strip(s, par):
                if not isinstance(s, int) or s >= 2:
                    sp.wait_ge(S("a_logits"), 4 * s - 4)
                sp.dma_start(Z[:, par, :], strip_dram[ds(s, 1), :, :].rearrange("h p j -> (h p) j")
                             ).then_inc(S(f"strip_loaded{par}"), 16)
            strip(0, 0)
            strip(1, 1)
            w_out = wcols("w_out", 0, KT)
            a, b = A_W // P, (A_W + B_W) // P

            def out_blocks(i0):
                return lambda i, j, slot: [
                    (Wraw[slot][:, 0:a, :], w_out[:, 0:a, ds(2 * P * i + P * (2 * i0 + j), P)]),
                    (Wraw[slot][:, a:2 * a, :], w_out[:, b:KT, ds(2 * P * i + P * (2 * i0 + j), P)]),
                    (Wraw[slot][:, 2 * a:KT, :], w_out[:, a:b, ds(2 * P * i + P * (2 * i0 + j), P)])]
            stream(gOut, 2, 2, out_blocks(0))

            def strip_pair(p):
                for par in range(2):
                    strip(2 * p + (2 + par), par)
            repeat(sp, PAIRS - 1, strip_pair)
            stream(gOut, 2, KT // 2 - 2, out_blocks(2), first=4)
            ff1 = wcols("w_ff1", 0, KT)
            ff2 = io["w_ff2"].rearrange("(g k p) c -> g p k c", k=KT, p=P)
            ada = io["w_ada_2"].rearrange("(k p) (m c) -> k p m c", p=P, c=ADA_COLS)
            sp.wait_ge(S("a_low"), PAIRS)

            def ff_group(o):
                for gi in range(2):
                    for half in range(2):
                        ph = gFF[gi][half]

                        def body(q, gi=gi, half=half, ph=ph):
                            for h in range(2):
                                for j in range(2):
                                    b = 4 * q + (2 * h + j)
                                    slot = ph.slot(j)
                                    if half == 0:
                                        src = ff1[:, :, ds(P * b + (2 * KT * P * o + KT * P * gi), P)]
                                    else:
                                        src = ff2[ds(2 * o + gi, 1), :, :, ds(P * b, P)].rearrange("g p k c -> (g p) k c")
                                    load(2 * FF_SLOTS * o + b + ph.n0, slot, [(Wraw[slot][:], src)])
                                for j in range(2):
                                    e, c = 2 * h + j, 4 * KT * o + 4 * q + (2 * KT * gi + KT * half + 2 * h + j)
                                    if not isinstance(c, int) or c >= ADA_DEEP:
                                        sp.wait_ge(S("ada_used"), c - 2)
                                    sp.dma_start(wada[:, e, :],
                                                 ada[ds(4 * o + (2 * gi + half), 1), :, ds(4 * q + e, 1), :]
                                                 .rearrange("k p m c -> (k p) (m c)")).then_inc(S(f"ada_loaded{e}"), 16)
                        (repeat if gi or half or not isinstance(o, int) or o else peeled)(sp, KT // 4, body)
            peeled(sp, FF_GROUPS // 2, ff_group)
            w_in2 = wcols("w_in_2", 0, KT)
            wga = io["w_gate_a_2"].rearrange("(t b) d e -> t b d e", b=2)
            wgx = io["w_gate_x_2"].rearrange("(t b) d e -> t b d e", b=2)

            def rnn_gates(t, par):
                if not isinstance(t, int) or t >= 2:
                    sp.wait_ge(S("rnn_gated"), t - 1)
                for w, bd in ((wga, BDa), (wgx, BDx)):
                    for b in range(2):
                        q = slice(b * RNN_BLOCK, (b + 1) * RNN_BLOCK)
                        sp.dma_start(bd[q, par, q], w[ds(t, 1), b, :, :].rearrange("t d e -> (t d) e")
                                     ).then_inc(S(f"rnn_weights{par}"), 16)

            stream(gX, 2, RT // 2, cols(w_in2, KT, lambda i, j: 2 * P * i + P * j))
            sp.wait_ge(S("bd_cleared"), 2)
            sp.dma_start(posr[:], io["positions_2"].to_broadcast([P, SEQ])).then_inc(S("reset_loaded"), 16)
            rnn_gates(0, 0)
            rnn_gates(1, 1)
            stream(gGate, 2, 1, cols(w_in2, KT, lambda i, j: COL_GATE + P * j))
            pairs = RT // 2

            def gate_round(i):
                for j in range(2):
                    slot = gGate.slot(j)
                    load(2 * i + (gGate.n0 + 2 + j), slot,
                         [(Wraw[slot][:], w_in2[:, :, ds(2 * P * i + (COL_GATE + 2 * P + P * j), P)])])
                for j in range(2):
                    rnn_gates(2 * i + (2 + j), j)
            repeat(sp, pairs - 1, gate_round)
            stream(gGate, 2, KT - pairs, cols(w_in2, KT, lambda i, j: 2 * P * i + (COL_GATE + 2 * P * pairs + P * j)),
                   first=2 * pairs)
            sp.wait_ge(S("rnn_low"), RT)
            sp.dma_start(posb[:], io["positions_2"].to_broadcast([P, SEQ])).then_inc(S("pos_loaded"), 16)
            stream(gLat, 2, (QT + KVT) // 2, cols(w_in2, KT, lambda i, j: 2 * P * i + (COL_LAT + P * j)))
            stream(gLat, 1, 1, cols(w_in2, KT, lambda i, j: COL_LAT + P * (QT + KVT - 1)), first=QT + KVT - 1)
            half = ROPE // 2
            stream(gRope, 1, 1, lambda i, j, slot: [
                (Wraw[slot][:, :, 0:QKD], w_in2[:, :, COL_ROPE - NOPE:COL_ROPE + ROPE]),
                (Wraw[slot][:, :, QKD:QKD + half], w_in2[:, :, COL_ROPE + half:COL_ROPE + ROPE]),
                (Wraw[slot][:, :, QKD + half:P], w_in2[:, :, COL_ROPE:COL_ROPE + half])])
            wpr = io["w_proj_rnn_2"].rearrange("(q k p) c -> q p k c", k=RNN_KS[0], p=P)
            stream(gPR, 4, KT // 2, lambda i, j, slot: [
                (Wraw[slot][:, 0:RNN_KS[0], :], wpr[j % 2][:, :, ds(2 * P * i + P * (j // 2), P)])])
            wuq, wukv = wcols("w_uq_2", 0, QT), wcols("w_ukv_2", 0, KVT)
            stream(gHead, 2, N_MLA // 2, lambda i, j, slot: [
                (Wraw[slot][:, 0:QT, 0:QKD], wuq[:, :, ds(2 * QKD * i + QKD * j, QKD)]),
                (Wraw[slot][:, 0:QT, QKD:QKD + half], wuq[:, :, ds(2 * QKD * i + (QKD * j + NOPE + half), half)]),
                (Wraw[slot][:, 0:QT, QKD + half:P], wuq[:, :, ds(2 * QKD * i + (QKD * j + NOPE), half)]),
                (Wraw[slot][:, QT:QT + KVT, :], wukv[:, :, ds(2 * P * i + P * j, P)])])
            stream(gPM, 2, KT // 2, cols(wcols("w_proj_mla_2", 0, KT), KT, lambda i, j: 2 * P * i + P * j))
            stream(gOut2, 2, KT // 2, cols(wcols("w_out_2", 0, KT), KT, lambda i, j: 2 * P * i + P * j))
            stream(gUp, 2, FT, cols(wcols("w_up_2", 0, KT), KT, lambda i, j: P * i + D_FF2 * j))
            downs, r = [], 0
            for k in DOWN_KS:
                downs.append(wcols("w_down_2", r * P, k))
                r += k
            stream(gDown, 2 * len(DOWN_KS), KT // 2, lambda i, j, slot: [
                (Wraw[slot][:, 0:DOWN_KS[j % 3], :], downs[j % 3][:, :, ds(2 * P * i + P * (j // 3), P)])])
            y_rows = out[0].rearrange("(t p) d -> p t d", p=P)
            for h in range(KT // 2):
                q = slice(2 * P * h, 2 * P * (h + 1))
                sp.wait_ge(S("rows_ready"), 2 * h + 2)
                sp.dma_start(y_rows[:, :, q], yrow[:, :, q]).then_inc(S("stored"), 16)
            sp.wait_ge(S("stored"), 16 * (KT // 2))

        @block.gpsimd
        def _(pool):
            def low(n, slot, kts=KT):
                pool.wait_ge(s_hi, n + 1)
                nc.gpsimd.tensor_tensor(WL[slot][:, 0:kts, :], Wraw[slot][:, 0:kts, :],
                                        WH[slot][:, 0:kts, :].bitcast(F32), ALU.subtract).then_inc(s_lo, 1)

            def lows(ph, per, rounds, first=0, extra=0):
                def body(i):
                    for j in range(per):
                        low((per + extra) * i + (ph.n0 + first + j), ph.slot(first + j), ph.ks[(first + j) % len(ph.ks)])
                repeat(pool, rounds, body)

            nc.gpsimd.memset(ones[:], 1.0).then_inc(S("ones_set"), 1)
            lows(gB, 2, NB_B // 2)
            lows(gB, 1, 1, first=NB_B - 1)

            def gla_products(g, par):
                pool.wait_ge(S(f"gla_values{par}"), 32 * g + (64 - 32 * par))
                for j in range(GLA_GROUP - 1):
                    if not isinstance(g, int) or g > 0:
                        pool.wait_ge(S("gla_scanned"), GLA_GROUP * g + (j + 1 - GLA_GROUP))
                    nc.gpsimd.tensor_tensor(kvp[:, j, :], bT[:, 1, :], vb[:, par, j, :], ALU.mult).then_inc(S("gla_kv"), 1)

            lows(gQK, 2, 1)

            def gla_round(i):
                for j in range(2):
                    gla_products(2 * i + j, j)
                    low(2 * i + (gQK.n0 + 2 + j), gQK.slot(j))
            peeled(pool, GLA_GROUPS // 2, gla_round)
            pool.wait_ge(s_ev, gV.b0)
            pool.wait_ge(S("values_turned"), PAIRS)

            def stage_qk(s, t, par):
                q = slice(HEAD_DIM * par, HEAD_DIM * (par + 1))
                if not isinstance(s, int) or s >= 2:
                    pool.wait_ge(S("a_v_staged"), s - 1)
                    pool.wait_ge(S("a_scored"), 4 * s - 4)
                for staged, src in ((Qs, qT), (Ks, kT)):
                    nc.gpsimd.tensor_copy(staged[q, :], src[q, ds(t, 1), :].rearrange("p a t -> p (a t)")
                                          ).then_inc(S("a_qk_staged"), 1)

            def stage_v(s, t, par, staged):
                q = slice(HEAD_DIM * par, HEAD_DIM * (par + 1))
                pool.wait_ge(S("a_qk_staged"), 2 * staged)
                if not isinstance(s, int) or s >= 2:
                    pool.wait_ge(S("a_weighted"), s - 1)
                nc.gpsimd.tensor_copy(Vs[:, :, q], Vt[:, ds(t, 1), :, q].rearrange("p a t d -> p (a t) d")
                                      ).then_inc(S("a_v_staged"), 1)

            stage_qk(0, 0, 0)
            stage_qk(1, 0, 1)
            stage_v(0, 0, 0, 2)

            def stage_pair(p):
                stage_qk(2 * p + 2, p + 1, 0)
                stage_v(2 * p + 1, p, 1, 2 * p + 3)
                stage_qk(2 * p + 3, p + 1, 1)
                stage_v(2 * p + 2, p + 1, 0, 2 * p + 4)
            lows(gOut, 2, 1)
            peeled(pool, PAIRS - 1, stage_pair)
            stage_v(2 * PAIRS - 1, PAIRS - 1, 1, 2 * PAIRS)
            pool.wait_ge(S("a_low"), PAIRS)
            nc.gpsimd.memset(adaacc[:], 0.0).then_inc(S("ada_used"), 1)
            lows(gOut, 2, KT // 2 - 1, first=2)

            def ff_group(o):
                for gi in range(2):
                    for half in range(2):
                        ph = gFF[gi][half]

                        def body(p, ph=ph):
                            for j in range(2):
                                low(2 * FF_SLOTS * o + 2 * p + (ph.n0 + j), ph.slot(j))
                        repeat(pool, KT // 2, body)
            repeat(pool, FF_GROUPS // 2, ff_group)
            lows(gX, 2, 1)
            pool.wait_ge(S("ada_used"), 1 + 2 * KT * FF_GROUPS)
            nc.gpsimd.memset(BDa[:], 0.0).then_inc(S("bd_cleared"), 1)
            nc.gpsimd.memset(BDx[:], 0.0).then_inc(S("bd_cleared"), 1)
            lows(gX, 2, RT // 2 - 1, first=2)
            lows(gGate, 2, KT)
            lows(gLat, 2, (QT + KVT) // 2)
            lows(gLat, 1, 1, first=QT + KVT - 1)
            lows(gRope, 1, 1)
            lows(gPR, 4, KT // 2)

            def heads(i):
                for j in range(2):
                    low(2 * i + (gHead.n0 + j), gHead.slot(j), QT + KVT)
            repeat(pool, N_MLA // 2, heads)
            for ph in (gPM, gOut2):
                lows(ph, 2, KT // 2)
            lows(gUp, 2, FT)
            lows(gDown, 2 * len(DOWN_KS), KT // 2)

        @block.scalar
        def _(act):
            own = Steps(act, S("scalar_steps"))
            A = nc.scalar.activation

            def high(ph, j, n, loaded, kts=KT):
                act.wait_ge(*loaded)
                if not isinstance(n, int) or n >= 2:
                    act.wait_ge(s_mm, n - 1)
                slot = ph.slot(j)
                A(WH[slot][:, 0:kts, :], Wraw[slot][:, 0:kts, :], ACT.Copy).then_inc(s_hi, 1)

            def highs(ph, per, rounds, first=0):
                def body(i):
                    for j in range(per):
                        high(ph, first + j, per * i + (ph.n0 + first + j), landed(ph, first + j, i, per),
                             ph.ks[(first + j) % len(ph.ks)])
                repeat(act, rounds, body)

            def ff_high(ph, j, o, p, at=0):
                per = FF_SLOTS
                sem, v = landed(ph, j)
                high(ph, j, 2 * FF_SLOTS * o + 2 * p + (ph.n0 + j), (sem, 16 * per * o + 16 * p + v))

            def squares(name, tiles, src, there=None):
                for k in range(tiles):
                    if there is not None:
                        act.wait_ge(*there(k))
                    if k >= 2:
                        act.wait_ge(*N(name, "summed", k - 1))
                    A(T[k % 2][:], src(k), ACT.Square).then_inc(S("norm_squared"), 1)

            def square(name, k, j, there, at=0, acc=5, weight=None):
                act.wait_ge(*there)
                if not isinstance(k, int) or k >= 3:
                    act.wait_ge(*N(name, "added", k - 2))
                A(T[acc if isinstance(k, int) and k == 0 else at + j][:], xT[:, ds(k, 1), :].rearrange("p a t -> p (a t)"),
                  ACT.Square, **({} if weight is None else {"scale": vec[:, ds(k + VEC[weight], 1)]})
                  ).then_inc(N(name, "squared", 0)[0], 1)

            def root(name, sums, dim, dst=None, bank=2):
                act.wait_ge(*N(name, "summed", sums))
                A((rstd if dst is None else dst)[:], ps[:, bank, :], ACT.Sqrt, bias=epsc, scale=1.0 / dim
                  ).then_inc(S("norm_root"), 1)

            def norm_highs(name, tiles, dsts, shift=None):
                for k in range(tiles):
                    act.wait_ge(*N(name, "scaled", k + 1))
                    A(dsts(k), T[2 + k % 4][:], ACT.Copy if shift is None else ACT.Identity,
                      **({} if shift is None else {"bias": shift(k)})).then_inc(S("norm_high"), 1)

            highs(gB, 2, 1)
            squares("n1", KT, lambda k: xT[:, k, :], lambda k: (S("x_turned"), k + 1))
            act.wait_ge(S("const_loaded"), 16)
            root("n1", KT, D_MODEL)
            norm_highs("n1", KT, lambda k: actH[:, k, :])
            highs(gB, 2, NB_B // 2 - 1, first=2)
            highs(gB, 1, 1, first=NB_B - 1)
            highs(gQK, 2, 1)
            act.wait_ge(s_ev, gB.b0 + NB_B)
            A(bT[:, 4:6, :], bT[:, 4:6, :], ACT.Silu).then_inc(S("gla_silu"), 1)
            act.wait_ge(S("gla_zmin"), 1)
            own.done(A(T[1][:], ps[:, 2, :], ACT.Abs, bias=vec[:, VEC["gla_b_a"]:VEC["gla_b_a"] + 1]))
            own.done(A(T[1][:], T[1][:], ACT.Exp, scale=-1.0))
            A(T[1][:], T[1][:], ACT.Ln, bias=ones[:, 0:1]).then_inc(S("gla_log"), 1)
            act.wait_ge(S("gla_logsig"), 1)
            A(alpha[:], T[0][:], ACT.Exp, scale=1.0 / B_TAU).then_inc(S("gla_alpha"), 1)
            act.wait_ge(S("tab_stored"), 16)

            def qk_evac(i, j):
                act.wait_ge(s_mm, 4 * i + (gQK.n0 + j + 1))
                A((qT, kT)[j % 2][:, ds(i + (PAIRS // 2) * (j // 2), 1), :].rearrange("p a t -> p (a t)"),
                  ps[:, gQK.bank(j), :], ACT.Copy).then_inc(s_ev, 1)

            def qk_round(i):
                for j in range(4):
                    high(gQK, 2 + j, 4 * i + (gQK.n0 + 2 + j), landed(gQK, 2 + j, i, 4))
                    qk_evac(i, j)
            repeat(act, PAIRS // 2 - 1, qk_round)
            last = PAIRS // 2 - 1
            for j in range(4):
                if j < 2:
                    high(gQK, 2 + j, 4 * last + gQK.n0 + 2 + j, landed(gQK, 2 + j, last, 4))
                else:
                    high(gV, j - 2, gV.n0 + j - 2, landed(gV, j - 2))
                qk_evac(last, j)

            def values_turned(v):
                act.wait_ge(S("v_turned"), v + 1)
                A(Vt[:, v // 2 + PAIRS // 2 * (v % 2), :, :].rearrange("p t d -> p (t d)"), ps[:, 5 + v % 2, :], ACT.Copy
                  ).then_inc(S("values_turned"), 1)

            for v in range(PAIRS):
                if v + 2 < PAIRS:
                    high(gV, v + 2, gV.n0 + v + 2, landed(gV, v + 2))
                act.wait_ge(s_mm, gV.n0 + v + 1)
                if v >= 2:
                    act.wait_ge(S("v_turned"), v - 1)
                A(T[2 + v % 2][:], ps[:, gV.bank(v), :], ACT.Copy).then_inc(s_ev, 1)
                if v:
                    values_turned(v - 1)
            values_turned(PAIRS - 1)
            act.wait_ge(S("gla_ms"), 1)
            A(T[0][:, 0:16], T[0][:, 0:16], ACT.Sqrt, bias=epsc, scale=1.0 / B_VAL).then_inc(S("gla_root"), 1)
            highs(gOut, 2, 1)
            for e in range(2):
                act.wait_ge(S("gla_out"), e + 1)
                A(actH[:, 2 * A_W // P + e, :], T[2 + e][:], ACT.Copy).then_inc(S("gla_high"), 1)

            def exps(pre, lp, s, par, i):
                off = i * (i + 1) // 2 * P
                act.wait_ge(S(pre + "_logits"), 4 * s + (i + 1))
                A(lp[:, par, off:off + (i + 1) * P], lp[:, par, off:off + (i + 1) * P], ACT.Exp,
                  bias=stat[:, 0, par, i:i + 1], scale=-1.0, accum_out=stat[:, 1, par, i:i + 1]
                  ).then_inc(S(pre + "_exp"), 1)

            def turned(pre, pt, s, i):
                act.wait_ge(S(pre + "_turned"), 4 * s + (i + 1))
                A(pt[:, 0:i + 1, i * P:(i + 1) * P], ps[:, 5 + i % 2, 0:(i + 1) * P].rearrange("p (k q) -> p k q", q=P),
                  ACT.Copy).then_inc(S(pre + "_pt"), 1)

            def pair_high(pre, p, dst):
                act.wait_ge(S(pre + "_weighted"), 2 * p + 2)
                A(dst[:, ds(p, 1), :].rearrange("p a t -> p (a t)"), ps[:, 7, :], ACT.Copy
                  ).then_inc(S(pre + "_high"), 1)

            def a_turned(s, par, i):
                turned("a", PT[:, par], s, i)

            def a_step(s, par):
                for i in range(TB):
                    exps("a", LP, s, par, i)
                    if not (isinstance(s, int) and s == 0):
                        a_turned(s - 1, 1 - par, i)

            a_step(0, 0)
            a_step(1, 1)

            def pair(p):
                a_step(2 * p + 2, 0)
                a_step(2 * p + 3, 1)
                pair_high("a", p, actH)
            repeat(act, PAIRS - 1, pair)
            for i in range(TB):
                a_turned(2 * PAIRS - 1, 1, i)
            pair_high("a", PAIRS - 1, actH)
            def out_squares(name, ph, next_high):
                def body(i, last=False):
                    for j in range(2):
                        if last:
                            next_high(j)
                        else:
                            high(ph, 2 + j, 2 * i + (ph.n0 + 2 + j), landed(ph, 2 + j, i))
                        square(name, 2 * i + j, j, (s_ev, 2 * i + (ph.b0 + j + 1)))
                peeled(act, KT // 2 - 1, body)
                body(KT // 2 - 1, True)
            out_squares("n2", gOut, lambda j: ff_high(gFF[0][0], j, 0, 0))
            root("n2", 1, D_MODEL)
            norm_highs("n2", KT, lambda k: actH[:, k, :])
            A(cact[:], vec[:, VEC["c_2"]:VEC["c_2"] + KT], ACT.Silu).then_inc(S("c_ready"), 1)
            own.done(A(nsp[:, 1, :], vec[:, VEC["lru_param_2"]:VEC["lru_param_2"] + RT], ACT.Abs))
            A(nsp[:, 1, :], nsp[:, 1, :], ACT.Exp, scale=-1.0).then_inc(S("lru_exp"), 1)

            def relu(ph, o, gi, p, j):
                b = 2 * FF_SLOTS * o + 2 * p + (ph.b0 + j)
                f = 2 * KT * o + 2 * p + (KT * gi + j)
                act.wait_ge(s_mm, 2 * FF_SLOTS * o + 2 * p + (ph.n0 + j + 1))
                if not isinstance(f, int) or f >= 2:
                    act.wait_ge(S("hid_squared"), f - 1)
                A(T[j][:], ps[:, ph.bank(j), :], ACT.Relu).then_inc(s_ev_act, 1)

            def square_high(o, gi, p, j):
                f = 2 * KT * o + 2 * p + (KT * gi + j)
                act.wait_ge(S("hid_squared"), f + 1)
                A(UH[:, ds(2 * p + (KT * gi + j), 1), :].rearrange("p a t -> p (a t)"), T[2 + j][:], ACT.Copy
                  ).then_inc(S("hid_high"), 1)

            s_ev_act = S("hid_relu")

            def ff_group(o):
                for gi in range(2):
                    one, two = gFF[gi]
                    nxt = gFF[gi + 1][0] if gi == 0 else None

                    def first(p, one=one, gi=gi):
                        for j in range(2):
                            ff_high(one, j, o, p + 1)
                            relu(one, o, gi, p, j)
                        for j in range(2):
                            square_high(o, gi, p, j)
                    (repeat if o or gi else peeled)(act, KT // 2 - 1, first)
                    for j in range(2):
                        ff_high(two, j, o, 0)
                        relu(one, o, gi, KT // 2 - 1, j)
                    for j in range(2):
                        square_high(o, gi, KT // 2 - 1, j)

                    last = o == FF_GROUPS // 2 - 1 and gi == 1

                    def second(p, two=two, last=last):
                        for j in range(2):
                            ff_high(two, j, o, p + 1)
                            if last:
                                final_squares(p, j)
                    (peeled if last else repeat)(act, KT // 2 - 1, second)
                    if gi == 0:
                        for j in range(2):
                            ff_high(nxt, j, o, 0)
            def final_squares(p, j):
                there = (S("x_added"), 2 * p + (KT * (FF_GROUPS - 1) + j + 1))
                square("n3", 2 * p + j, j, there)
                square("n4", 2 * p + j, j, there, 2, 4, "final_norm_w")
            ff_group(0)
            for j in range(2):
                ff_high(gFF[0][0], j, 1, 0)
            ff_group(1)
            for j in range(2):
                high(gX, j, gX.n0 + j, landed(gX, j))
                final_squares(KT // 2 - 1, j)
            root("n3", 1, D_MODEL)
            act.wait_ge(S("n4_mean"), 1)
            A(r4[:], r2[:], ACT.Sqrt, bias=epsc, scale=1.0 / D_MODEL).then_inc(S("norm_root"), 1)
            act.wait_ge(S("mod_ready"), 1)
            norm_highs("n4", KT, lambda k: actH[:, k, :], lambda k: mod[:, k:k + 1])

            def bias_at(name, t, j):
                return vec[:, ds(t + (VEC[name] + j), 1)]

            def rnn_sigmoids(t, j):
                act.wait_ge(S("rnn_gated"), t + (j + 1))
                if not isinstance(t, int) or t > 0:
                    act.wait_ge(S("rnn_low"), t + (j - 1))
                A(T[j][:], ps[:, 2 + 2 * j, :], ACT.Sigmoid, bias=bias_at("b_gate_a_2", t, j)).then_inc(S("rnn_sig"), 1)
                A(T[2 + j][:], ps[:, 3 + 2 * j, :], ACT.Sigmoid, bias=bias_at("b_gate_x_2", t, j)).then_inc(S("rnn_sig"), 1)

            def rnn_rest(t):
                marks = []
                for j in range(2):
                    act.wait_ge(S("rnn_loga"), t + (j + 1))
                    A(rA[:, j, :], T[j][:], ACT.Exp).then_inc(S("rnn_a"), 1)
                    A(rTh[:, j, :], T[j][:], ACT.Tanh, scale=-1.0).then_inc(S("rnn_tanh"), 1)
                for j in range(2):
                    act.wait_ge(S("rnn_m2"), t + (j + 1))
                    A(rTh[:, j, :], rTh[:, j, :], ACT.Sqrt).then_inc(S("rnn_mult"), 1)
                for j in range(2):
                    act.wait_ge(S("rnn_state"), t + (j + 1))
                    A(UH[:, ds(t + j, 1), :].rearrange("p a t -> p (a t)"), T[j][:], ACT.Copy).then_inc(S("rnn_high"), 1)

            highs(gX, 2, RT // 2 - 1, first=2)
            highs(gGate, 2, 1)

            def gate_round(dst, t0, rnn=False, ahead=True):
                def body(i):
                    for j in range(2):
                        if ahead:
                            high(gGate, 2 + j, 2 * i + (gGate.n0 + 2 + j), landed(gGate, 2 + j, i))
                        else:
                            high(gLat, j, gLat.n0 + j, landed(gLat, j))
                        act.wait_ge(s_mm, 2 * i + (gGate.n0 + j + 1))
                        A(dst[:, ds(2 * i + (j - t0), 1), :].rearrange("p a t -> p (a t)"), ps[:, gGate.bank(j), :],
                          ACT.Sigmoid).then_inc(S("gate_evacuated"), 1)
                        if rnn:
                            rnn_sigmoids(2 * i, j)
                    if rnn:
                        rnn_rest(2 * i)
                return body
            peeled(act, KT // 2, gate_round(gR, 0, rnn=True))
            for i in range(KT // 2, RT // 2):
                gate_round(gM, KT, rnn=True)(i)
            for i in range(RT // 2, KT):
                gate_round(gM, KT, ahead=i + 1 < KT)(i)
            act.wait_ge(S("rot_angle"), 1)
            A(CS[NOPE:P, :], rott[NOPE:P, :], ACT.Sin).then_inc(S("rot_ready"), 1)
            for b in range(2, QT + KVT):
                high(gLat, b, gLat.n0 + b, landed(gLat, b))
            high(gRope, 0, gRope.n0, landed(gRope, 0))
            act.wait_ge(s_ev, gLat.b0 + QT)
            squares("nq", QT, lambda k: lat[:, k, :])

            def pr_high(n):
                high(gPR, n, gPR.n0 + n, landed(gPR, n), RNN_KS[n % 2])
            pr_high(0)
            root("nq", QT, Q_LORA)
            act.wait_ge(s_ev, gLat.b0 + QT + KVT)
            squares("nkv", KVT, lambda k: lat[:, QT + k, :])
            pr_high(1)
            root("nkv", KVT, KV_LORA, Vf, 3)
            norm_highs("nq", QT, lambda k: actH[:, k, :])
            pr_high(2)
            norm_highs("nkv", KVT, lambda k: actH[:, QT + k, :])
            pr_high(3)

            def pr_round(i):
                for j in range(4):
                    high(gPR, j, 4 * i + (gPR.n0 + 4 + j), landed(gPR, 4 + j, i, 4), RNN_KS[j % 2])
            repeat(act, KT // 2 - 1, pr_round)

            def head_high(s, par):
                sem, v = landed(gHead, par)
                p = (s - par) // 2 if isinstance(s, int) else None
                high(gHead, par, s + gHead.n0, (sem, 64 * p + v) if p is not None else (sem, (s - par) * 32 + v),
                     QT + KVT)

            def key_evac(s, par):
                act.wait_ge(s_mm, s + (gHead.n0 + 1))
                A(Kp[0:NOPE, par, :], ps[0:NOPE, 1, :], ACT.Copy).then_inc(S("m_k_ready"), 1)

            def value_evac(s, par):
                act.wait_ge(S("m_v_turned"), s + 1)
                if not isinstance(s, int) or s >= 2:
                    act.wait_ge(S("m_weighted"), s - 1)
                A(Vp[:, par, :, :], ps[:, 1, 0:TB * VH].rearrange("p (t d) -> p t d", d=VH), ACT.Copy
                  ).then_inc(S("m_v_ready"), 1)

            head_high(0, 0)
            head_high(1, 1)
            key_evac(0, 0)
            value_evac(0, 0)

            def head(s, par, more, ahead):
                for i in range(TB):
                    exps("m", LP2, s, par, i)
                    if not (isinstance(s, int) and s == 0):
                        turned("m", PT2, s - 1, i)
                if more:
                    key_evac(s + 1, 1 - par)
                if ahead:
                    head_high(s + 2, par)
                if more:
                    value_evac(s + 1, 1 - par)

            head(0, 0, True, True)

            def head_pair(p):
                head(2 * p + 1, 1, True, True)
                head(2 * p + 2, 0, True, True)
                pair_high("m", p, UH)
            repeat(act, N_MLA // 2 - 2, head_pair)
            head(N_MLA - 3, 1, True, True)
            head(N_MLA - 2, 0, True, False)
            pair_high("m", N_MLA // 2 - 2, UH)
            head(N_MLA - 1, 1, False, False)
            for i in range(TB):
                turned("m", PT2, N_MLA - 1, i)
            highs(gPM, 2, 1)
            pair_high("m", N_MLA // 2 - 1, UH)

            def merged_high(p, j):
                act.wait_ge(S("merged"), 2 * p + (j + 1))
                A(actH[:, ds(2 * p + j, 1), :].rearrange("p a t -> p (a t)"), T[j][:], ACT.Copy).then_inc(S("merged_high"), 1)

            def pm_round(p):
                for j in range(2):
                    sem, v = landed(gPM, 2 + j)
                    high(gPM, j, 2 * p + (gPM.n0 + 2 + j), (sem, 16 * p + v))
                for j in range(2):
                    merged_high(p, j)
            repeat(act, KT // 2 - 1, pm_round)
            highs(gOut2, 2, 1)
            for j in range(2):
                merged_high(KT // 2 - 1, j)
            out_squares("n5", gOut2, lambda j: high(gUp, j, gUp.n0 + j, landed(gUp, j)))
            root("n5", 1, D_MODEL)
            act.wait_ge(S("mod_ready"), 2)
            norm_highs("n5", KT, lambda k: actH[:, k, :], lambda k: mod[:, 3 * KT + k:3 * KT + k + 1])

            def up_parts(t, j):
                act.wait_ge(S("up_gate"), t + 1)
                if not isinstance(t, int) or t >= 2:
                    act.wait_ge(S("up_low"), t - 1)
                A(act2[:, j, :], cg[:, j, :], ACT.Silu).then_inc(S("up_silu"), 1)

            def up_high(t, j):
                act.wait_ge(S("up_product"), t + 1)
                A(UH[:, ds(t, 1), :].rearrange("p a t -> p (a t)"), act2[:, j, :], ACT.Copy).then_inc(S("up_high"), 1)

            def up_round(p):
                for j in range(2):
                    for h in range(2):
                        sem, v = landed(gUp, 2 * j + 2 + h)
                        high(gUp, h, 4 * p + (gUp.n0 + 2 * j + 2 + h), (sem, 32 * p + v))
                    up_parts(2 * p + j, j)
                    up_high(2 * p + j, j)
            peeled(act, FT // 2 - 1, up_round)
            for h in range(2):
                high(gUp, h, gUp.n0 + 2 * FT - 2 + h, landed(gUp, 2 * FT - 2 + h))
            up_parts(FT - 2, 0)
            up_high(FT - 2, 0)
            for h in range(2):
                high(gDown, h, gDown.n0 + h, landed(gDown, h), DOWN_KS[h])
            up_parts(FT - 1, 1)
            up_high(FT - 1, 1)
            n = len(DOWN_KS)

            def down_round(i, last=False):
                for j in range(2 * n):
                    if not (last and j >= 2 * n - 2):
                        high(gDown, 2 + j, 2 * n * i + (gDown.n0 + 2 + j), landed(gDown, 2 + j, i, 2 * n), DOWN_KS[(2 + j) % n])
                    if j % n == n - 1:
                        square("n6", 2 * i + j // n, j // n, (s_ev, 2 * i + (gDown.b0 + j // n + 1)))
            peeled(act, KT // 2 - 1, down_round)
            down_round(KT // 2 - 1, True)
            root("n6", 1, D_MODEL)
            for k in range(KT):
                act.wait_ge(S("y_turned"), k + 1)
                A(yrow[:, :, k * P:(k + 1) * P], ps[:, 4 + k % 2, :].rearrange("p (t f) -> p t f", f=P), ACT.Copy
                  ).then_inc(S("rows_ready"), 1)

        @block.vector
        def _(dve):
            own = Steps(dve, S("vector_steps"))
            V = nc.vector

            def vcol(name, k=0):
                return vec[:, VEC[name] + k:VEC[name] + k + 1]

            def copies(ph, per, rounds, dst, first=0, after=0):
                def body(i):
                    for j in range(per):
                        n = per * i + (ph.n0 + first + j)
                        dve.wait_ge(s_mm, n + 1)
                        V.tensor_copy(dst(i, j), ps[:, ph.bank(first + j), :]).then_inc(s_ev, 1)
                repeat(dve, rounds, body)

            def add_square(name, k, j, at=0, acc=5):
                if isinstance(k, int) and k == 0:
                    return
                dve.wait_ge(*N(name, "squared", k + 1))
                if not isinstance(k, int) or k >= 2:
                    dve.wait_ge(*N(name, "added", k - 1))
                V.tensor_tensor(T[acc][:], T[acc][:], T[at + j][:], ALU.add).then_inc(N(name, "added", 0)[0], 1)

            def adds(ph, name, gate=None, per=1):
                def body(i):
                    for j in range(2):
                        dve.wait_ge(s_mm, 2 * per * i + (ph.n0 + per * (j + 1)))
                        x = xT[:, ds(2 * i + j, 1), :].rearrange("p a t -> p (a t)")
                        if gate is None:
                            V.tensor_tensor(x, ps[:, ph.bank(j), :], x, ALU.add).then_inc(s_ev, 1)
                        else:
                            V.scalar_tensor_tensor(x, ps[:, ph.bank(j), :], mod[:, ds(2 * i + (gate + j), 1)], x,
                                                   ALU.mult, ALU.add).then_inc(s_ev, 1)
                        add_square(name, 2 * i + j, j)
                return body

            def norm_scaled(name, k, src, gain, by):
                V.scalar_tensor_tensor(T[2 + k % 4][:], src(k), gain(k), by[:], ALU.mult, ALU.mult
                                       ).then_inc(S("norm_scaled"), 1)

            def norm_split(name, tiles, src, gain, dstL, dstH, shift=None, by=None):
                for k in range(tiles):
                    if k >= 4:
                        low(name, k - 4, dstL, dstH, shift)
                        dve.wait_ge(*N(name, "low", k - 3))
                    norm_scaled(name, k, src, gain, rstd if by is None else by)
                for k in range(max(0, tiles - 4), tiles):
                    low(name, k, dstL, dstH, shift)

            def norm_plain(src, gain, dst):
                for k in range(KT):
                    V.scalar_tensor_tensor(dst(k), src(k), gain(k), rstd[:], ALU.mult, ALU.mult).then_inc(S("norm_done"), 1)

            def norm_parts(name, *args, **kw):
                dve.wait_ge(*N(name, "root", 1))
                own.done(V.reciprocal(rstd[:], rstd[:]))
                norm_split(name, *args, **kw)

            def low(name, k, dstL, dstH, shift):
                dve.wait_ge(*N(name, "high", k + 1))
                t = T[2 + k % 4][:]
                if shift is None:
                    V.tensor_tensor(dstL(k), t, dstH(k).bitcast(F32), ALU.subtract).then_inc(S("norm_low"), 1)
                else:
                    V.scalar_tensor_tensor(dstL(k), t, shift(k), dstH(k).bitcast(F32), ALU.add, ALU.subtract
                                           ).then_inc(S("norm_low"), 1)

            for k in range(KT):
                dve.wait_ge(S("x_transposed"), k + 1)
                V.tensor_copy(xT[:, k, :], ps[:, 6 + k % 2, :]).then_inc(S("x_turned"), 1)
            for g, (at, n) in enumerate(VEC_ROWS):
                dve.wait_ge(S("vec_transposed"), g + 1)
                V.tensor_copy(vec[:, at:at + n], ps[:, 2 + g, 0:n]).then_inc(S("vecs_turned"), 1)
            dve.wait_ge(S("tabs_made"), 1)
            dve.wait_ge(S("tables_loaded"), 64)
            for h in range(2):
                q = slice(h * TAB // 2, (h + 1) * TAB // 2)
                V.scalar_tensor_tensor(tabs[:, q], ps[0:2 * PAIRS, 3 + h, 0:TAB // 2], math.sqrt(HEAD_DIM), maskt[:, q],
                                       ALU.mult, ALU.add).then_inc(S("tabs_ready"), 1)
            dve.wait_ge(S("vecs_turned"), len(VEC_GROUPS))
            dve.wait_ge(S("x_turned"), KT)
            norm_parts("n1", KT, lambda k: xT[:, k, :], lambda k: vcol("norm1_w", k), lambda k: actL[:, k, :],
                       lambda k: actH[:, k, :])
            copies(gB, 2, NB_B // 2, lambda i, j: bT[:, ds(2 * i + j, 1), :].rearrange("p a t -> p (a t)"))
            copies(gB, 1, 1, lambda i, j: bT[:, NB_B - 1, :], first=NB_B - 1)
            dve.wait_ge(s_ev, gB.b0 + NB_B)
            own.done(V.tensor_scalar(bT[:, 0, :], bT[:, 0, :], float(B_KEY ** -0.5), None, ALU.mult))
            dve.wait_ge(S("gla_z"), 1)
            V.tensor_scalar(T[0][:], ps[:, 2, :], vcol("gla_b_a"), 0.0, ALU.add, ALU.min).then_inc(S("gla_zmin"), 1)
            dve.wait_ge(S("gla_log"), 1)
            V.tensor_tensor(T[0][:], T[0][:], T[1][:], ALU.subtract).then_inc(S("gla_logsig"), 1)
            dve.wait_ge(S("gla_alpha"), 1)

            def gla_last_product(g, par):
                dve.wait_ge(S(f"gla_values{par}"), 32 * g + (64 - 32 * par))
                if not isinstance(g, int) or g > 0:
                    dve.wait_ge(S("gla_scanned"), GLA_GROUP * g)
                V.tensor_tensor(kvp[:, GLA_GROUP - 1, :], bT[:, 1, :], vb[:, par, GLA_GROUP - 1, :], ALU.mult
                                ).then_inc(S("gla_kv_last"), 1)

            def gla_scan(g, j):
                if j < GLA_GROUP - 1:
                    dve.wait_ge(S("gla_kv"), (GLA_GROUP - 1) * g + (j + 1))
                else:
                    dve.wait_ge(S("gla_kv_last"), g + 1)
                if not isinstance(g, int) or g > 0 or j >= 2:
                    dve.wait_ge(S("gla_read"), GLA_GROUP * g + (j - 1))
                V.tensor_tensor_scan(scanned[:, j % 2, :], alpha[:], kvp[:, j, :], 0.0, ALU.mult, ALU.add
                                     ).then_inc(S("gla_scanned"), 1)

            def gla_read(g, par, j):
                dve.wait_ge(S("gla_scanned"), GLA_GROUP * g + (j + 1))
                if not isinstance(g, int) or g >= 2:
                    dve.wait_ge(S("gla_summed"), GLA_GROUP * g + (j + 1 - 2 * GLA_GROUP))
                V.tensor_tensor(qs[:, par, j, :], scanned[:, j % 2, :], bT[:, 0, :], ALU.mult).then_inc(S("gla_read"), 1)

            def gla_round(i):
                for par in range(2):
                    g = 2 * i + par
                    gla_last_product(g, par)
                    gla_scan(g, 0)
                    gla_scan(g, 1)
                    for j in range(2, GLA_GROUP):
                        gla_read(g, par, j - 2)
                        gla_scan(g, j)
                    gla_read(g, par, GLA_GROUP - 2)
                    gla_read(g, par, GLA_GROUP - 1)
            peeled(dve, GLA_GROUPS // 2, gla_round)
            dve.wait_ge(S("gla_summed"), B_VAL)
            own.done(V.tensor_copy(oTok[:].rearrange("p t f -> p (t f)"), ps[:, 2:4, :].rearrange("p b f -> p (b f)")))
            own.done(V.tensor_tensor(oSq[:], oTok[:], oTok[:], ALU.mult))
            V.tensor_reduce(T[0][:, 0:TB * B_HEADS], oSq[:].rearrange("p t (h v) -> p (t h) v", v=B_VAL), AX_X, ALU.add
                            ).then_inc(S("gla_ms"), 1)
            dve.wait_ge(S("gla_root"), 1)
            own.done(V.reciprocal(T[0][:, 0:TB * B_HEADS], T[0][:, 0:TB * B_HEADS]))
            V.tensor_tensor(oTok[:].rearrange("p t (h v) -> p (t h) v", v=B_VAL),
                            oTok[:].rearrange("p t (h v) -> p (t h) v", v=B_VAL),
                            T[0][:, 0:TB * B_HEADS].unsqueeze(2).to_broadcast([P, TB * B_HEADS, B_VAL]), ALU.mult
                            ).then_inc(S("gla_normed"), 1)
            for e in range(2):
                dve.wait_ge(S("gla_turned"), e + 1)
                dve.wait_ge(S("gla_silu"), 1)
                dve.wait_ge(S("v_turned"), PAIRS)
                V.scalar_tensor_tensor(T[2 + e][:], ps[:, 5 + e, :], vcol("gla_norm_w", e), bT[:, 4 + e, :], ALU.mult, ALU.mult
                                       ).then_inc(S("gla_out"), 1)
            for e in range(2):
                dve.wait_ge(S("gla_high"), e + 1)
                k = 2 * A_W // P + e
                V.tensor_tensor(actL[:, k, :], T[2 + e][:], actH[:, k, :].bitcast(F32), ALU.subtract
                                ).then_inc(S("gla_low"), 1)

            S_BANK = (3, 4, 2, 3)

            def logits(pre, lp, s, par, i, z, scale):
                n, off = (i + 1) * P, i * (i + 1) // 2 * P
                dve.wait_ge(S(pre + "_scored"), 4 * s + (i + 1))
                dve.sem_inc(S("scores_seen"), 1)
                V.tensor_tensor_reduce(lp[:, par, off:off + n], ps[:, S_BANK[i], 0:n], z((TB - 1 - i) * P), -scale, BIG,
                                       ALU.add, ALU.min, stat[:, 0, par, i:i + 1]).then_inc(S(pre + "_logits"), 1)

            def normed(pre, lp, s, par, i):
                n, off = (i + 1) * P, i * (i + 1) // 2 * P
                dve.wait_ge(S(pre + "_exp"), 4 * s + (i + 1))
                own.done(V.reciprocal(stat[:, 2, par, i:i + 1], stat[:, 1, par, i:i + 1]))
                V.tensor_scalar(lp[:, par, off:off + n], lp[:, par, off:off + n], stat[:, 2, par, i:i + 1], None, ALU.mult
                                ).then_inc(S(pre + "_normed"), 1)

            def head(pre, lp, s, par, z, scale, after=None):
                for i in range(TB):
                    logits(pre, lp, s, par, i, z, scale)
                    if i > 0:
                        normed(pre, lp, s, par, i - 1)
                normed(pre, lp, s, par, TB - 1)
                if after is not None:
                    after()

            def pair_low(pre, p, dstL, dstH):
                dve.wait_ge(S(pre + "_high"), p + 1)
                q = lambda t: t[:, ds(p, 1), :].rearrange("p a t -> p (a t)")
                V.tensor_tensor(q(dstL), ps[:, 7, :], q(dstH).bitcast(F32), ALU.subtract).then_inc(S(pre + "_low"), 1)

            SC_A = HEAD_DIM ** -0.5

            def a_head(s, par, p):
                dve.wait_ge(S(f"strip_loaded{par}"), 16 * p + 16)
                head("a", LP, s, par, lambda at: Z[:, par, at:SEQ], SC_A)
            a_head(0, 0, 0)
            a_head(1, 1, 0)

            def pair(p):
                own.enter(p, 2 * TB)
                a_head(2 * p + 2, 0, p + 1)
                a_head(2 * p + 3, 1, p + 1)
                pair_low("a", p, actL, actH)
            repeat(dve, PAIRS - 1, pair)
            own.leave(PAIRS - 1)
            pair_low("a", PAIRS - 1, actL, actH)
            peeled(dve, KT // 2, adds(gOut, "n2"))
            dve.wait_ge(s_ev, gOut.b0 + KT)
            norm_parts("n2", KT, lambda k: xT[:, k, :], lambda k: vcol("norm2_w", k), lambda k: actL[:, k, :],
                       lambda k: actH[:, k, :])
            dve.wait_ge(S("c_ready"), 1)
            sp0, sp1, sp2 = nsp[:, 0, :], nsp[:, 1, :], nsp[:, 2, :]
            dve.wait_ge(S("lru_exp"), 1)
            own.done(V.tensor_scalar(sp0, sp1, 2.0, None, ALU.add))
            own.done(V.reciprocal(sp0, sp0))
            own.done(V.tensor_tensor(sp1, sp1, sp0, ALU.mult))
            own.done(V.tensor_tensor(sp2, sp1, sp1, ALU.mult))
            own.done(V.tensor_scalar(sp0, sp2, 1.0 / LOG_TERMS[0], 1.0 / LOG_TERMS[1], ALU.mult, ALU.add))
            for term in LOG_TERMS[2:]:
                own.done(V.tensor_tensor(sp0, sp0, sp2, ALU.mult))
                own.done(V.tensor_scalar(sp0, sp0, 1.0 / term, None, ALU.add))
            own.done(V.scalar_tensor_tensor(sp1, sp1, 2.0, sp0, ALU.mult, ALU.mult))
            own.done(V.tensor_scalar(sp0, vec[:, VEC["lru_param_2"]:VEC["lru_param_2"] + RT], -1.0, 0.0,
                                     ALU.mult, ALU.max))
            own.done(V.tensor_tensor(sp0, sp0, sp1, ALU.add))
            own.done(V.tensor_scalar(sp0, sp0, -LRU_C, None, ALU.mult))

            def ada_chunk(o, gi, half, p, j, h):
                c = 4 * KT * o + 2 * p + (2 * KT * gi + KT * half + j)
                e = 2 * h + j
                nth = KT * o + (KT // 2 * gi + KT // 4 * half)
                q = (p - h) // 2 if isinstance(p, int) else None
                v = 16 * nth + (16 * q if q is not None else (p - h) * 8) + 16
                dve.wait_ge(S(f"ada_loaded{e}"), v)
                dve.wait_ge(S("ada_used"), c + 1)
                q = adaacc[:, ds(2 * ADA_COLS * p + ADA_COLS * j, ADA_COLS)]
                V.scalar_tensor_tensor(q, wada[:, e, :], cact[:, ds(4 * o + (2 * gi + half), 1)], q, ALU.mult, ALU.add
                                       ).then_inc(S("ada_used"), 1)

            def by_two(body):
                return lambda q: (body(2 * q, 0), body(2 * q + 1, 1))

            def ff_group(o):
                for gi in range(2):
                    one, two = gFF[gi]

                    def first(p, h, one=one, gi=gi):
                        for j in range(2):
                            f = 2 * KT * o + 2 * p + (KT * gi + j)
                            dve.wait_ge(S("hid_relu"), f + 1)
                            if not isinstance(f, int) or f >= 2:
                                dve.wait_ge(S("hid_low"), f - 1)
                            V.tensor_tensor(T[2 + j][:], T[j][:], T[j][:], ALU.mult).then_inc(S("hid_squared"), 1)
                        for j in range(2):
                            f = 2 * KT * o + 2 * p + (KT * gi + j)
                            dve.wait_ge(S("hid_high"), f + 1)
                            u = lambda t: t[:, ds(2 * p + (KT * gi + j), 1), :].rearrange("p a t -> p (a t)")
                            V.tensor_tensor(u(UL), T[2 + j][:], u(UH).bitcast(F32), ALU.subtract).then_inc(S("hid_low"), 1)
                        for j in range(2):
                            ada_chunk(o, gi, 0, p, j, h)
                    (repeat if o or gi else peeled)(dve, KT // 4, by_two(first))

                    last = o == FF_GROUPS // 2 - 1 and gi == 1

                    def second(p, h, two=two, gi=gi, last=last):
                        for j in range(2):
                            dve.wait_ge(s_mm, 2 * FF_SLOTS * o + 2 * p + (two.n0 + j + 1))
                            x = xT[:, ds(2 * p + j, 1), :].rearrange("p a t -> p (a t)")
                            dve.wait_ge(S("x_added"), KT * (2 * o + gi)) if gi or not isinstance(o, int) or o else None
                            V.tensor_tensor(x, ps[:, two.bank(j), :], x, ALU.add).then_inc(S("x_added"), 1)
                            ada_chunk(o, gi, 1, p, j, h)
                            if last:
                                add_square("n3", 2 * p + j, j)
                                add_square("n4", 2 * p + j, j, 2, 4)
                    (peeled if last else repeat)(dve, KT // 4, by_two(second))
            ff_group(0)
            ff_group(1)
            dve.wait_ge(S("x_added"), KT * FF_GROUPS)
            dve.wait_ge(*N("n3", "root", 1))
            own.done(V.reciprocal(rstd[:], rstd[:]))
            own.done(V.tensor_tensor(r2[:], rstd[:], rstd[:], ALU.mult))
            dve.wait_ge(*N("n4", "summed", 1))
            V.tensor_tensor(r2[:], ps[:, 4, :], r2[:], ALU.mult).then_inc(S("n4_mean"), 1)
            dve.wait_ge(S("ada_summed"), 1)
            own.done(V.tensor_tensor(mod[:, 0:2 * KT], ps[:, 3, 0:2 * KT], vec[:, VEC["b_ada_2"]:VEC["b_ada_2"] + 2 * KT],
                                     ALU.add))
            own.done(V.scalar_tensor_tensor(gainA[:, 0, :], mod[:, KT:2 * KT], 1.0,
                                            vec[:, VEC["norm1_g_2"]:VEC["norm1_g_2"] + KT], ALU.add, ALU.mult))
            V.tensor_tensor(gainA[:, 0, :], gainA[:, 0, :], vec[:, VEC["final_norm_w"]:VEC["final_norm_w"] + KT], ALU.mult
                            ).then_inc(S("mod_ready"), 1)
            dve.wait_ge(S("mod_ready"), 1)
            dve.wait_ge(*N("n4", "root", 1))
            own.done(V.reciprocal(r4[:], r4[:]))
            own.done(V.tensor_tensor(r4[:], r4[:], rstd[:], ALU.mult))
            norm_split("n4", KT, lambda k: xT[:, k, :], lambda k: gainA[:, 0, k:k + 1], lambda k: actL[:, k, :],
                       lambda k: actH[:, k, :], shift=lambda k: mod[:, k:k + 1], by=r4)
            norm_plain(lambda k: xT[:, k, :], lambda k: vcol("final_norm_w", k), lambda k: xT[:, k, :])
            dve.wait_ge(S("ada_summed"), 2)
            own.done(V.tensor_tensor(mod[:, 2 * KT:6 * KT], ps[:, 5, 0:4 * KT],
                                     vec[:, VEC["b_ada_2"] + 2 * KT:VEC["b_ada_2"] + 6 * KT], ALU.add))
            V.scalar_tensor_tensor(gainA[:, 1, :], mod[:, 4 * KT:5 * KT], 1.0,
                                   vec[:, VEC["norm2_g_2"]:VEC["norm2_g_2"] + KT], ALU.add, ALU.mult
                                   ).then_inc(S("mod_ready"), 1)
            dve.wait_ge(S("mod_ready"), 2)
            def conv(t, j):
                dve.wait_ge(s_mm, t + (gX.n0 + j + 1))
                y = lambda a: xc[:, ds(t + j, 1), a:SEQ].rearrange("p a t -> p (a t)")
                w = lambda k: vec[:, ds(t + (VEC["conv_w_2"] + RT * k + j), 1)]
                own.done(V.tensor_scalar(y(0), ps[:, gX.bank(j), :], w(CONV_W - 1),
                                         vec[:, ds(t + (VEC["conv_b_2"] + j), 1)], ALU.mult, ALU.add))
                for k in range(1, CONV_W):
                    ins = V.scalar_tensor_tensor(y(k), ps[:, gX.bank(j), 0:SEQ - k], w(CONV_W - 1 - k), y(k),
                                                 ALU.mult, ALU.add)
                    if k < CONV_W - 1:
                        own.done(ins)
                    else:
                        ins.then_inc(s_ev, 1)

            def rnn_loga(t, j):
                dve.wait_ge(S("rnn_sig"), 2 * t + (2 * j + 2))
                V.scalar_tensor_tensor(T[j][:], T[j][:], nsp[:, 0, ds(t + j, 1)], T[4][:], ALU.mult, ALU.add
                                       ).then_inc(S("rnn_loga"), 1)

            def rnn_tiles(t):
                for j in range(2):
                    x = xc[:, ds(t + j, 1), :].rearrange("p a t -> p (a t)")
                    own.done(V.tensor_tensor(T[2 + j][:], T[2 + j][:], x, ALU.mult))
                for j in range(2):
                    dve.wait_ge(S("rnn_tanh"), t + (j + 1))
                    own.done(V.tensor_tensor(T[5][:], rA[:, j, :], rA[:, j, :], ALU.mult))
                    V.scalar_tensor_tensor(rTh[:, j, :], T[5][:], 1.0, rTh[:, j, :], ALU.add, ALU.mult
                                           ).then_inc(S("rnn_m2"), 1)
                    dve.wait_ge(S("rnn_m2"), t + (j + 1))
                for j in range(2):
                    dve.wait_ge(S("rnn_mult"), t + (j + 1))
                    own.done(V.tensor_tensor(rTh[:, j, :], rTh[:, j, :], T[2 + j][:], ALU.mult))
                    V.tensor_tensor_scan(T[j][:], rA[:, j, :], rTh[:, j, :], 0.0, ALU.mult, ALU.add
                                         ).then_inc(S("rnn_state"), 1)
                for j in range(2):
                    dve.wait_ge(S("rnn_high"), t + (j + 1))
                    u = lambda b: b[:, ds(t + j, 1), :].rearrange("p a t -> p (a t)")
                    V.tensor_tensor(u(UL), T[j][:], u(UH).bitcast(F32), ALU.subtract).then_inc(S("rnn_low"), 1)

            def x_round(p):
                own.enter(p, 2 * (CONV_W - 1))
                for j in range(2):
                    conv(2 * p, j)
            repeat(dve, RT // 2, x_round)
            own.leave(RT // 2)

            dve.wait_ge(S("reset_loaded"), 16)
            own.done(V.tensor_copy(T[4][:], posr[:]))
            own.done(V.tensor_scalar(T[4][:], T[4][:], 0.0, NEG, ALU.is_equal, ALU.mult))

            def rnn_round(p):
                own.enter(p, 6)
                for j in range(2):
                    rnn_loga(2 * p, j)
                rnn_tiles(2 * p)
            repeat(dve, RT // 2, rnn_round)
            own.leave(RT // 2)
            dve.wait_ge(S("rnn_low"), RT)
            def pr_round(i):
                for j in range(2):
                    dve.wait_ge(s_mm, 4 * i + (gPR.n0 + 2 * j + 2))
                    g = gR[:, ds(2 * i + j, 1), :].rearrange("p a t -> p (a t)")
                    V.tensor_tensor(g, ps[:, gPR.bank(j), :], g, ALU.mult).then_inc(s_ev, 1)
            dve.wait_ge(S("pos_loaded"), 16)
            c1 = 6.28125
            c2 = float(np.float32(2 * math.pi - c1) - np.float32(2 * math.pi - c1) % np.float32(2.0 ** -20))
            c3 = float(2 * math.pi - c1 - c2)
            rnd = float(1.5 * 2 ** 23)
            own.done(V.tensor_copy(rott[:], posb[:]))
            own.done(V.tensor_scalar(rott[:], rott[:], const[:, C_INVF:C_INVF + 1], None, ALU.mult))
            own.done(V.tensor_scalar(rotk[:], rott[:], float(1 / (2 * math.pi)), const[:, C_TURN:C_TURN + 1], ALU.mult, ALU.add))
            own.done(V.tensor_scalar(rotk[:], rotk[:], rnd, None, ALU.add))
            own.done(V.tensor_scalar(rotk[:], rotk[:], -rnd, None, ALU.add))
            for c in (c1, c2, c3):
                own.done(V.scalar_tensor_tensor(rott[:], rotk[:], -c, rott[:], ALU.mult, ALU.add))
            own.done(V.tensor_scalar(rott[:], rott[:], const[:, C_PHASE:C_PHASE + 1], 3.1415925, ALU.add, ALU.min))
            own.done(V.memset(CS[0:NOPE, :], 1.0))
            V.tensor_scalar(rott[:], rott[:], -3.1415925, None, ALU.max).then_inc(S("rot_angle"), 1)
            dve.wait_ge(S("rot_ready"), 1)
            copies(gLat, 2, (QT + KVT) // 2, lambda i, j: lat[:, ds(2 * i + j, 1), :].rearrange("p a t -> p (a t)"))
            copies(gLat, 1, 1, lambda i, j: lat[:, QT + KVT - 1, :], first=QT + KVT - 1)
            dve.wait_ge(*N("nq", "root", 1))
            own.done(V.reciprocal(rstd[:], rstd[:]))
            for k in range(QT):
                norm_scaled("nq", k, lambda k: lat[:, k, :], lambda k: vcol("q_norm_g_2", k), rstd)
            dve.wait_ge(*N("nkv", "root", 1))
            own.done(V.reciprocal(Vf[:], Vf[:]))
            for k in range(QT):
                low("nq", k, lambda k: actL[:, k, :], lambda k: actH[:, k, :], None)
            dve.wait_ge(*N("nq", "low", QT))
            for k in range(KVT):
                norm_scaled("nkv", k, lambda k: lat[:, QT + k, :], lambda k: vcol("kv_norm_g_2", k), Vf)
            dve.wait_ge(s_mm, gRope.n0 + 1)
            V.tensor_tensor(T[4][NOPE:P, :], ps[NOPE:P, gRope.bank(0), :], CS[NOPE:P, :], ALU.mult).then_inc(s_ev, 1)
            dve.wait_ge(s_ev, gRope.b0 + 1)
            own.done(V.tensor_copy(T[5][NOPE:QKD, :], T[4][QKD:P, :]))
            for par in range(2):
                own.done(V.tensor_tensor(Kp[NOPE:QKD, par, :], T[4][NOPE:QKD, :], T[5][NOPE:QKD, :], ALU.add))
                V.tensor_copy(Kp[QKD:P, par, :], Kp[NOPE:QKD, par, :]).then_inc(S("krot_ready"), 1)
            dve.wait_ge(S("krot_ready"), 2)
            for k in range(KVT):
                low("nkv", k, lambda k: actL[:, QT + k, :], lambda k: actH[:, QT + k, :], None)
            dve.wait_ge(S("gate_evacuated"), 2 * KT)
            repeat(dve, KT // 2, pr_round)

            def value_rows(s):
                dve.wait_ge(s_mm, s + (gHead.n0 + 1))
                if not isinstance(s, int) or s > 0:
                    dve.wait_ge(S("m_v_turned"), s)
                V.tensor_copy(Vf[NOPE:P, :], ps[NOPE:P, 1, :]).then_inc(S("m_v_rows"), 1)

            def query_evac(s, par):
                dve.wait_ge(S("m_q_made"), s + 1)
                V.tensor_tensor(Qp[:, par, :], ps[:, 0, :], CS[:], ALU.mult).then_inc(S("m_q_ready"), 1)

            SC_M = QKD ** -0.5
            z_m = lambda at: strip[:, at:SEQ]
            query_evac(0, 0)
            value_rows(0)

            def ahead(s, par):
                return lambda: (query_evac(s, par), value_rows(s))
            head("m", LP2, 0, 0, z_m, SC_M, ahead(1, 1))

            def head_pair(p):
                own.enter(p, 2 * TB)
                head("m", LP2, 2 * p + 1, 1, z_m, SC_M, ahead(2 * p + 2, 0))
                head("m", LP2, 2 * p + 2, 0, z_m, SC_M, ahead(2 * p + 3, 1))
                pair_low("m", p, UL, UH)
            repeat(dve, N_MLA // 2 - 1, head_pair)
            own.leave(N_MLA // 2 - 1)
            head("m", LP2, N_MLA - 1, 1, z_m, SC_M)
            pair_low("m", N_MLA // 2 - 1, UL, UH)

            def pm_round(i):
                for j in range(2):
                    dve.wait_ge(s_mm, 2 * i + (gPM.n0 + j + 1))
                    m = lambda t: t[:, ds(2 * i + j, 1), :].rearrange("p a t -> p (a t)")
                    if not isinstance(i, int) or i > 0:
                        dve.wait_ge(S("merged_low"), 2 * i + (j - 1))
                    V.tensor_tensor(T[j][:], ps[:, gPM.bank(j), :], m(gM), ALU.mult).then_inc(s_ev, 1)
                    dve.wait_ge(s_ev, 2 * i + (gPM.b0 + j + 1))
                    V.tensor_tensor(T[j][:], T[j][:], m(gR), ALU.add).then_inc(S("merged"), 1)
                for j in range(2):
                    m = lambda t: t[:, ds(2 * i + j, 1), :].rearrange("p a t -> p (a t)")
                    dve.wait_ge(S("merged_high"), 2 * i + (j + 1))
                    V.tensor_tensor(m(actL), T[j][:], m(actH).bitcast(F32), ALU.subtract).then_inc(S("merged_low"), 1)
            peeled(dve, KT // 2, pm_round)

            peeled(dve, KT // 2, adds(gOut2, "n5", 2 * KT))
            dve.wait_ge(s_ev, gOut2.b0 + KT)
            norm_parts("n5", KT, lambda k: xT[:, k, :], lambda k: gainA[:, 1, k:k + 1], lambda k: actL[:, k, :],
                       lambda k: actH[:, k, :], shift=lambda k: mod[:, 3 * KT + k:3 * KT + k + 1])

            def ffn_conv(t, j, h, dst, sem):
                dve.wait_ge(s_mm, 2 * t + (gUp.n0 + h + 1))
                w = lambda k: vec[:, ds(t + (VEC[f"ffn_conv_w{k}"] + FT * h), 1)]
                own.done(V.tensor_scalar(dst[:, j, :], ps[:, gUp.bank(h), :], w(FFN_CONV - 1),
                                         vec[:, ds(t + (VEC["ffn_conv_b_2"] + FT * h), 1)], ALU.mult, ALU.add))
                own.done(V.scalar_tensor_tensor(dst[:, j, 1:SEQ], ps[:, gUp.bank(h), 0:SEQ - 1], w(FFN_CONV - 2),
                                                dst[:, j, 1:SEQ], ALU.mult, ALU.add))
                V.scalar_tensor_tensor(dst[:, j, 2:SEQ], ps[:, gUp.bank(h), 0:SEQ - 2], w(FFN_CONV - 3),
                                       dst[:, j, 2:SEQ], ALU.mult, ALU.add).then_inc(S(sem), 1)

            def up_pair(t, j):
                ffn_conv(t, j, 0, cg, "up_gate")
                ffn_conv(t, j, 1, cv, "up_value")
                dve.wait_ge(S("up_value"), t + 1)
                dve.wait_ge(S("up_silu"), t + 1)
                V.tensor_tensor(act2[:, j, :], act2[:, j, :], cv[:, j, :], ALU.mult).then_inc(S("up_product"), 1)
                dve.wait_ge(S("up_high"), t + 1)
                u = lambda b: b[:, ds(t, 1), :].rearrange("p a t -> p (a t)")
                V.tensor_tensor(u(UL), act2[:, j, :], u(UH).bitcast(F32), ALU.subtract).then_inc(S("up_low"), 1)

            def up_round(p):
                own.enter(p, 8)
                up_pair(2 * p, 0)
                up_pair(2 * p + 1, 1)
            repeat(dve, FT // 2, up_round)
            own.leave(FT // 2)
            peeled(dve, KT // 2, adds(gDown, "n6", 5 * KT, len(DOWN_KS)))
            dve.wait_ge(s_ev, gDown.b0 + KT)
            dve.wait_ge(*N("n6", "root", 1))
            own.done(V.reciprocal(rstd[:], rstd[:]))
            norm_plain(lambda k: xT[:, k, :], lambda k: vcol("final_g_2", k), lambda k: yout[:, k, :])
        @block.tensor
        def _(pe):
            MM = nc.tensor.matmul

            def three(o, wh, wl, ah, al, first, last):
                MM(o, wh, ah, start=first, stop=False)
                MM(o, wh, al, start=False, stop=False)
                return MM(o, wl, ah, start=False, stop=last)

            def block_product(ph, n, j, q, actin, k0, ready, evac, after=None):
                kts, last = ph.ks[q], q == len(ph.ks) - 1
                slot, bank = ph.slot(len(ph.ks) * j + q), ph.bank(j)
                pe.wait_ge(s_lo, n + 1)
                if q == 0:
                    for sem, v in evac:
                        pe.wait_ge(sem, v)
                for k in range(kts):
                    if ready is not None:
                        pe.wait_ge(*ready(k0 + k))
                    mm = three(ps[:, bank, :], WH[slot][:, k, :], WL[slot][:, k, :], actin(0, k0 + k), actin(1, k0 + k),
                               q == 0 and k == 0, last and k == kts - 1)
                    if k == kts - 1:
                        mm.then_inc(s_mm, 1)
                    if after is not None:
                        after(k)

            def free(b):
                return [(s_ev, b - 1)] if not isinstance(b, int) or b >= 2 else []

            def products(ph, per, rounds, actin, ready=None, first=0, evac=free):
                nk = len(ph.ks)

                def body(i):
                    for j in range(per):
                        k0 = 0
                        for q in range(nk):
                            block_product(ph, per * nk * i + (ph.n0 + nk * (first + j) + q), first + j, q, actin, k0,
                                          ready if j == 0 else None, evac(per * i + (ph.b0 + first + j)))
                            k0 += ph.ks[q]
                repeat(pe, rounds, body)

            x_in = lambda part, k: (actH, actL)[part][:, k, :]

            def mean_square(name, tiles, bank=2):
                for k in range(tiles):
                    pe.wait_ge(*N(name, "squared", k + 1))
                    MM(ps[:, bank, :], ones[:], T[k % 2][:], start=(k == 0), stop=(k == tiles - 1)
                       ).then_inc(S("norm_summed"), 1)

            def norm_sum(name, acc=5, bank=2):
                pe.wait_ge(*N(name, "added", KT - 1))
                MM(ps[:, bank, :], ones[:], T[acc][:], start=True, stop=True).then_inc(S("norm_summed"), 1)

            def pair_product(ph, n, actin, ready, evac, order=range(KT), lag=KT):
                for step in range(KT + lag):
                    for j, at in ((0, step), (1, step - lag)):
                        if not 0 <= at < KT:
                            continue
                        if at == 0:
                            pe.wait_ge(s_lo, n + j + 1)
                            for sem, v in evac(j):
                                pe.wait_ge(sem, v)
                        k = order[at]
                        if j == 0:
                            pe.wait_ge(*ready(k))
                        mm = three(ps[:, ph.bank(j), :], WH[ph.slot(j)][:, k, :], WL[ph.slot(j)][:, k, :], actin(0, k),
                                   actin(1, k), at == 0, at == KT - 1)
                        if at == KT - 1:
                            mm.then_inc(s_mm, 1)

            pe.wait_ge(S("const_loaded"), 16)
            for k in range(KT):
                pe.wait_ge(S(f"x_loaded{k // (KT // 2)}"), 16)
                if k >= 2:
                    pe.wait_ge(S("x_turned"), k - 1)
                for t in range(TB):
                    mm = nc.tensor.transpose(ps[:, 6 + k % 2, t * P:(t + 1) * P], xn[:, t, k * P:(k + 1) * P], ident)
                mm.then_inc(S("x_transposed"), 1)
            pe.wait_ge(S("vec_loaded"), 16 * sum(len(g) for g in VEC_GROUPS))
            for g, (at, n) in enumerate(VEC_ROWS):
                nc.tensor.transpose(ps[:, 2 + g, 0:n], vrows[0:n, g, :], ident[0:n, 0:n]).then_inc(S("vec_transposed"), 1)
            pe.wait_ge(S("tables_loaded"), 64)
            pe.wait_ge(S("vecs_turned"), len(VEC_GROUPS))
            for h in range(2):
                mm = MM(ps[0:2 * PAIRS, 3 + h, 0:TAB // 2], relb[:], onehot[:, h * TAB // 2:(h + 1) * TAB // 2],
                        start=True, stop=True)
            mm.then_inc(S("tabs_made"), 1)
            pe.wait_ge(S("ones_set"), 1)
            mean_square("n1", KT)
            n1 = lambda k: N("n1", "low", k + 1)
            pair_product(gB, gB.n0, x_in, n1, lambda j: [], lag=LAG)
            products(gB, 2, NB_B // 2 - 1, x_in, first=2)
            products(gB, 1, 1, x_in, first=NB_B - 1)
            pe.wait_ge(s_ev, gB.b0 + NB_B)
            MM(ps[:, 2, :], wa2[:], bT[0:B_RANK, NB_B - 1, :], start=True, stop=True).then_inc(S("gla_z"), 1)

            def gla_sums(g, par):
                def after(k):
                    if k % 2 == 0:
                        return
                    j = k // 2
                    pe.wait_ge(S("gla_read"), GLA_GROUP * g + (j + 1))
                    for t in range(TB):
                        o = ps[:, 2 + t // 2, (t % 2) * B_W:(t % 2 + 1) * B_W].rearrange("p (h v) -> p h v", v=B_VAL)
                        mm = MM(o[:, :, ds(GLA_GROUP * g + j, 1)].rearrange("p h a -> p (h a)"),
                                qs[:, par, j, t * P:(t + 1) * P], headsum, start=True, stop=True)
                    mm.then_inc(S("gla_summed"), 1)
                return after

            products(gQK, 2, 1, x_in)

            def qk_round(i):
                for j in range(2):
                    block_product(gQK, 2 * i + (gQK.n0 + 2 + j), j, 0, x_in, 0, None, free(2 * i + (gQK.b0 + 2 + j)),
                                  gla_sums(2 * i + j, j))
            repeat(pe, PAIRS - 1, qk_round)

            def turn_values(v):
                pe.wait_ge(s_ev, gV.b0 + v + 1)
                if v >= 2:
                    pe.wait_ge(S("values_turned"), v - 1)
                for t in range(TB):
                    q = slice(t * P, (t + 1) * P)
                    mm = nc.tensor.transpose(ps[:, 5 + v % 2, q], T[2 + v % 2][:, q], ident)
                mm.then_inc(S("v_turned"), 1)

            for v in range(PAIRS):
                block_product(gV, gV.n0 + v, v, 0, x_in, 0, None, free(gV.b0 + v), gla_sums(2 * PAIRS - 2 + v, v % 2))
                if v:
                    turn_values(v - 1)
            turn_values(PAIRS - 1)
            pe.wait_ge(S("gla_normed"), 1)
            for e in range(2):
                for t in range(TB):
                    mm = nc.tensor.transpose(ps[:, 5 + e, t * P:(t + 1) * P], oTok[:, t, e * P:(e + 1) * P], ident)
                mm.then_inc(S("gla_turned"), 1)

            S_BANK = (3, 4, 2, 3)

            def scores(pre, s, i, q, k):
                n = (i + 1) * P
                if i == TB - 1:
                    pe.wait_ge(S(pre + "_logits"), 4 * s + 1)
                elif not isinstance(s, int) or s > 0:
                    pe.wait_ge(S(pre + "_logits"), 4 * s)
                MM(ps[:, S_BANK[i], 0:n], q(i), k(n), start=True, stop=True).then_inc(S(pre + "_scored"), 1)

            def turn(pre, lp, s, par, i, weighed):
                off = i * (i + 1) // 2 * P
                pe.wait_ge(S(pre + "_normed"), 4 * s + (i + 1))
                if i >= 2 or not weighed and not (isinstance(s, int) and s == 0):
                    pe.wait_ge(S(pre + "_pt"), 4 * s + (i - 1))
                for k in range(i + 1):
                    mm = nc.tensor.transpose(ps[:, 5 + i % 2, k * P:(k + 1) * P],
                                             lp[:, par, off + k * P:off + (k + 1) * P], ident)
                mm.then_inc(S(pre + "_turned"), 1)

            def weigh(pre, pt, s, par, p, v):
                pe.wait_ge(S(pre + "_pt"), 4 * s + 4)
                if par == 0 and not (isinstance(p, int) and p == 0):
                    pe.wait_ge(S(pre + "_low"), p)
                for k in range(TB):
                    mm = MM(ps[HEAD_DIM * par:HEAD_DIM * (par + 1), 7, k * P:SEQ], v(k), pt[:, k, k * P:SEQ],
                            start=(k == 0), stop=(k == TB - 1))
                mm.then_inc(S(pre + "_weighted"), 1)

            def a_weigh(s, par, p):
                pe.wait_ge(S("a_v_staged"), s + 1)
                weigh("a", PT[:, par], s, par, p, lambda k: Vs[:, k, HEAD_DIM * par:HEAD_DIM * (par + 1)])

            def a_step(s, par, p=None):
                q = slice(HEAD_DIM * par, HEAD_DIM * (par + 1))
                pe.wait_ge(S("a_qk_staged"), 2 * s + 2)
                for i in range(TB):
                    scores("a", s, i, lambda i: Qs[q, i * P:(i + 1) * P], lambda n: Ks[q, 0:n])
                    if not (isinstance(s, int) and s == 0):
                        turn("a", LP, s - 1, 1 - par, i, False)
                    if i == 1 and p is not None:
                        a_weigh(s - 2, par, p)

            a_step(0, 0)
            a_step(1, 1)

            def a_pair(p):
                a_step(2 * p + 2, 0, p)
                a_step(2 * p + 3, 1, p)
            repeat(pe, PAIRS - 1, a_pair)
            for i in range(TB):
                turn("a", LP, 2 * PAIRS - 1, 1, i, False)
                if i == 1:
                    a_weigh(2 * PAIRS - 2, 0, PAIRS - 1)
            a_weigh(2 * PAIRS - 1, 1, PAIRS - 1)
            pair_product(gOut, gOut.n0, x_in, lambda k: (S("a_low"), k + 1) if k < PAIRS else (S("gla_low"), k + 1 - PAIRS),
                         lambda j: free(gOut.b0 + j), [*range(PAIRS, KT), *range(PAIRS)])
            products(gOut, 2, KT // 2 - 1, x_in, first=2)
            norm_sum("n2")
            n2 = lambda k: N("n2", "low", k + 1)

            def ff_group(o):
                for gi in range(2):
                    one, two = gFF[gi]
                    hid = lambda part, k, gi=gi: (UH, UL)[part][:, KT * gi + k, :]

                    blocks = KT * (2 * o + gi)
                    n = 2 * FF_SLOTS * o

                    def first(p, one=one, blocks=blocks, n=n):
                        for j in range(2):
                            block_product(one, 2 * p + (n + one.n0 + j), j, 0, x_in, 0, None,
                                          [(S("hid_relu"), 2 * p + (blocks + j - 1))])
                    pair_product(one, n + one.n0, x_in, n2, lambda j: [(S("x_added"), blocks - 1 + j) if blocks
                                                                       else (s_ev, gOut.b0 + KT - 1 + j)],
                                 lag=KT if blocks else LAG)
                    repeat(pe, KT // 2 - 1, lambda p: first(p + 1))

                    def second(p, two=two, hid=hid, blocks=blocks, n=n):
                        for j in range(2):
                            block_product(two, 2 * p + (n + two.n0 + j), j, 0, hid, 0, None,
                                          [(S("x_added"), 2 * p + (blocks + j - 1))])
                    pair_product(two, n + two.n0, hid, lambda k: (S("hid_low"), blocks + k + 1),
                                 lambda j: [(S("hid_relu"), blocks + KT - 1 + j)])
                    repeat(pe, KT // 2 - 1, lambda p: second(p + 1))
            ff_group(0)
            ff_group(1)
            norm_sum("n3")
            norm_sum("n4", 4, 4)
            pe.wait_ge(S("ada_used"), 1 + 2 * KT * FF_GROUPS)
            for bank, m0, m1 in ((3, 0, 2 * KT), (5, 2 * KT, 6 * KT)):
                for m in range(m0, m1):
                    mm = MM(ps[:, bank, m - m0:m - m0 + 1], adaacc[:, m * P:(m + 1) * P], ones[:, 0:1], start=True, stop=True)
                mm.then_inc(S("ada_summed"), 1)
            n4 = lambda k: N("n4", "low", k + 1)
            pair_product(gX, gX.n0, x_in, n4, lambda j: [(S("x_added"), KT * FF_GROUPS - 1 + j)], lag=LAG)
            products(gX, 2, RT // 2 - 1, x_in, first=2)

            def rnn_gate(t, j):
                pe.wait_ge(S(f"rnn_weights{j}"), t * 32 + 64)
                pe.wait_ge(s_ev, t + (gX.b0 + j + 1))
                if not isinstance(t, int) or t > 0:
                    pe.wait_ge(S("rnn_sig"), 2 * t + (2 * j - 2))
                x = xc[:, ds(t + j, 1), :].rearrange("p a t -> p (a t)")
                MM(ps[:, 2 + 2 * j, :], BDa[:, j, :], x, start=True, stop=True)
                MM(ps[:, 3 + 2 * j, :], BDx[:, j, :], x, start=True, stop=True).then_inc(S("rnn_gated"), 1)

            def gate_round(i, rnn):
                for j in range(2):
                    if isinstance(i, int) and i == 0:
                        prev = [(s_ev, gX.b0 + RT - 1 + j)]
                    else:
                        prev = [(S("gate_evacuated"), 2 * i + (j - 1))]
                    block_product(gGate, 2 * i + (gGate.n0 + j), j, 0, x_in, 0, None, prev)
                    if rnn:
                        rnn_gate(2 * i, j)
            pairs = RT // 2
            peeled(pe, pairs, lambda i: gate_round(i, True))
            repeat(pe, KT - pairs, lambda i: gate_round(i + pairs, False))
            y_in = lambda part, k: (UH, UL)[part][:, k, :]
            pe.wait_ge(S("gate_evacuated"), 2 * KT)
            seen = lambda b: [(s_ev, b - 1)]
            products(gLat, 2, (QT + KVT) // 2, x_in, evac=seen)
            products(gLat, 1, 1, x_in, first=QT + KVT - 1, evac=seen)
            mean_square("nq", QT)
            products(gRope, 1, 1, x_in, evac=seen)
            mean_square("nkv", KVT, 3)
            pe.wait_ge(S("rnn_low"), RT)
            products(gPR, 2, KT // 2, y_in, evac=seen)
            pe.wait_ge(*N("nkv", "low", KVT))
            pe.wait_ge(s_ev, gPR.b0 + KT)

            def head_products(s, par):
                pe.wait_ge(s_lo, s + (gHead.n0 + 1))
                slot = gHead.slot(par)
                if not isinstance(s, int) or s > 0:
                    pe.wait_ge(S("m_q_ready"), s)
                for k in range(QT):
                    mm = three(ps[:, 0, :], WH[slot][:, k, :], WL[slot][:, k, :], actH[:, k, :], actL[:, k, :],
                               k == 0, k == QT - 1)
                mm.then_inc(S("m_q_made"), 1)
                if not isinstance(s, int) or s > 0:
                    pe.wait_ge(S("m_v_ready"), s)
                for k in range(KVT):
                    mm = three(ps[:, 1, :], WH[slot][:, QT + k, :], WL[slot][:, QT + k, :], actH[:, QT + k, :], actL[:, QT + k, :],
                               k == 0, k == KVT - 1)
                mm.then_inc(s_mm, 1)

            def head_values(s):
                pe.wait_ge(S("m_k_ready"), s + 1)
                pe.wait_ge(S("m_v_rows"), s + 1)
                for t in range(TB):
                    mm = MM(ps[:, 1, t * VH:(t + 1) * VH], Vf[NOPE:P, t * P:(t + 1) * P], ident[NOPE:P, NOPE:P],
                            start=True, stop=True)
                mm.then_inc(S("m_v_turned"), 1)

            def m_weigh(s, par, p):
                pe.wait_ge(S("m_v_ready"), s + 1)
                weigh("m", PT2, s, par, p, lambda k: Vp[:, par, k, :])

            def m_head(s, par, p=None, more=True):
                pe.wait_ge(S("m_q_ready"), s + 1)
                pe.wait_ge(S("m_k_ready"), s + 1)
                for i in range(TB):
                    scores("m", s, i, lambda i: Qp[:, par, i * P:(i + 1) * P], lambda n: Kp[:, par, 0:n])
                    if p is not None:
                        turn("m", LP2, s - 1, 1 - par, i, True)
                if more:
                    head_products(s + 1, 1 - par)
                if p is not None:
                    m_weigh(s - 1, 1 - par, p)
                if more:
                    head_values(s + 1)

            pe.wait_ge(S("krot_ready"), 2)
            head_products(0, 0)
            head_values(0)
            m_head(0, 0)

            def m_pair(p):
                m_head(2 * p + 1, 1, p)
                m_head(2 * p + 2, 0, p)
            repeat(pe, N_MLA // 2 - 1, m_pair)
            m_head(N_MLA - 1, 1, N_MLA // 2 - 1, more=False)
            for i in range(TB):
                turn("m", LP2, N_MLA - 1, 1, i, True)
            m_weigh(N_MLA - 1, 1, N_MLA // 2 - 1)
            pair_product(gPM, gPM.n0, y_in, lambda k: (S("m_low"), k + 1),
                         lambda j: [(S("m_q_ready"), N_MLA), (S("m_v_ready"), N_MLA)])
            products(gPM, 2, KT // 2 - 1, y_in, first=2, evac=seen)
            pair_product(gOut2, gOut2.n0, x_in, lambda k: (S("merged_low"), k + 1), lambda j: seen(gOut2.b0 + j))
            products(gOut2, 2, KT // 2 - 1, x_in, first=2, evac=seen)
            norm_sum("n5")

            def up_round(p):
                for h in range(2):
                    block_product(gUp, 2 * p + (gUp.n0 + h), h, 0, x_in, 0, None, [(S(("up_gate", "up_value")[h]), p)])
            pair_product(gUp, gUp.n0, x_in, lambda k: N("n5", "low", k + 1), lambda j: [(s_ev, gOut2.b0 + KT - 1 + j)],
                         lag=LAG)
            repeat(pe, FT - 1, lambda p: up_round(p + 1))
            products(gDown, 2, KT // 2, y_in, lambda k: (S("up_low"), k + 1),
                     evac=lambda b: [(s_ev, b - 1), (S("up_value"), FT)])
            norm_sum("n6")
            for k in range(KT):
                pe.wait_ge(*N("n6", "done", k + 1))
                if k >= 2:
                    pe.wait_ge(S("rows_ready"), k - 1)
                for t in range(TB):
                    mm = nc.tensor.transpose(ps[:, 4 + k % 2, t * P:(t + 1) * P], yout[:, k, t * P:(t + 1) * P], ident)
                mm.then_inc(S("y_turned"), 1)


INPUTS = ["x", "norm1_w", "w_in", "gla_w_a2", "gla_b_a", "gla_norm_w", "w_out", "norm2_w", "w_ff1", "w_ff2", "rel_bias",
          "final_norm_w", "c_2", "positions_2", "w_ada_2", "b_ada_2", "norm1_g_2", "w_in_2", "conv_w_2", "conv_b_2",
          "w_gate_a_2", "b_gate_a_2", "w_gate_x_2", "b_gate_x_2", "lru_param_2", "q_norm_g_2", "w_uq_2", "kv_norm_g_2",
          "w_ukv_2", "w_proj_rnn_2", "w_proj_mla_2", "w_out_2", "norm2_g_2", "w_up_2", "ffn_conv_w_2", "ffn_conv_b_2",
          "w_down_2", "final_g_2"]
WITHOUT_LAYERS = {"x", "rel_bias", "final_norm_w", "positions_2", "final_g_2"}


def kernel(**inputs):
    import concourse.bacc as bacc
    from concourse.bass_utils import run_bass_kernel_spmd

    nc = bacc.Bacc("TRN2", target_bir_lowering=False, num_devices=1)
    arrays, io = {}, {}

    def give(name, a):
        a = np.ascontiguousarray(a)
        arrays[f"in_{name}"] = a
        ap = nc.dram_tensor(f"in_{name}", a.shape, mybir.dt.from_np(a.dtype), kind="ExternalInput").ap()
        io[name] = ap if name in WITHOUT_LAYERS or name.startswith("const") else ap[0]

    for name in INPUTS:
        give(name, inputs[name])
    for name, a in shape_constants().items():
        give(name, a)
    out = nc.dram_tensor("out", (1, SEQ, D_MODEL), F32, kind="ExternalOutput").ap()
    hybrid_stack(nc, io, out)
    r = run_bass_kernel_spmd(nc, [arrays], core_ids=[0])
    return r.results[0]["out"]
```

```python
import math
from contextlib import ExitStack

import numpy as np

import concourse.bass as bass
from concourse import mybir

F32 = mybir.dt.float32
F32R = mybir.dt.float32r
I32 = mybir.dt.int32
ACT = mybir.ActivationFunctionType
ALU = mybir.AluOpType
AX_X = mybir.AxisListType.X
ds = bass.ds

P = 128
SEQ = 512
D_MODEL = 1024
KT = D_MODEL // P
TB = SEQ // P
EPS = 1e-6
NEG = -1e30
BIG = 3e38

HEAD_DIM = 64
A_HEADS = C_HEADS = 6
A_BRANCHES = ((128, 1), (512, 4), (2048, 16))
B_HEADS, B_KEY, B_VAL, B_RANK, B_TAU = 4, 32, 64, 16, 16.0
REL_BUCKETS, REL_MAX_DIST = 32, 2048
A_W, C_W, B_QK, B_W = A_HEADS * HEAD_DIM, C_HEADS * HEAD_DIM, B_HEADS * B_KEY, B_HEADS * B_VAL
COL_AQ, COL_AK, COL_AV = 0, A_W, 2 * A_W
COL_B = 3 * A_W
COL_CQ = COL_B + 2 * B_QK + 2 * B_W + B_RANK
COL_CK, COL_CV = COL_CQ + C_W, COL_CQ + 2 * C_W
NB_B = 7
PAIRS = (A_HEADS + C_HEADS) // 2
TAB = SEQ + P
GLA_GROUP = 4
GLA_GROUPS = B_VAL // GLA_GROUP
FF_GROUPS = 4 * D_MODEL // D_MODEL
ADA_COLS = 6 * D_MODEL // KT

ADA_DEEP = 4

D_RNN, RNN_BLOCK, CONV_W, LRU_C = 1280, 64, 4, 8.0
RT = D_RNN // P
LOG_TERMS = tuple(range(17, 0, -2))
N_MLA, NOPE, ROPE, VH, Q_LORA, KV_LORA = 16, 64, 32, 64, 384, 256
QKD = NOPE + ROPE
QT, KVT = Q_LORA // P, KV_LORA // P
ROPE_THETA = 10000.0
D_FF2, FFN_CONV = 2816, 3
FT = D_FF2 // P
COL_LAT, COL_ROPE, COL_GATE = D_RNN, D_RNN + Q_LORA + KV_LORA, D_RNN + Q_LORA + KV_LORA + ROPE
LAG = 4
DOWN_KS = (8, 7, 7)
RNN_KS = (5, 5)

VEC_GROUPS = [
    [("norm1_w", 8), ("norm2_w", 8), ("final_norm_w", 8), ("gla_norm_w", 2), ("gla_b_a", 1), ("norm1_g_2", 8),
     ("q_norm_g_2", 3), ("kv_norm_g_2", 2), ("norm2_g_2", 8), ("final_g_2", 8), ("c_2", 8),
     ("conv_b_2", 10), ("b_gate_a_2", 10), ("b_gate_x_2", 10), ("lru_param_2", 10)],
    [("conv_w_2", 40), ("b_ada_2", 48)],
    [("ffn_conv_w0", 44), ("ffn_conv_w1", 44)],
    [("ffn_conv_w2", 44), ("ffn_conv_b_2", 44)],
]
VEC = {}
VEC_ROWS = []
_at = 0
for _g in VEC_GROUPS:
    VEC_ROWS.append((_at, sum(n for _, n in _g)))
    for _name, _n in _g:
        VEC[_name] = _at
        _at += _n
N_VEC = _at

C_IDENT, C_STRIP = 0, P
SUM_ROWS = P // GLA_GROUP
SUM_GROUPS = SUM_ROWS // B_HEADS
C_HEADSUM = C_STRIP + SEQ
C_INVF = C_HEADSUM + 2 * SUM_ROWS - B_HEADS
C_PHASE, C_TURN, C_EPS = C_INVF + 1, C_INVF + 2, C_INVF + 3
N_CONST = C_INVF + 4


def shape_constants():
    f32 = np.float32
    j = np.arange(TAB)
    dist = SEQ - 1 - j
    n = np.maximum(dist, 0)
    exact = REL_BUCKETS // 2
    logv = np.log(np.maximum(n, 1).astype(f32) / f32(exact)) / f32(math.log(REL_MAX_DIST / exact))
    large = np.minimum(exact + (logv * f32(REL_BUCKETS - exact)).astype(np.int32), REL_BUCKETS - 1)
    bucket = np.where(n < exact, n, large)
    onehot = (bucket[None, :] == np.arange(REL_BUCKETS)[:, None]).astype(f32)
    visits = np.zeros(TAB)
    for window, dilation in A_BRANCHES:
        visits += (dist >= 0) & (dist <= window) & (dist % dilation == 0)
    scale = math.sqrt(HEAD_DIM)
    mask_a = np.where(visits > 0, scale * np.log(np.maximum(visits, 1)), NEG)
    mask_c = np.where(dist >= 0, 0.0, NEG)
    mask = np.concatenate([np.tile(mask_a, (A_HEADS, 1)), np.tile(mask_c, (C_HEADS, 1))]).astype(f32)
    c = np.zeros((P, N_CONST), f32)
    p = np.arange(P)
    c[:, C_IDENT:C_IDENT + P] = np.eye(P)
    d = (SEQ - P) + p[:, None] - np.arange(SEQ)[None, :]
    c[:, C_STRIP:C_STRIP + SEQ] = np.where(d >= 0, 0.0, NEG)
    c[p, C_HEADSUM + SUM_ROWS - B_HEADS + p // B_KEY] = 1.0
    half = ROPE // 2
    rate = ROPE_THETA ** (-np.arange(half) / half)
    c[NOPE:, C_INVF] = np.concatenate([rate, rate, -rate, rate])
    c[:NOPE + ROPE, C_PHASE] = math.pi / 2
    c[:NOPE + ROPE, C_TURN] = 0.25
    c[:, C_EPS] = EPS
    return {"const_tile": c, "const_onehot": onehot, "const_mask": mask}


def repeat(eng, n, body):
    if n == 1:
        body(0)
    elif n > 1:
        with eng.Fori(0, n) as i:
            body(i)


def peeled(eng, n, body):
    body(0)
    repeat(eng, n - 1, lambda i: body(i + 1))


class Steps:

    def __init__(self, eng, sem):
        self.eng, self.sem, self.before, self.k, self.at, self.inside = eng, sem, 0, 0, 0, False

    def enter(self, i, per):
        if not self.inside:
            self.before += self.k
        self.k, self.at, self.per, self.inside = 0, per * i, per, True

    def leave(self, rounds):
        assert self.k == self.per, (self.k, self.per)
        self.before, self.k, self.at, self.inside = self.before + self.per * rounds, 0, 0, False

    def done(self, ins):
        self.k += 1
        ins.then_inc(self.sem, 1)
        self.eng.wait_ge(self.sem, self.at + (self.before + self.k))


class Phase:

    slots = 0
    blocks = 0

    def __init__(self, nb, ks=(KT,), counted=True):
        assert counted or nb % 2 == 0
        self.n0, self.b0, self.nb, self.ks = Phase.slots, Phase.blocks, nb, ks
        Phase.slots += nb * len(ks)
        Phase.blocks += nb * counted

    def slot(self, n):
        return (self.n0 + n) % 2

    def bank(self, b):
        return (self.b0 + b) % 2


def hybrid_stack(nc, io, out):
    Phase.slots = Phase.blocks = 0
    ctx = ExitStack()
    with ctx:
        sems = {}

        def S(name):
            if name not in sems:
                sems[name] = ctx.enter_context(nc.semaphore(name))
            return sems[name]

        top = [-(-nc.sbuf_base // 64) * 64]

        def place(name, shape, offset, dt=F32):
            return nc.alloc_sbuf_tensor_at(name, shape, dt, offset=offset)

        def size(shape):
            return 4 * int(np.prod(shape[1:]))

        def keep(name, shape, dt=F32):
            t = place(name, shape, top[0], dt)
            top[0] += -(-size(shape) // 64) * 64
            return t

        xT = keep("xT", [P, KT, SEQ])
        actH = keep("actH", [P, KT, SEQ], F32R)
        actL = keep("actL", [P, KT, SEQ], F32R)
        Wraw = [keep(f"Wraw{i}", [P, KT, P]) for i in range(2)]
        WH = [keep(f"WH{i}", [P, KT, P], F32R) for i in range(2)]
        WL = [keep(f"WL{i}", [P, KT, P], F32R) for i in range(2)]
        const = keep("const", [P, N_CONST])
        ones = keep("ones", [P, P])
        half = keep("half", [P, TB])
        rtok = keep("rtok", [P, 4, TB])
        vec = keep("vec", [P, N_VEC])
        cact = keep("cact", [P, KT])
        mod = keep("mod", [P, 6 * KT])
        gainA = keep("gainA", [P, 2, KT])
        nsp = keep("nsp", [P, 3, RT])
        stat = keep("stat", [P, 4, 2, TB])
        rstd = keep("rstd", [P, SEQ])
        T = [keep(f"T{i}", [P, SEQ]) for i in range(6)]
        R = top[0]
        END = nc.sbuf_usable_end

        ident = const[:, C_IDENT:C_IDENT + P]
        strip = const[:, C_STRIP:C_STRIP + SEQ]

        def headsum(u):
            at = C_HEADSUM + SUM_ROWS - B_HEADS * (u + 1)
            return const[:, at:at + SUM_ROWS]

        epsc = const[:, C_EPS:C_EPS + 1]

        def region(specs, start=R):
            made, at = [], start
            for name, shape, dt in specs:
                made.append(place(name, shape, at, dt))
                at += -(-size(shape) // 64) * 64
            assert at <= END, (at, END)
            return made

        bT, qT, kT, Vt, alpha, oTok, oSq, Z, Qs, Ks, Vs, vb, kvp, scanned, qs = region([
            ("bT", [P, NB_B, SEQ], F32), ("qT", [P, PAIRS, SEQ], F32), ("kT", [P, PAIRS, SEQ], F32),
            ("Vt", [P, PAIRS, TB, P], F32), ("alpha", [P, SEQ], F32), ("oTok", [P, TB, B_W], F32),
            ("oSq", [P, TB, B_W], F32), ("Z", [P, 2, SEQ], F32),
            ("Qs", [P, SEQ], F32), ("Ks", [P, SEQ], F32), ("Vs", [P, TB, P], F32),
            ("vb", [P, 2, GLA_GROUP, SEQ], F32), ("kvp", [P, GLA_GROUP, SEQ], F32), ("scanned", [P, 2, SEQ], F32),
            ("qs", [P, 2, GLA_GROUP, SEQ], F32)])
        vb0 = R + sum(size(t.shape) for t in (bT, qT, kT, Vt, alpha, oTok, oSq, Z, Qs, Ks, Vs))
        (LP,) = region([("LP", [P, 2, TB * (TB + 1) // 2 * P], F32)], vb0)
        (PT,) = region([("PT", [P, 2, TB, SEQ], F32)], vb0 + size(vb.shape) + size(kvp.shape) + size(scanned.shape))
        xn, vrows, onehot, maskt, relb, tabs, wa2 = region([
            ("xn", [P, TB, D_MODEL], F32), ("vrows", [P, len(VEC_GROUPS), P], F32), ("onehot", [REL_BUCKETS, TAB], F32),
            ("maskt", [2 * PAIRS, TAB], F32), ("relb", [REL_BUCKETS, 2 * PAIRS], F32), ("tabs", [2 * PAIRS, TAB], F32),
            ("wa2", [B_RANK, B_QK], F32)], R + size(bT.shape))
        UH, UL, adaacc = region([
            ("UH", [P, FT, SEQ], F32R), ("UL", [P, FT, SEQ], F32R), ("adaacc", [P, 6 * D_MODEL], F32)])
        (wada,) = region([("wada", [P, ADA_DEEP, ADA_COLS], F32)], R + size([P, 2 * KT, SEQ]))
        tailH, tailL, rest = R + size([P, RT, SEQ]), R + size(UH.shape) + size([P, RT, SEQ]), R + 2 * size(UH.shape)
        gR, PT2 = region([("gR", [P, KT, SEQ], F32), ("PT2", [P, TB, SEQ], F32)], tailH)
        posr, BDa, BDx = region([("posr", [P, SEQ], I32), ("BDa", [P, 2, P], F32), ("BDx", [P, 2, P], F32)],
                                tailH + size(gR.shape))
        gM, Qp, Kp = region([("gM", [P, KT, SEQ], F32), ("Qp", [P, 2, SEQ], F32), ("Kp", [P, 2, SEQ], F32)], tailL)
        xc, rA, rTh = region([("xc", [P, RT, SEQ], F32), ("rA", [P, 2, SEQ], F32), ("rTh", [P, 2, SEQ], F32)], rest)
        LP2, lat, Vp, CS, Vf = region([
            ("LP2", [P, 2, TB * (TB + 1) // 2 * P], F32), ("lat", [P, QT + KVT, SEQ], F32),
            ("Vp", [P, 2, TB, VH], F32), ("CS", [P, SEQ], F32), ("Vf", [P, SEQ], F32)], rest)
        posb, rotk, rott = region([("posb", [P, SEQ], I32), ("rotk", [P, SEQ], F32), ("rott", [P, SEQ], F32)], rest)
        cg, cv, act2 = region([("cg", [P, 2, SEQ], F32), ("cv", [P, 2, SEQ], F32), ("act2", [P, 2, SEQ], F32)], rest)
        yout, yrow = region([("yout", [P, 2, SEQ], F32), ("yrow", [P, TB, D_MODEL], F32)], rest)

        ps = ctx.enter_context(nc.psum_tensor("ps", [P, 8, SEQ], F32))
        tab_dram = nc.dram_tensor("tab_dram", [2 * PAIRS, TAB], F32, kind="Internal").ap()
        strip_dram = nc.dram_tensor("strip_dram", [2 * PAIRS, P, SEQ], F32, kind="Internal").ap()
        bv_dram = nc.dram_tensor("bv_dram", [B_W, SEQ], F32, kind="Internal").ap()

        gB = Phase(NB_B)
        gQK = Phase(4 * PAIRS // 2)
        gV = Phase(PAIRS)
        gOut = Phase(KT)
        gFF = [(Phase(KT, counted=False), Phase(KT, counted=False)) for _ in range(FF_GROUPS)]
        gX = Phase(RT)
        gGate = Phase(2 * KT, counted=False)
        gLat = Phase(QT + KVT)
        gRope = Phase(1)
        gPR = Phase(KT, RNN_KS)
        gHead = Phase(N_MLA, counted=False)
        gPM = Phase(KT)
        gOut2 = Phase(KT)
        gUp = Phase(2 * FT, counted=False)
        gDown = Phase(KT, DOWN_KS)

        s_raw = [S("raw0_loaded"), S("raw1_loaded")]
        s_hi, s_lo = S("weights_high"), S("weights_low")
        s_mm = S("block_multiplied")
        s_ev = S("block_evacuated")
        def wcols(name, rows0, kts):
            return io[name][rows0:rows0 + kts * P, :].rearrange("(k p) c -> p k c", p=P)

        loads = {}
        slot_base = {}
        total = [0, 0]
        for ph, dmas in ([(gB, 1), (gQK, 1), (gV, 1), (gOut, 3)] + [(g, 1) for pair in gFF for g in pair]
                         + [(gX, 1), (gGate, 1), (gLat, 1), (gRope, 3), (gPR, 1), (gHead, 4), (gPM, 1), (gOut2, 1),
                            (gUp, 1), (gDown, 1)]):
            loads[ph] = dmas
            slot_base[ph] = list(total)
            for n in range(ph.nb * len(ph.ks)):
                total[ph.slot(n)] += 16 * dmas

        def landed(ph, j, i=0, per=2):
            slot = ph.slot(j)
            k = len([x for x in range(j + 1) if ph.slot(x) == slot])
            return s_raw[slot], i * (16 * loads[ph] * (per // 2)) + (slot_base[ph][slot] + 16 * loads[ph] * k)

        norms = [("n1", KT, 1, 1), ("n2", KT, 1, 1), ("n3", KT, 0, 1), ("n4", KT, 1, 1), ("nq", QT, 1, 0),
                 ("nkv", KVT, 1, 0), ("n5", KT, 1, 1), ("n6", KT, 0, 1)]

        def N(name, kind, v):
            apart = kind in ("squared", "added")
            if name == "n4" and apart:
                return S("n4_" + kind), v
            for other, tiles, split, running in norms:
                if other == name:
                    return S("norm_" + kind), v
                if other != "n4" or not apart:
                    v += {"root": 1 - running, "mean": running, "power": running, "spread": running, "squared": tiles, "added": (tiles - 1) * running, "summed": 1 if running else tiles,
                          "done": tiles * (1 - split)}.get(kind, tiles * split)

        FF_SLOTS = 2 * KT

        block = ctx.enter_context(nc.Block())

        @block.sync
        def _(sp):
            def load(n, slot, pieces):
                if not isinstance(n, int) or n >= 2:
                    sp.wait_ge(s_lo, n - 1)
                for dst, src in pieces:
                    sp.dma_start(dst, src).then_inc(s_raw[slot], 16)

            def stream(ph, per, rounds, piece, first=0):
                def body(i):
                    for j in range(per):
                        slot = ph.slot(first + j)
                        load(per * i + (ph.n0 + first + j), slot, piece(i, j, slot))
                repeat(sp, rounds, body)

            def cols(view, kts, at):
                return lambda i, j, slot: [(Wraw[slot][:, 0:kts, :], view[:, :, ds(at(i, j), P)])]

            sp.dma_start(const[:], io["const_tile"]).then_inc(S("const_loaded"), 16)
            x_rows = io["x"][0].rearrange("(t p) d -> p t d", p=P)
            for h in range(2):
                q = slice(h * D_MODEL // 2, (h + 1) * D_MODEL // 2)
                sp.dma_start(xn[:, :, q], x_rows[:, :, q]).then_inc(S(f"x_loaded{h}"), 16)
            w_in = wcols("w_in", 0, KT)
            b_cols = cols(w_in, KT, lambda i, j: 2 * P * i + (COL_B + P * j))
            stream(gB, 2, 1, b_cols)
            for g, names in enumerate(VEC_GROUPS):
                r = 0
                for name, n in names:
                    if name.startswith("ffn_conv_w"):
                        src = io["ffn_conv_w_2"][int(name[-1])]
                    elif name == "conv_w_2":
                        src = io[name].rearrange("k c -> (k c)")
                    else:
                        src = io[name]
                    sp.dma_start(vrows[r:r + n, g, :], src.rearrange("(r c) -> r c", c=P)).then_inc(S("vec_loaded"), 16)
                    r += n
            for dst, src in ((onehot, io["const_onehot"]), (maskt, io["const_mask"]), (relb, io["rel_bias"]),
                             (wa2, io["gla_w_a2"])):
                sp.dma_start(dst[:], src).then_inc(S("tables_loaded"), 16)
            sp.wait_ge(S("tabs_ready"), 2)
            sp.dma_start(tab_dram, tabs[:]).then_inc(S("tab_stored"), 16)
            stream(gB, 2, 1, cols(w_in, KT, lambda i, j: COL_B + 2 * P + P * j), first=2)
            sp.wait_ge(S("tab_stored"), 16)
            sp.dma_start(strip_dram, bass.AP(tab_dram.tensor, P - 1, [[TAB, 2 * PAIRS], [-1, P], [1, SEQ]])
                         ).then_inc(S("strips_stored"), 16)
            stream(gB, 2, NB_B // 2 - 2, cols(w_in, KT, lambda i, j: 2 * P * i + (COL_B + 4 * P + P * j)), first=4)
            stream(gB, 1, 1, cols(w_in, KT, lambda i, j: COL_B + P * (NB_B - 1)), first=NB_B - 1)
            bases = (COL_AQ, COL_AK, COL_CQ, COL_CK)

            def qk_load(c, i, j):
                slot = gQK.slot(j)
                load(gQK.n0 + c, slot, [(Wraw[slot][:], w_in[:, :, ds(P * i + bases[j], P)])])

            def v_load(c, i, j):
                slot = gV.slot(j)
                load(gQK.n0 + c, slot, [(Wraw[slot][:], w_in[:, :, ds(P * i + (COL_AV, COL_CV)[j], P)])])

            qk_load(0, 0, 0)
            qk_load(1, 0, 1)
            sp.wait_ge(s_ev, gB.b0 + 4)
            sp.dma_start(bv_dram.rearrange("(k p) t -> p k t", p=P), bT[:, 2:4, :]).then_inc(S("bv_stored"), 16)
            sp.wait_ge(S("bv_stored"), 16)

            def gla_values(g, par):
                if not isinstance(g, int) or g >= 2:
                    sp.wait_ge(S("gla_scanned"), GLA_GROUP * g - GLA_GROUP)
                for h in range(B_HEADS):
                    src = bv_dram[ds(h * B_VAL + GLA_GROUP * g, GLA_GROUP), :].rearrange("v t -> (v t)")
                    sp.dma_start(vb[h * B_KEY:(h + 1) * B_KEY, par, :, :].rearrange("p v t -> p (v t)"),
                                 src.unsqueeze(0).to_broadcast([B_KEY, GLA_GROUP * SEQ])
                                 ).then_inc(S(f"gla_values{par}"), 16)

            gla_values(0, 0)
            gla_values(1, 1)
            qk_load(2, 0, 2)
            qk_load(3, 0, 3)
            gla_values(2, 0)

            def qk_round(i):
                for j in range(4):
                    qk_load(4 * i + (4 + j), i + 1, j)
                    gla_values(4 * i + (3 + j), (3 + j) % 2)
            repeat(sp, 2, qk_round)
            qk_blocks = 4 * PAIRS // 2

            def v_round(i):
                for j in range(2):
                    v_load(2 * i + (qk_blocks + j), i, j)
                    gla_values(2 * i + (qk_blocks - 1 + j), (qk_blocks - 1 + j) % 2)
            repeat(sp, PAIRS // 2 - 1, v_round)
            v_load(qk_blocks + PAIRS - 2, PAIRS // 2 - 1, 0)
            gla_values(GLA_GROUPS - 1, (GLA_GROUPS - 1) % 2)
            v_load(qk_blocks + PAIRS - 1, PAIRS // 2 - 1, 1)
            sp.wait_ge(S("strips_stored"), 16)

            def strip(s, par):
                if not isinstance(s, int) or s >= 2:
                    sp.wait_ge(S("a_logits"), 4 * s - 4)
                sp.dma_start(Z[:, par, :], strip_dram[ds(s, 1), :, :].rearrange("h p j -> (h p) j")
                             ).then_inc(S(f"strip_loaded{par}"), 16)
            strip(0, 0)
            strip(1, 1)
            w_out = wcols("w_out", 0, KT)
            a, b = A_W // P, (A_W + B_W) // P

            def out_blocks(i0):
                return lambda i, j, slot: [
                    (Wraw[slot][:, 0:a, :], w_out[:, 0:a, ds(2 * P * i + P * (2 * i0 + j), P)]),
                    (Wraw[slot][:, a:2 * a, :], w_out[:, b:KT, ds(2 * P * i + P * (2 * i0 + j), P)]),
                    (Wraw[slot][:, 2 * a:KT, :], w_out[:, a:b, ds(2 * P * i + P * (2 * i0 + j), P)])]
            stream(gOut, 2, 2, out_blocks(0))

            def strip_pair(p):
                for par in range(2):
                    strip(2 * p + (2 + par), par)
            repeat(sp, PAIRS - 1, strip_pair)
            stream(gOut, 2, KT // 2 - 2, out_blocks(2), first=4)
            ff1 = wcols("w_ff1", 0, KT)
            ff2 = io["w_ff2"].rearrange("(g k p) c -> g p k c", k=KT, p=P)
            ada = io["w_ada_2"].rearrange("(k p) (m c) -> k p m c", p=P, c=ADA_COLS)
            sp.wait_ge(S("a_low"), PAIRS)

            def ff_group(o):
                for gi in range(2):
                    for half in range(2):
                        ph = gFF[gi][half]

                        def body(q, gi=gi, half=half, ph=ph):
                            for h in range(2):
                                for j in range(2):
                                    b = 4 * q + (2 * h + j)
                                    slot = ph.slot(j)
                                    if half == 0:
                                        src = ff1[:, :, ds(P * b + (2 * KT * P * o + KT * P * gi), P)]
                                    else:
                                        src = ff2[ds(2 * o + gi, 1), :, :, ds(P * b, P)].rearrange("g p k c -> (g p) k c")
                                    load(2 * FF_SLOTS * o + b + ph.n0, slot, [(Wraw[slot][:], src)])
                                for j in range(2):
                                    e, c = 2 * h + j, 4 * KT * o + 4 * q + (2 * KT * gi + KT * half + 2 * h + j)
                                    if not isinstance(c, int) or c >= ADA_DEEP:
                                        sp.wait_ge(S("ada_used"), c - 2)
                                    sp.dma_start(wada[:, e, :],
                                                 ada[ds(4 * q + e, 1), :, ds(4 * o + (2 * gi + half), 1), :]
                                                 .rearrange("k p m c -> (k p) (m c)")).then_inc(S(f"ada_loaded{e}"), 16)
                        (repeat if gi or half or not isinstance(o, int) or o else peeled)(sp, KT // 4, body)
            peeled(sp, FF_GROUPS // 2, ff_group)
            w_in2 = wcols("w_in_2", 0, KT)
            wga = io["w_gate_a_2"].rearrange("(t b) d e -> t b d e", b=2)
            wgx = io["w_gate_x_2"].rearrange("(t b) d e -> t b d e", b=2)

            def rnn_gates(t, par):
                if not isinstance(t, int) or t >= 2:
                    sp.wait_ge(S("rnn_gated"), t - 1)
                for w, bd in ((wga, BDa), (wgx, BDx)):
                    for b in range(2):
                        q = slice(b * RNN_BLOCK, (b + 1) * RNN_BLOCK)
                        sp.dma_start(bd[q, par, q], w[ds(t, 1), b, :, :].rearrange("t d e -> (t d) e")
                                     ).then_inc(S(f"rnn_weights{par}"), 16)

            stream(gX, 2, RT // 2, cols(w_in2, KT, lambda i, j: 2 * P * i + P * j))
            sp.wait_ge(S("bd_cleared"), 2)
            sp.dma_start(posr[:], io["positions_2"].to_broadcast([P, SEQ])).then_inc(S("reset_loaded"), 16)
            rnn_gates(0, 0)
            rnn_gates(1, 1)
            stream(gGate, 2, 1, cols(w_in2, KT, lambda i, j: COL_GATE + P * j))
            pairs = RT // 2

            def gate_round(i):
                for j in range(2):
                    slot = gGate.slot(j)
                    load(2 * i + (gGate.n0 + 2 + j), slot,
                         [(Wraw[slot][:], w_in2[:, :, ds(2 * P * i + (COL_GATE + 2 * P + P * j), P)])])
                for j in range(2):
                    rnn_gates(2 * i + (2 + j), j)
            repeat(sp, pairs - 1, gate_round)
            stream(gGate, 2, KT - pairs, cols(w_in2, KT, lambda i, j: 2 * P * i + (COL_GATE + 2 * P * pairs + P * j)),
                   first=2 * pairs)
            sp.wait_ge(S("rnn_low"), RT)
            sp.dma_start(posb[:], io["positions_2"].to_broadcast([P, SEQ])).then_inc(S("pos_loaded"), 16)
            stream(gLat, 2, (QT + KVT) // 2, cols(w_in2, KT, lambda i, j: 2 * P * i + (COL_LAT + P * j)))
            stream(gLat, 1, 1, cols(w_in2, KT, lambda i, j: COL_LAT + P * (QT + KVT - 1)), first=QT + KVT - 1)
            half = ROPE // 2
            stream(gRope, 1, 1, lambda i, j, slot: [
                (Wraw[slot][:, :, 0:QKD], w_in2[:, :, COL_ROPE - NOPE:COL_ROPE + ROPE]),
                (Wraw[slot][:, :, QKD:QKD + half], w_in2[:, :, COL_ROPE + half:COL_ROPE + ROPE]),
                (Wraw[slot][:, :, QKD + half:P], w_in2[:, :, COL_ROPE:COL_ROPE + half])])
            wpr = io["w_proj_rnn_2"].rearrange("(q k p) c -> q p k c", k=RNN_KS[0], p=P)
            stream(gPR, 4, KT // 2, lambda i, j, slot: [
                (Wraw[slot][:, 0:RNN_KS[0], :], wpr[j % 2][:, :, ds(2 * P * i + P * (j // 2), P)])])
            wuq, wukv = wcols("w_uq_2", 0, QT), wcols("w_ukv_2", 0, KVT)
            stream(gHead, 2, N_MLA // 2, lambda i, j, slot: [
                (Wraw[slot][:, 0:QT, 0:QKD], wuq[:, :, ds(2 * QKD * i + QKD * j, QKD)]),
                (Wraw[slot][:, 0:QT, QKD:QKD + half], wuq[:, :, ds(2 * QKD * i + (QKD * j + NOPE + half), half)]),
                (Wraw[slot][:, 0:QT, QKD + half:P], wuq[:, :, ds(2 * QKD * i + (QKD * j + NOPE), half)]),
                (Wraw[slot][:, QT:QT + KVT, :], wukv[:, :, ds(2 * P * i + P * j, P)])])
            stream(gPM, 2, KT // 2, cols(wcols("w_proj_mla_2", 0, KT), KT, lambda i, j: 2 * P * i + P * j))
            stream(gOut2, 2, KT // 2, cols(wcols("w_out_2", 0, KT), KT, lambda i, j: 2 * P * i + P * j))
            stream(gUp, 2, FT, cols(wcols("w_up_2", 0, KT), KT, lambda i, j: P * i + D_FF2 * j))
            downs, r = [], 0
            for k in DOWN_KS:
                downs.append(wcols("w_down_2", r * P, k))
                r += k
            stream(gDown, 2 * len(DOWN_KS), KT // 2, lambda i, j, slot: [
                (Wraw[slot][:, 0:DOWN_KS[j % 3], :], downs[j % 3][:, :, ds(2 * P * i + P * (j // 3), P)])])
            y_rows = out[0].rearrange("(t p) d -> p t d", p=P)
            for t in range(TB):
                sp.wait_ge(S(f"rows_scaled{t % 2}"), t // 2 + 1)
                sp.dma_start(y_rows[:, t, :], yrow[:, t, :]).then_inc(S("stored"), 16)
            sp.wait_ge(S("stored"), 16 * TB)

        @block.gpsimd
        def _(pool):
            def low(n, slot, kts=KT):
                pool.wait_ge(s_hi, n + 1)
                nc.gpsimd.tensor_tensor(WL[slot][:, 0:kts, :], Wraw[slot][:, 0:kts, :],
                                        WH[slot][:, 0:kts, :].bitcast(F32), ALU.subtract).then_inc(s_lo, 1)

            def lows(ph, per, rounds, first=0, extra=0):
                def body(i):
                    for j in range(per):
                        low((per + extra) * i + (ph.n0 + first + j), ph.slot(first + j), ph.ks[(first + j) % len(ph.ks)])
                repeat(pool, rounds, body)

            def power(name, at=0):
                pool.wait_ge(*N(name, "mean", 1))
                nc.gpsimd.tensor_tensor(rtok[:, at + 1, :], rtok[:, at, :], half[:], ALU.pow).then_inc(S("norm_power"), 1)

            nc.gpsimd.memset(half[:], -0.5).then_inc(S("half_set"), 1)
            nc.gpsimd.memset(ones[:], 1.0).then_inc(S("ones_set"), 1)
            lows(gB, 2, 1)
            pool.wait_ge(S("half_set"), 1)
            power("n1")
            lows(gB, 2, NB_B // 2 - 1, first=2)
            lows(gB, 1, 1, first=NB_B - 1)

            def gla_products(g, par):
                pool.wait_ge(S(f"gla_values{par}"), 32 * g + (64 - 32 * par))
                for j in range(GLA_GROUP - 1):
                    if not isinstance(g, int) or g > 0:
                        pool.wait_ge(S("gla_scanned"), GLA_GROUP * g + (j + 1 - GLA_GROUP))
                    nc.gpsimd.tensor_tensor(kvp[:, j, :], bT[:, 1, :], vb[:, par, j, :], ALU.mult).then_inc(S("gla_kv"), 1)

            lows(gQK, 2, 1)

            def gla_round(i):
                for j in range(2):
                    gla_products(2 * i + j, j)
                    low(2 * i + (gQK.n0 + 2 + j), gQK.slot(j))
            peeled(pool, GLA_GROUPS // 2, gla_round)
            pool.wait_ge(s_ev, gV.b0)
            pool.wait_ge(S("values_turned"), PAIRS)

            def stage_qk(s, t, par):
                q = slice(HEAD_DIM * par, HEAD_DIM * (par + 1))
                if not isinstance(s, int) or s >= 2:
                    pool.wait_ge(S("a_v_staged"), s - 1)
                    pool.wait_ge(S("a_scored"), 4 * s - 4)
                for staged, src in ((Qs, qT), (Ks, kT)):
                    nc.gpsimd.tensor_copy(staged[q, :], src[q, ds(t, 1), :].rearrange("p a t -> p (a t)")
                                          ).then_inc(S("a_qk_staged"), 1)

            def stage_v(s, t, par, staged):
                q = slice(HEAD_DIM * par, HEAD_DIM * (par + 1))
                pool.wait_ge(S("a_qk_staged"), 2 * staged)
                if not isinstance(s, int) or s >= 2:
                    pool.wait_ge(S("a_weighted"), s - 1)
                nc.gpsimd.tensor_copy(Vs[:, :, q], Vt[:, ds(t, 1), :, q].rearrange("p a t d -> p (a t) d")
                                      ).then_inc(S("a_v_staged"), 1)

            stage_qk(0, 0, 0)
            stage_qk(1, 0, 1)
            stage_v(0, 0, 0, 2)

            def stage_pair(p):
                stage_qk(2 * p + 2, p + 1, 0)
                stage_v(2 * p + 1, p, 1, 2 * p + 3)
                stage_qk(2 * p + 3, p + 1, 1)
                stage_v(2 * p + 2, p + 1, 0, 2 * p + 4)
            lows(gOut, 2, 1)
            peeled(pool, PAIRS - 1, stage_pair)
            stage_v(2 * PAIRS - 1, PAIRS - 1, 1, 2 * PAIRS)
            pool.wait_ge(S("a_low"), PAIRS)
            nc.gpsimd.memset(adaacc[:], 0.0).then_inc(S("ada_used"), 1)
            lows(gOut, 2, KT // 2 - 1, first=2)

            def ff_group(o):
                for gi in range(2):
                    for half in range(2):
                        ph = gFF[gi][half]

                        def body(p, ph=ph):
                            for j in range(2):
                                low(2 * FF_SLOTS * o + 2 * p + (ph.n0 + j), ph.slot(j))

                        if gi or half or o:
                            repeat(pool, KT // 2, body)
                        else:
                            low(ph.n0, ph.slot(0))
                            power("n2")
                            low(ph.n0 + 1, ph.slot(1))
                            repeat(pool, KT // 2 - 1, lambda p: body(p + 1))
            for o in range(FF_GROUPS // 2):
                ff_group(o)
            lows(gX, 2, 1)
            power("n3")
            power("n4", 2)
            pool.wait_ge(S("ada_used"), 1 + 2 * KT * FF_GROUPS)
            nc.gpsimd.memset(BDa[:], 0.0).then_inc(S("bd_cleared"), 1)
            nc.gpsimd.memset(BDx[:], 0.0).then_inc(S("bd_cleared"), 1)
            lows(gX, 2, RT // 2 - 1, first=2)
            lows(gGate, 2, KT)
            lows(gLat, 2, (QT + KVT) // 2)
            lows(gLat, 1, 1, first=QT + KVT - 1)
            lows(gRope, 1, 1)
            lows(gPR, 4, KT // 2)

            def heads(i):
                for j in range(2):
                    low(2 * i + (gHead.n0 + j), gHead.slot(j), QT + KVT)
            repeat(pool, N_MLA // 2, heads)
            for ph in (gPM, gOut2):
                lows(ph, 2, KT // 2)
            low(gUp.n0, gUp.slot(0))
            power("n5")
            low(gUp.n0 + 1, gUp.slot(1))
            lows(gUp, 2, FT - 1, first=2)
            lows(gDown, 2 * len(DOWN_KS), KT // 2)
            power("n6")

        @block.scalar
        def _(act):
            own = Steps(act, S("scalar_steps"))
            A = nc.scalar.activation

            def high(ph, j, n, loaded, kts=KT):
                act.wait_ge(*loaded)
                if not isinstance(n, int) or n >= 2:
                    act.wait_ge(s_mm, n - 1)
                slot = ph.slot(j)
                A(WH[slot][:, 0:kts, :], Wraw[slot][:, 0:kts, :], ACT.Copy).then_inc(s_hi, 1)

            def highs(ph, per, rounds, first=0):
                def body(i):
                    for j in range(per):
                        high(ph, first + j, per * i + (ph.n0 + first + j), landed(ph, first + j, i, per),
                             ph.ks[(first + j) % len(ph.ks)])
                repeat(act, rounds, body)

            def ff_high(ph, j, o, p, at=0):
                per = FF_SLOTS
                sem, v = landed(ph, j)
                high(ph, j, 2 * FF_SLOTS * o + 2 * p + (ph.n0 + j), (sem, 16 * per * o + 16 * p + v))

            def squares(name, tiles, src):
                for k in range(tiles):
                    if k >= 2:
                        act.wait_ge(*N(name, "summed", k - 1))
                    A(T[k % 2][:], src(k), ACT.Square).then_inc(S("norm_squared"), 1)

            def square(name, k, j, there, at=0, acc=5, weight=None):
                act.wait_ge(*there)
                if not isinstance(k, int) or k >= 3:
                    act.wait_ge(*N(name, "added", k - 2))
                A(T[acc if isinstance(k, int) and k == 0 else at + j][:], xT[:, ds(k, 1), :].rearrange("p a t -> p (a t)"),
                  ACT.Square, **({} if weight is None else {"scale": vec[:, ds(k + VEC[weight], 1)]})
                  ).then_inc(N(name, "squared", 0)[0], 1)

            def root(name, sums, dim, dst=None, bank=2):
                act.wait_ge(*N(name, "summed", sums))
                A((rstd if dst is None else dst)[:], ps[:, bank, :], ACT.Sqrt, bias=epsc, scale=1.0 / dim
                  ).then_inc(S("norm_root"), 1)

            def norm_highs(name, tiles, dsts, shift=None):
                for k in range(tiles):
                    act.wait_ge(*N(name, "scaled", k + 1))
                    A(dsts(k), T[2 + k % 4][:], ACT.Copy if shift is None else ACT.Identity,
                      **({} if shift is None else {"bias": shift(k)})).then_inc(S("norm_high"), 1)

            def x_square(k):
                if k % 2:
                    act.wait_ge(S("x_transposed"), k + 1)
                    A(xT[:, k, :], ps[:, 7, :], ACT.Copy).then_inc(S("x_turned1"), 1)
                square("n1", k, k % 2, (S(f"x_turned{k % 2}"), k // 2 + 1))
            for k in range(KT // 2):
                x_square(k)
            highs(gB, 2, 1)
            for k in range(KT // 2, KT):
                x_square(k)
            act.wait_ge(S("const_loaded"), 16)
            norm_highs("n1", KT, lambda k: actH[:, k, :])
            highs(gB, 2, NB_B // 2 - 1, first=2)
            highs(gB, 1, 1, first=NB_B - 1)
            highs(gQK, 2, 1)
            act.wait_ge(s_ev, gB.b0 + NB_B)
            act.wait_ge(S("gla_zmin"), 1)
            own.done(A(T[1][:], ps[:, 2, :], ACT.Abs, bias=vec[:, VEC["gla_b_a"]:VEC["gla_b_a"] + 1]))
            own.done(A(T[1][:], T[1][:], ACT.Exp, scale=-1.0))
            A(T[1][:], T[1][:], ACT.Ln, bias=ones[:, 0:1]).then_inc(S("gla_log"), 1)
            act.wait_ge(S("gla_logsig"), 1)
            A(alpha[:], T[0][:], ACT.Exp, scale=1.0 / B_TAU).then_inc(S("gla_alpha"), 1)
            A(bT[:, 4:6, :], bT[:, 4:6, :], ACT.Silu).then_inc(S("gla_silu"), 1)
            act.wait_ge(S("tab_stored"), 16)

            def qk_evac(i, j):
                act.wait_ge(s_mm, 4 * i + (gQK.n0 + j + 1))
                A((qT, kT)[j % 2][:, ds(i + (PAIRS // 2) * (j // 2), 1), :].rearrange("p a t -> p (a t)"),
                  ps[:, gQK.bank(j), :], ACT.Copy).then_inc(s_ev, 1)

            def qk_round(i):
                for j in range(4):
                    high(gQK, 2 + j, 4 * i + (gQK.n0 + 2 + j), landed(gQK, 2 + j, i, 4))
                    qk_evac(i, j)
            repeat(act, PAIRS // 2 - 1, qk_round)
            last = PAIRS // 2 - 1
            for j in range(4):
                if j < 2:
                    high(gQK, 2 + j, 4 * last + gQK.n0 + 2 + j, landed(gQK, 2 + j, last, 4))
                else:
                    high(gV, j - 2, gV.n0 + j - 2, landed(gV, j - 2))
                qk_evac(last, j)

            def values_turned(v):
                act.wait_ge(S("v_turned"), v + 1)
                A(Vt[:, v // 2 + PAIRS // 2 * (v % 2), :, :].rearrange("p t d -> p (t d)"), ps[:, 5 + v % 2, :], ACT.Copy
                  ).then_inc(S("values_turned"), 1)

            def sums_out(b):
                act.wait_ge(S("gla_summed"), (b + 1) * GLA_GROUP * SUM_GROUPS)
                A(T[b][:], ps[:, 2 + b, :], ACT.Copy).then_inc(S("gla_out_of_psum"), 1)

            sums_out(0)
            for v in range(PAIRS):
                if v + 2 < PAIRS:
                    high(gV, v + 2, gV.n0 + v + 2, landed(gV, v + 2))
                act.wait_ge(s_mm, gV.n0 + v + 1)
                if v >= 2:
                    act.wait_ge(S("v_turned"), v - 1)
                A(T[2 + v % 2][:], ps[:, gV.bank(v), :], ACT.Copy).then_inc(s_ev, 1)
                if v:
                    values_turned(v - 1)
            values_turned(PAIRS - 1)
            sums_out(1)
            act.wait_ge(S("gla_ms"), 1)
            A(T[0][:, 0:16], T[0][:, 0:16], ACT.Sqrt, bias=epsc, scale=1.0 / B_VAL).then_inc(S("gla_root"), 1)
            highs(gOut, 2, 1)
            for e in range(2):
                act.wait_ge(S("gla_out"), e + 1)
                A(actH[:, 2 * A_W // P + e, :], T[2 + e][:], ACT.Copy).then_inc(S("gla_high"), 1)

            def exps(pre, lp, s, par, i):
                off = i * (i + 1) // 2 * P
                act.wait_ge(S(pre + "_logits"), 4 * s + (i + 1))
                A(lp[:, par, off:off + (i + 1) * P], lp[:, par, off:off + (i + 1) * P], ACT.Exp,
                  bias=stat[:, 0, par, i:i + 1], scale=-1.0, accum_out=stat[:, 1, par, i:i + 1]
                  ).then_inc(S(pre + "_exp"), 1)

            def turned(pre, pt, s, i):
                act.wait_ge(S(pre + "_turned"), 4 * s + (i + 1))
                A(pt[:, 0:i + 1, i * P:(i + 1) * P], ps[:, 5 + i % 2, 0:(i + 1) * P].rearrange("p (k q) -> p k q", q=P),
                  ACT.Copy).then_inc(S(pre + "_pt"), 1)

            def pair_high(pre, p, dst):
                act.wait_ge(S(pre + "_weighted"), 2 * p + 2)
                A(dst[:, ds(p, 1), :].rearrange("p a t -> p (a t)"), ps[:, 7, :], ACT.Copy
                  ).then_inc(S(pre + "_high"), 1)

            def a_turned(s, par, i):
                turned("a", PT[:, par], s, i)

            def a_step(s, par, p=None):
                for i in range(TB):
                    exps("a", LP, s, par, i)
                    if i == 2 and p is not None:
                        pair_high("a", p, actH)
                    if not (isinstance(s, int) and s == 0):
                        a_turned(s - 1, 1 - par, i)

            a_step(0, 0)
            a_step(1, 1)

            def pair(p):
                a_step(2 * p + 2, 0)
                a_step(2 * p + 3, 1, p)
            repeat(act, PAIRS - 1, pair)
            for i in range(TB):
                a_turned(2 * PAIRS - 1, 1, i)
            pair_high("a", PAIRS - 1, actH)
            def out_squares(name, ph, next_high):
                def body(i, last=False):
                    for j in range(2):
                        if last:
                            next_high(j)
                        else:
                            high(ph, 2 + j, 2 * i + (ph.n0 + 2 + j), landed(ph, 2 + j, i))
                        square(name, 2 * i + j, j, (s_ev, 2 * i + (ph.b0 + j + 1)))
                peeled(act, KT // 2 - 1, body)
                body(KT // 2 - 1, True)
            out_squares("n2", gOut, lambda j: ff_high(gFF[0][0], j, 0, 0))
            norm_highs("n2", KT, lambda k: actH[:, k, :])
            A(cact[:], vec[:, VEC["c_2"]:VEC["c_2"] + KT], ACT.Silu).then_inc(S("c_ready"), 1)
            own.done(A(nsp[:, 1, :], vec[:, VEC["lru_param_2"]:VEC["lru_param_2"] + RT], ACT.Abs))
            A(nsp[:, 1, :], nsp[:, 1, :], ACT.Exp, scale=-1.0).then_inc(S("lru_exp"), 1)

            def relu(ph, o, gi, p, j):
                b = 2 * FF_SLOTS * o + 2 * p + (ph.b0 + j)
                f = 2 * KT * o + 2 * p + (KT * gi + j)
                act.wait_ge(s_mm, 2 * FF_SLOTS * o + 2 * p + (ph.n0 + j + 1))
                if not isinstance(f, int) or f >= 2:
                    act.wait_ge(S("hid_squared"), f - 1)
                A(T[j][:], ps[:, ph.bank(j), :], ACT.Relu).then_inc(s_ev_act, 1)

            def square_high(o, gi, p, j):
                f = 2 * KT * o + 2 * p + (KT * gi + j)
                act.wait_ge(S("hid_squared"), f + 1)
                A(UH[:, ds(2 * p + (KT * gi + j), 1), :].rearrange("p a t -> p (a t)"), T[2 + j][:], ACT.Copy
                  ).then_inc(S("hid_high"), 1)

            s_ev_act = S("hid_relu")

            def ff_group(o):
                for gi in range(2):
                    one, two = gFF[gi]
                    nxt = gFF[gi + 1][0] if gi == 0 else None

                    def first(p, one=one, gi=gi):
                        for j in range(2):
                            ff_high(one, j, o, p + 1)
                            relu(one, o, gi, p, j)
                        for j in range(2):
                            square_high(o, gi, p, j)
                    (repeat if o or gi else peeled)(act, KT // 2 - 1, first)
                    for j in range(2):
                        ff_high(two, j, o, 0)
                        relu(one, o, gi, KT // 2 - 1, j)
                    for j in range(2):
                        square_high(o, gi, KT // 2 - 1, j)

                    last = o == FF_GROUPS // 2 - 1 and gi == 1

                    def second(p, two=two, last=last):
                        for j in range(2):
                            ff_high(two, j, o, p + 1)
                            if last:
                                final_squares(p, j)
                    (peeled if last else repeat)(act, KT // 2 - 1, second)
                    if gi == 0:
                        for j in range(2):
                            ff_high(nxt, j, o, 0)
            def final_squares(p, j):
                there = (S("x_added"), 2 * p + (KT * (FF_GROUPS - 1) + j + 1))
                square("n3", 2 * p + j, j, there)
                square("n4", 2 * p + j, j, there, 2, 4, "final_norm_w")
            ff_group(0)
            for j in range(2):
                ff_high(gFF[0][0], j, 1, 0)
            ff_group(1)
            for j in range(2):
                high(gX, j, gX.n0 + j, landed(gX, j))
                final_squares(KT // 2 - 1, j)
            act.wait_ge(S("mod_ready"), 1)
            norm_highs("n4", KT, lambda k: actH[:, k, :], lambda k: mod[:, k:k + 1])

            def bias_at(name, t, j):
                return vec[:, ds(t + (VEC[name] + j), 1)]

            def rnn_sigmoids(t, j):
                act.wait_ge(S("rnn_gated"), t + (j + 1))
                if not isinstance(t, int) or t > 0:
                    act.wait_ge(S("rnn_low"), t + (j - 1))
                A(T[j][:], ps[:, 2 + 2 * j, :], ACT.Sigmoid, bias=bias_at("b_gate_a_2", t, j)).then_inc(S("rnn_sig"), 1)
                A(T[2 + j][:], ps[:, 3 + 2 * j, :], ACT.Sigmoid, bias=bias_at("b_gate_x_2", t, j)).then_inc(S("rnn_sig"), 1)

            def rnn_rest(t, between):
                marks = []
                for j in range(2):
                    act.wait_ge(S("rnn_loga"), t + (j + 1))
                    A(rA[:, j, :], T[j][:], ACT.Exp).then_inc(S("rnn_a"), 1)
                    A(rTh[:, j, :], T[j][:], ACT.Tanh, scale=-1.0).then_inc(S("rnn_tanh"), 1)
                for j in range(2):
                    act.wait_ge(S("rnn_m2"), t + (j + 1))
                    A(rTh[:, j, :], rTh[:, j, :], ACT.Sqrt).then_inc(S("rnn_mult"), 1)
                between()
                for j in range(2):
                    act.wait_ge(S("rnn_state"), t + (j + 1))
                    A(UH[:, ds(t + j, 1), :].rearrange("p a t -> p (a t)"), T[j][:], ACT.Copy).then_inc(S("rnn_high"), 1)

            highs(gX, 2, RT // 2 - 1, first=2)
            highs(gGate, 2, 1)

            def gate_round(dst, t0, rnn=False, ahead=True):
                def evac(i, j, dst, t0):
                    act.wait_ge(s_mm, 2 * i + (gGate.n0 + j + 1))
                    A(dst[:, ds(2 * i + (j - t0), 1), :].rearrange("p a t -> p (a t)"), ps[:, gGate.bank(j), :],
                      ACT.Sigmoid).then_inc(S("gate_evacuated"), 1)

                def body(i):
                    after_rnn = not (isinstance(i, int) and (i == 0 or i > RT // 2))
                    last_rnn = isinstance(i, int) and i == RT // 2 - 1
                    for j in range(2):
                        if not ahead and j == 0:
                            high(gLat, 0, gLat.n0, landed(gLat, 0))
                        elif ahead and not (j == 0 and after_rnn):
                            high(gGate, 2 + j, 2 * i + (gGate.n0 + 2 + j), landed(gGate, 2 + j, i))
                        if rnn or j or not after_rnn:
                            evac(i, j, dst, t0)
                        if not ahead and j == 1:
                            high(gLat, 1, gLat.n0 + 1, landed(gLat, 1))
                        if rnn:
                            rnn_sigmoids(2 * i, j)

                    def between():
                        high(gGate, 4, 2 * i + (gGate.n0 + 4), landed(gGate, 4, i))
                        if last_rnn:
                            evac(i + 1, 0, gM, KT)
                    if rnn:
                        rnn_rest(2 * i, between)
                return body
            peeled(act, KT // 2, gate_round(gR, 0, rnn=True))
            for i in range(KT // 2, RT // 2):
                gate_round(gM, KT, rnn=True)(i)
            for i in range(RT // 2, KT):
                gate_round(gM, KT, ahead=i + 1 < KT)(i)
            act.wait_ge(S("rot_angle"), 1)
            A(CS[NOPE:P, :], rott[NOPE:P, :], ACT.Sin).then_inc(S("rot_ready"), 1)
            for b in range(2, QT + KVT):
                high(gLat, b, gLat.n0 + b, landed(gLat, b))
            high(gRope, 0, gRope.n0, landed(gRope, 0))
            act.wait_ge(s_ev, gLat.b0 + QT)
            squares("nq", QT, lambda k: lat[:, k, :])

            def pr_high(n):
                high(gPR, n, gPR.n0 + n, landed(gPR, n), RNN_KS[n % 2])
            pr_high(0)
            root("nq", QT, Q_LORA)
            act.wait_ge(s_ev, gLat.b0 + QT + KVT)
            squares("nkv", KVT, lambda k: lat[:, QT + k, :])
            pr_high(1)
            root("nkv", KVT, KV_LORA, Vf, 3)
            norm_highs("nq", QT, lambda k: actH[:, k, :])
            pr_high(2)
            pr_high(3)
            norm_highs("nkv", KVT, lambda k: actH[:, QT + k, :])

            def pr_round(i):
                for j in range(4):
                    high(gPR, j, 4 * i + (gPR.n0 + 4 + j), landed(gPR, 4 + j, i, 4), RNN_KS[j % 2])
            repeat(act, KT // 2 - 1, pr_round)

            def head_high(s, par):
                sem, v = landed(gHead, par)
                p = (s - par) // 2 if isinstance(s, int) else None
                high(gHead, par, s + gHead.n0, (sem, 64 * p + v) if p is not None else (sem, (s - par) * 32 + v),
                     QT + KVT)

            def key_evac(s, par):
                act.wait_ge(S("m_kv_made"), s + 1)
                A(Kp[0:NOPE, par, :], ps[0:NOPE, 1, :], ACT.Copy).then_inc(S("m_k_ready"), 1)

            def value_evac(s, par):
                act.wait_ge(S("m_v_turned"), s + 1)
                if not isinstance(s, int) or s >= 2:
                    act.wait_ge(S("m_weighted"), s - 1)
                A(Vp[:, par, :, :], ps[:, 1, 0:TB * VH].rearrange("p (t d) -> p t d", d=VH), ACT.Copy
                  ).then_inc(S("m_v_ready"), 1)

            head_high(0, 0)
            head_high(1, 1)
            key_evac(0, 0)
            value_evac(0, 0)

            def head(s, par, more, ahead, p=None):
                for i in range(TB):
                    exps("m", LP2, s, par, i)
                    if not (isinstance(s, int) and s == 0):
                        turned("m", PT2, s - 1, i)
                    if i == 0 and p is not None:
                        pair_high("m", p, UH)
                if more:
                    key_evac(s + 1, 1 - par)
                if ahead:
                    head_high(s + 2, par)
                if more:
                    value_evac(s + 1, 1 - par)

            head(0, 0, True, True)

            def head_pair(p, before=None):
                head(2 * p + 1, 1, True, True, before)
                head(2 * p + 2, 0, True, True)
            head_pair(0)
            repeat(act, N_MLA // 2 - 3, lambda p: head_pair(p + 1, p))
            head(N_MLA - 3, 1, True, True, N_MLA // 2 - 3)
            head(N_MLA - 2, 0, True, False)
            head(N_MLA - 1, 1, False, False, N_MLA // 2 - 2)
            for i in range(TB):
                turned("m", PT2, N_MLA - 1, i)
            highs(gPM, 2, 1)
            pair_high("m", N_MLA // 2 - 1, UH)

            def merged_high(p, j):
                act.wait_ge(S("merged"), 2 * p + (j + 1))
                A(actH[:, ds(2 * p + j, 1), :].rearrange("p a t -> p (a t)"), T[j][:], ACT.Copy).then_inc(S("merged_high"), 1)

            def pm_round(p):
                for j in range(2):
                    sem, v = landed(gPM, 2 + j)
                    high(gPM, j, 2 * p + (gPM.n0 + 2 + j), (sem, 16 * p + v))
                for j in range(2):
                    merged_high(p, j)
            repeat(act, KT // 2 - 1, pm_round)
            highs(gOut2, 2, 1)
            for j in range(2):
                merged_high(KT // 2 - 1, j)
            out_squares("n5", gOut2, lambda j: high(gUp, j, gUp.n0 + j, landed(gUp, j)))
            act.wait_ge(S("mod_ready"), 2)
            norm_highs("n5", KT, lambda k: actH[:, k, :], lambda k: mod[:, 3 * KT + k:3 * KT + k + 1])

            def up_parts(t, j):
                act.wait_ge(S("up_gate"), t + 1)
                if not isinstance(t, int) or t >= 2:
                    act.wait_ge(S("up_low"), t - 1)
                A(act2[:, j, :], cg[:, j, :], ACT.Silu).then_inc(S("up_silu"), 1)

            def up_high(t, j):
                act.wait_ge(S("up_product"), t + 1)
                A(UH[:, ds(t, 1), :].rearrange("p a t -> p (a t)"), act2[:, j, :], ACT.Copy).then_inc(S("up_high"), 1)

            def up_round(p):
                for j in range(2):
                    for h in range(2):
                        sem, v = landed(gUp, 2 * j + 2 + h)
                        high(gUp, h, 4 * p + (gUp.n0 + 2 * j + 2 + h), (sem, 32 * p + v))
                    up_parts(2 * p + j, j)
                    up_high(2 * p + j, j)
            peeled(act, FT // 2 - 1, up_round)
            for h in range(2):
                high(gUp, h, gUp.n0 + 2 * FT - 2 + h, landed(gUp, 2 * FT - 2 + h))
            up_parts(FT - 2, 0)
            up_high(FT - 2, 0)
            for h in range(2):
                high(gDown, h, gDown.n0 + h, landed(gDown, h), DOWN_KS[h])
            up_parts(FT - 1, 1)
            up_high(FT - 1, 1)
            n = len(DOWN_KS)

            def row_tile(k, par):
                act.wait_ge(S("y_turned"), k + 1)
                A(yrow[:, :, ds(k * P, P)], ps[:, 4 + par, :].rearrange("p (t f) -> p t f", f=P), ACT.Copy
                  ).then_inc(S("rows_turned"), 1)

            def down_round(i, last=False):
                for j in range(2 * n):
                    if not (last and j >= 2 * n - 2):
                        high(gDown, 2 + j, 2 * n * i + (gDown.n0 + 2 + j), landed(gDown, 2 + j, i, 2 * n), DOWN_KS[(2 + j) % n])
                    if j % n == n - 1:
                        if j // n or not isinstance(i, int) or i > 0:
                            row_tile(2 * i + j // n - 1, 1 - j // n)
                        square("n6", 2 * i + j // n, j // n, (s_ev, 2 * i + (gDown.b0 + j // n + 1)))
            peeled(act, KT // 2 - 1, down_round)
            down_round(KT // 2 - 1, True)
            row_tile(KT - 1, 1)
            act.wait_ge(S("rows_turned"), KT)
            act.wait_ge(*N("n6", "power", 1))
            for t in range(1, TB, 2):
                A(yrow[:, t, :], yrow[:, t, :], ACT.Copy, scale=rtok[:, 1, t:t + 1]).then_inc(S("rows_scaled1"), 1)

        @block.vector
        def _(dve):
            own = Steps(dve, S("vector_steps"))
            V = nc.vector

            def vcol(name, k=0):
                return vec[:, VEC[name] + k:VEC[name] + k + 1]

            def copies(ph, per, rounds, dst, first=0, after=0):
                def body(i):
                    for j in range(per):
                        n = per * i + (ph.n0 + first + j)
                        dve.wait_ge(s_mm, n + 1)
                        V.tensor_copy(dst(i, j), ps[:, ph.bank(first + j), :]).then_inc(s_ev, 1)
                repeat(dve, rounds, body)

            def add_square(name, k, j, at=0, acc=5):
                if isinstance(k, int) and k == 0:
                    return
                dve.wait_ge(*N(name, "squared", k + 1))
                if not isinstance(k, int) or k >= 2:
                    dve.wait_ge(*N(name, "added", k - 1))
                V.tensor_tensor(T[acc][:], T[acc][:], T[at + j][:], ALU.add).then_inc(N(name, "added", 0)[0], 1)

            def adds(ph, name, gate=None, per=1):
                def body(i):
                    for j in range(2):
                        dve.wait_ge(s_mm, 2 * per * i + (ph.n0 + per * (j + 1)))
                        x = xT[:, ds(2 * i + j, 1), :].rearrange("p a t -> p (a t)")
                        if gate is None:
                            V.tensor_tensor(x, ps[:, ph.bank(j), :], x, ALU.add).then_inc(s_ev, 1)
                        else:
                            V.scalar_tensor_tensor(x, ps[:, ph.bank(j), :], mod[:, ds(2 * i + (gate + j), 1)], x,
                                                   ALU.mult, ALU.add).then_inc(s_ev, 1)
                        add_square(name, 2 * i + j, j)
                return body

            def mean(name, bank=2, at=0):
                dve.wait_ge(*N(name, "summed", 1))
                V.tensor_scalar(rtok[:, at, :], ps[:, bank, 0:TB], 1.0 / D_MODEL, EPS, ALU.mult, ALU.add
                                ).then_inc(S("norm_mean"), 1)

            def norm_scaled(name, k, src, gain, by):
                V.scalar_tensor_tensor(T[2 + k % 4][:], src(k), gain(k), by, ALU.mult, ALU.mult
                                       ).then_inc(S("norm_scaled"), 1)

            def norm_split(name, tiles, src, gain, dstL, dstH, shift=None, bank=2):
                for k in range(tiles):
                    if k >= 2:
                        low(name, k - 2, dstL, dstH, shift)
                    if k >= 4:
                        dve.wait_ge(*N(name, "low", k - 3))
                    norm_scaled(name, k, src, gain, ps[:, bank, :])
                for k in range(tiles - 2, tiles):
                    low(name, k, dstL, dstH, shift)

            def norm_plain(src, gain, dst, by):
                for k in range(KT):
                    V.scalar_tensor_tensor(dst(k), src(k), gain(k), by, ALU.mult, ALU.mult).then_inc(S("norm_done"), 1)

            def norm_parts(name, *args, **kw):
                dve.wait_ge(*N(name, "spread", 1))
                norm_split(name, *args, **kw)

            def low(name, k, dstL, dstH, shift):
                dve.wait_ge(*N(name, "high", k + 1))
                t = T[2 + k % 4][:]
                if shift is None:
                    V.tensor_tensor(dstL(k), t, dstH(k).bitcast(F32), ALU.subtract).then_inc(S("norm_low"), 1)
                else:
                    V.scalar_tensor_tensor(dstL(k), t, shift(k), dstH(k).bitcast(F32), ALU.add, ALU.subtract
                                           ).then_inc(S("norm_low"), 1)

            for k in range(KT):
                if k % 2 == 0:
                    dve.wait_ge(S("x_transposed"), k + 1)
                    V.tensor_copy(xT[:, k, :], ps[:, 6, :]).then_inc(S("x_turned0"), 1)
                if k >= 2:
                    add_square("n1", k - 2, k % 2)
            add_square("n1", KT - 2, 0)
            add_square("n1", KT - 1, 1)
            for g, (at, n) in enumerate(VEC_ROWS):
                dve.wait_ge(S("vec_transposed"), g + 1)
                V.tensor_copy(vec[:, at:at + n], ps[:, 2 + g, 0:n]).then_inc(S("vecs_turned"), 1)
            dve.wait_ge(S("vecs_turned"), len(VEC_GROUPS))
            for par in range(2):
                dve.wait_ge(S(f"x_turned{par}"), KT // 2)
            mean("n1", 1)
            dve.wait_ge(S("tabs_made"), 1)
            dve.wait_ge(S("tables_loaded"), 64)
            for h in range(2):
                q = slice(h * TAB // 2, (h + 1) * TAB // 2)
                V.scalar_tensor_tensor(tabs[:, q], ps[0:2 * PAIRS, 3 + h, 0:TAB // 2], math.sqrt(HEAD_DIM), maskt[:, q],
                                       ALU.mult, ALU.add).then_inc(S("tabs_ready"), 1)
            norm_parts("n1", KT, lambda k: xT[:, k, :], lambda k: vcol("norm1_w", k), lambda k: actL[:, k, :],
                       lambda k: actH[:, k, :])
            copies(gB, 2, NB_B // 2, lambda i, j: bT[:, ds(2 * i + j, 1), :].rearrange("p a t -> p (a t)"))
            copies(gB, 1, 1, lambda i, j: bT[:, NB_B - 1, :], first=NB_B - 1)
            dve.wait_ge(s_ev, gB.b0 + NB_B)
            own.done(V.tensor_scalar(bT[:, 0, :], bT[:, 0, :], float(B_KEY ** -0.5), None, ALU.mult))
            dve.wait_ge(S("gla_z"), 1)
            V.tensor_scalar(T[0][:], ps[:, 2, :], vcol("gla_b_a"), 0.0, ALU.add, ALU.min).then_inc(S("gla_zmin"), 1)
            dve.wait_ge(S("gla_log"), 1)
            V.tensor_tensor(T[0][:], T[0][:], T[1][:], ALU.subtract).then_inc(S("gla_logsig"), 1)
            dve.wait_ge(S("gla_alpha"), 1)

            def gla_last_product(g, par):
                dve.wait_ge(S(f"gla_values{par}"), 32 * g + (64 - 32 * par))
                if not isinstance(g, int) or g > 0:
                    dve.wait_ge(S("gla_scanned"), GLA_GROUP * g)
                V.tensor_tensor(kvp[:, GLA_GROUP - 1, :], bT[:, 1, :], vb[:, par, GLA_GROUP - 1, :], ALU.mult
                                ).then_inc(S("gla_kv_last"), 1)

            def gla_scan(g, j):
                if j < GLA_GROUP - 1:
                    dve.wait_ge(S("gla_kv"), (GLA_GROUP - 1) * g + (j + 1))
                else:
                    dve.wait_ge(S("gla_kv_last"), g + 1)
                if not isinstance(g, int) or g > 0 or j >= 2:
                    dve.wait_ge(S("gla_read"), GLA_GROUP * g + (j - 1))
                V.tensor_tensor_scan(scanned[:, j % 2, :], alpha[:], kvp[:, j, :], 0.0, ALU.mult, ALU.add
                                     ).then_inc(S("gla_scanned"), 1)

            def gla_read(g, par, j):
                dve.wait_ge(S("gla_scanned"), GLA_GROUP * g + (j + 1))
                if not isinstance(g, int) or g >= 2:
                    dve.wait_ge(S("gla_summed"), GLA_GROUP * g + (j + 1 - 2 * GLA_GROUP))
                V.tensor_tensor(qs[:, par, j, :], scanned[:, j % 2, :], bT[:, 0, :], ALU.mult).then_inc(S("gla_read"), 1)

            def gla_round(i):
                for par in range(2):
                    g = 2 * i + par
                    gla_last_product(g, par)
                    gla_scan(g, 0)
                    gla_scan(g, 1)
                    for j in range(2, GLA_GROUP):
                        gla_read(g, par, j - 2)
                        gla_scan(g, j)
                    gla_read(g, par, GLA_GROUP - 2)
                    gla_read(g, par, GLA_GROUP - 1)
            peeled(dve, GLA_GROUPS // 2, gla_round)
            for b in range(2):
                dve.wait_ge(S("gla_tokens"), b + 1)
                for t in range(TB):
                    own.done(V.tensor_copy(
                        oTok[:, t, :].rearrange("p (h b u j) -> p b h u j", b=2, u=SUM_GROUPS, j=GLA_GROUP)[:, b],
                        ps[:, 2 + b, t * P:(t + 1) * P].rearrange("p (j u h) -> p h u j", j=GLA_GROUP, u=SUM_GROUPS)))
            own.done(V.tensor_tensor(oSq[:], oTok[:], oTok[:], ALU.mult))
            V.tensor_reduce(T[0][:, 0:TB * B_HEADS], oSq[:].rearrange("p t (h v) -> p (t h) v", v=B_VAL), AX_X, ALU.add
                            ).then_inc(S("gla_ms"), 1)
            dve.wait_ge(S("gla_root"), 1)
            own.done(V.reciprocal(T[0][:, 0:TB * B_HEADS], T[0][:, 0:TB * B_HEADS]))
            V.tensor_tensor(oTok[:].rearrange("p t (h v) -> p (t h) v", v=B_VAL),
                            oTok[:].rearrange("p t (h v) -> p (t h) v", v=B_VAL),
                            T[0][:, 0:TB * B_HEADS].unsqueeze(2).to_broadcast([P, TB * B_HEADS, B_VAL]), ALU.mult
                            ).then_inc(S("gla_normed"), 1)
            for e in range(2):
                dve.wait_ge(S("gla_turned"), e + 1)
                dve.wait_ge(S("gla_silu"), 1)
                dve.wait_ge(S("v_turned"), PAIRS)
                V.scalar_tensor_tensor(T[2 + e][:], ps[:, 5 + e, :], vcol("gla_norm_w", e), bT[:, 4 + e, :], ALU.mult, ALU.mult
                                       ).then_inc(S("gla_out"), 1)
            for e in range(2):
                dve.wait_ge(S("gla_high"), e + 1)
                k = 2 * A_W // P + e
                V.tensor_tensor(actL[:, k, :], T[2 + e][:], actH[:, k, :].bitcast(F32), ALU.subtract
                                ).then_inc(S("gla_low"), 1)

            S_BANK = (3, 4, 2, 3)

            def logits(pre, lp, s, par, i, z, scale):
                n, off = (i + 1) * P, i * (i + 1) // 2 * P
                dve.wait_ge(S(pre + "_scored"), 4 * s + (i + 1))
                dve.sem_inc(S("scores_seen"), 1)
                V.tensor_tensor_reduce(lp[:, par, off:off + n], ps[:, S_BANK[i], 0:n], z((TB - 1 - i) * P), -scale, BIG,
                                       ALU.add, ALU.min, stat[:, 0, par, i:i + 1]).then_inc(S(pre + "_logits"), 1)

            def normed(pre, lp, s, par, i):
                n, off = (i + 1) * P, i * (i + 1) // 2 * P
                dve.wait_ge(S(pre + "_exp"), 4 * s + (i + 1))
                own.done(V.reciprocal(stat[:, 2, par, i:i + 1], stat[:, 1, par, i:i + 1]))
                V.tensor_scalar(lp[:, par, off:off + n], lp[:, par, off:off + n], stat[:, 2, par, i:i + 1], None, ALU.mult
                                ).then_inc(S(pre + "_normed"), 1)

            def head(pre, lp, s, par, z, scale, after=None, between=None, at=None):
                for i in range(TB):
                    logits(pre, lp, s, par, i, z, scale)
                    if i > 0:
                        normed(pre, lp, s, par, i - 1)
                    if i == at:
                        between()
                normed(pre, lp, s, par, TB - 1)
                if after is not None:
                    after()

            def pair_low(pre, p, dstL, dstH):
                dve.wait_ge(S(pre + "_high"), p + 1)
                q = lambda t: t[:, ds(p, 1), :].rearrange("p a t -> p (a t)")
                V.tensor_tensor(q(dstL), ps[:, 7, :], q(dstH).bitcast(F32), ALU.subtract).then_inc(S(pre + "_low"), 1)

            SC_A = HEAD_DIM ** -0.5

            def a_head(s, par, p, **kw):
                dve.wait_ge(S(f"strip_loaded{par}"), 16 * p + 16)
                head("a", LP, s, par, lambda at: Z[:, par, at:SEQ], SC_A, **kw)
            a_head(0, 0, 0)
            a_head(1, 1, 0)

            def pair(p):
                own.enter(p, 2 * TB)
                a_head(2 * p + 2, 0, p + 1)
                a_head(2 * p + 3, 1, p + 1, between=lambda: pair_low("a", p, actL, actH), at=TB - 1)
            repeat(dve, PAIRS - 1, pair)
            own.leave(PAIRS - 1)
            pair_low("a", PAIRS - 1, actL, actH)
            peeled(dve, KT // 2, adds(gOut, "n2"))
            dve.wait_ge(s_ev, gOut.b0 + KT)
            mean("n2")
            norm_parts("n2", KT, lambda k: xT[:, k, :], lambda k: vcol("norm2_w", k), lambda k: actL[:, k, :],
                       lambda k: actH[:, k, :])
            dve.wait_ge(S("c_ready"), 1)
            sp0, sp1, sp2 = nsp[:, 0, :], nsp[:, 1, :], nsp[:, 2, :]
            dve.wait_ge(S("lru_exp"), 1)
            own.done(V.tensor_scalar(sp0, sp1, 2.0, None, ALU.add))
            own.done(V.reciprocal(sp0, sp0))
            own.done(V.tensor_tensor(sp1, sp1, sp0, ALU.mult))
            own.done(V.tensor_tensor(sp2, sp1, sp1, ALU.mult))
            own.done(V.tensor_scalar(sp0, sp2, 1.0 / LOG_TERMS[0], 1.0 / LOG_TERMS[1], ALU.mult, ALU.add))
            for term in LOG_TERMS[2:]:
                own.done(V.tensor_tensor(sp0, sp0, sp2, ALU.mult))
                own.done(V.tensor_scalar(sp0, sp0, 1.0 / term, None, ALU.add))
            own.done(V.scalar_tensor_tensor(sp1, sp1, 2.0, sp0, ALU.mult, ALU.mult))
            own.done(V.tensor_scalar(sp0, vec[:, VEC["lru_param_2"]:VEC["lru_param_2"] + RT], -1.0, 0.0,
                                     ALU.mult, ALU.max))
            own.done(V.tensor_tensor(sp0, sp0, sp1, ALU.add))
            own.done(V.tensor_scalar(sp0, sp0, -LRU_C, None, ALU.mult))

            def ada_chunk(o, gi, half, p, j, h):
                c = 4 * KT * o + 2 * p + (2 * KT * gi + KT * half + j)
                e = 2 * h + j
                nth = KT * o + (KT // 2 * gi + KT // 4 * half)
                q = (p - h) // 2 if isinstance(p, int) else None
                v = 16 * nth + (16 * q if q is not None else (p - h) * 8) + 16
                dve.wait_ge(S(f"ada_loaded{e}"), v)
                dve.wait_ge(S("ada_used"), c + 1)
                q = adaacc[:, ds(ADA_COLS * (4 * o + 2 * gi + half), ADA_COLS)]
                V.scalar_tensor_tensor(q, wada[:, e, :], cact[:, ds(2 * p + j, 1)], q, ALU.mult, ALU.add
                                       ).then_inc(S("ada_used"), 1)

            def by_two(body):
                return lambda q: (body(2 * q, 0), body(2 * q + 1, 1))

            def ff_group(o):
                for gi in range(2):
                    one, two = gFF[gi]

                    def first(p, h, one=one, gi=gi):
                        for j in range(2):
                            f = 2 * KT * o + 2 * p + (KT * gi + j)
                            dve.wait_ge(S("hid_relu"), f + 1)
                            if not isinstance(f, int) or f >= 2:
                                dve.wait_ge(S("hid_low"), f - 1)
                            V.tensor_tensor(T[2 + j][:], T[j][:], T[j][:], ALU.mult).then_inc(S("hid_squared"), 1)
                        for j in range(2):
                            f = 2 * KT * o + 2 * p + (KT * gi + j)
                            dve.wait_ge(S("hid_high"), f + 1)
                            u = lambda t: t[:, ds(2 * p + (KT * gi + j), 1), :].rearrange("p a t -> p (a t)")
                            V.tensor_tensor(u(UL), T[2 + j][:], u(UH).bitcast(F32), ALU.subtract).then_inc(S("hid_low"), 1)
                        for j in range(2):
                            ada_chunk(o, gi, 0, p, j, h)
                    (repeat if o or gi else peeled)(dve, KT // 4, by_two(first))

                    last = o == FF_GROUPS // 2 - 1 and gi == 1

                    def second(p, h, two=two, gi=gi, last=last):
                        for j in range(2):
                            dve.wait_ge(s_mm, 2 * FF_SLOTS * o + 2 * p + (two.n0 + j + 1))
                            x = xT[:, ds(2 * p + j, 1), :].rearrange("p a t -> p (a t)")
                            dve.wait_ge(S("x_added"), KT * (2 * o + gi)) if gi or not isinstance(o, int) or o else None
                            V.tensor_tensor(x, ps[:, two.bank(j), :], x, ALU.add).then_inc(S("x_added"), 1)
                            ada_chunk(o, gi, 1, p, j, h)
                            if last:
                                add_square("n3", 2 * p + j, j)
                                add_square("n4", 2 * p + j, j, 2, 4)
                    (peeled if last else repeat)(dve, KT // 4, by_two(second))
            ff_group(0)
            ff_group(1)
            dve.wait_ge(S("x_added"), KT * FF_GROUPS)
            mean("n3")
            dve.wait_ge(*N("n3", "power", 1))
            own.done(V.tensor_tensor(rtok[:, 2, :], rtok[:, 1, :], rtok[:, 1, :], ALU.mult))
            dve.wait_ge(*N("n4", "summed", 1))
            own.done(V.tensor_tensor(rtok[:, 2, :], ps[:, 4, 0:TB], rtok[:, 2, :], ALU.mult))
            V.tensor_scalar(rtok[:, 2, :], rtok[:, 2, :], 1.0 / D_MODEL, EPS, ALU.mult, ALU.add).then_inc(S("norm_mean"), 1)
            dve.wait_ge(S("ada_summed"), 2 * FF_GROUPS)
            own.done(V.tensor_tensor(mod[:], ps[:, 3, 0:6 * KT], vec[:, VEC["b_ada_2"]:VEC["b_ada_2"] + 6 * KT], ALU.add))
            own.done(V.scalar_tensor_tensor(gainA[:, 0, :], mod[:, KT:2 * KT], 1.0,
                                            vec[:, VEC["norm1_g_2"]:VEC["norm1_g_2"] + KT], ALU.add, ALU.mult))
            V.tensor_tensor(gainA[:, 0, :], gainA[:, 0, :], vec[:, VEC["final_norm_w"]:VEC["final_norm_w"] + KT], ALU.mult
                            ).then_inc(S("mod_ready"), 1)
            dve.wait_ge(S("mod_ready"), 1)
            dve.wait_ge(*N("n4", "power", 1))
            V.tensor_tensor(rtok[:, 3, :], rtok[:, 3, :], rtok[:, 1, :], ALU.mult).then_inc(S("n4_scale"), 1)
            dve.wait_ge(*N("n3", "spread", 1))
            norm_split("n4", KT, lambda k: xT[:, k, :], lambda k: gainA[:, 0, k:k + 1], lambda k: actL[:, k, :],
                       lambda k: actH[:, k, :], shift=lambda k: mod[:, k:k + 1], bank=4)
            dve.wait_ge(*N("n4", "spread", 1))
            own.done(V.tensor_copy(rstd[:], ps[:, 2, :]))
            V.scalar_tensor_tensor(gainA[:, 1, :], mod[:, 4 * KT:5 * KT], 1.0,
                                   vec[:, VEC["norm2_g_2"]:VEC["norm2_g_2"] + KT], ALU.add, ALU.mult
                                   ).then_inc(S("mod_ready"), 1)
            dve.wait_ge(S("mod_ready"), 2)
            def conv(t, j):
                dve.wait_ge(s_mm, t + (gX.n0 + j + 1))
                y = lambda a: xc[:, ds(t + j, 1), a:SEQ].rearrange("p a t -> p (a t)")
                w = lambda k: vec[:, ds(t + (VEC["conv_w_2"] + RT * k + j), 1)]
                own.done(V.tensor_scalar(y(0), ps[:, gX.bank(j), :], w(CONV_W - 1),
                                         vec[:, ds(t + (VEC["conv_b_2"] + j), 1)], ALU.mult, ALU.add))
                for k in range(1, CONV_W):
                    ins = V.scalar_tensor_tensor(y(k), ps[:, gX.bank(j), 0:SEQ - k], w(CONV_W - 1 - k), y(k),
                                                 ALU.mult, ALU.add)
                    if k < CONV_W - 1:
                        own.done(ins)
                    else:
                        ins.then_inc(s_ev, 1)

            def rnn_loga(t, j):
                dve.wait_ge(S("rnn_sig"), 2 * t + (2 * j + 2))
                V.scalar_tensor_tensor(T[j][:], T[j][:], nsp[:, 0, ds(t + j, 1)], T[4][:], ALU.mult, ALU.add
                                       ).then_inc(S("rnn_loga"), 1)

            def rnn_tiles(t):
                for j in range(2):
                    x = xc[:, ds(t + j, 1), :].rearrange("p a t -> p (a t)")
                    own.done(V.tensor_tensor(T[2 + j][:], T[2 + j][:], x, ALU.mult))
                for j in range(2):
                    dve.wait_ge(S("rnn_tanh"), t + (j + 1))
                    own.done(V.tensor_tensor(T[5][:], rA[:, j, :], rA[:, j, :], ALU.mult))
                    V.scalar_tensor_tensor(rTh[:, j, :], T[5][:], 1.0, rTh[:, j, :], ALU.add, ALU.mult
                                           ).then_inc(S("rnn_m2"), 1)
                    dve.wait_ge(S("rnn_m2"), t + (j + 1))
                for j in range(2):
                    dve.wait_ge(S("rnn_mult"), t + (j + 1))
                    own.done(V.tensor_tensor(rTh[:, j, :], rTh[:, j, :], T[2 + j][:], ALU.mult))
                    V.tensor_tensor_scan(T[j][:], rA[:, j, :], rTh[:, j, :], 0.0, ALU.mult, ALU.add
                                         ).then_inc(S("rnn_state"), 1)
                for j in range(2):
                    dve.wait_ge(S("rnn_high"), t + (j + 1))
                    u = lambda b: b[:, ds(t + j, 1), :].rearrange("p a t -> p (a t)")
                    V.tensor_tensor(u(UL), T[j][:], u(UH).bitcast(F32), ALU.subtract).then_inc(S("rnn_low"), 1)

            def x_round(p):
                own.enter(p, 2 * (CONV_W - 1))
                for j in range(2):
                    conv(2 * p, j)
            repeat(dve, RT // 2, x_round)
            own.leave(RT // 2)

            dve.wait_ge(S("reset_loaded"), 16)
            own.done(V.tensor_copy(T[4][:], posr[:]))
            own.done(V.tensor_scalar(T[4][:], T[4][:], 0.0, NEG, ALU.is_equal, ALU.mult))

            def rnn_round(p):
                own.enter(p, 6)
                for j in range(2):
                    rnn_loga(2 * p, j)
                rnn_tiles(2 * p)
            repeat(dve, RT // 2, rnn_round)
            own.leave(RT // 2)
            dve.wait_ge(S("rnn_low"), RT)
            norm_plain(lambda k: xT[:, k, :], lambda k: vcol("final_norm_w", k), lambda k: xT[:, k, :], rstd[:])

            def pr_round(i):
                for j in range(2):
                    dve.wait_ge(s_mm, 4 * i + (gPR.n0 + 2 * j + 2))
                    g = gR[:, ds(2 * i + j, 1), :].rearrange("p a t -> p (a t)")
                    V.tensor_tensor(g, ps[:, gPR.bank(j), :], g, ALU.mult).then_inc(s_ev, 1)
            dve.wait_ge(S("pos_loaded"), 16)
            c1 = 6.28125
            c2 = float(np.float32(2 * math.pi - c1) - np.float32(2 * math.pi - c1) % np.float32(2.0 ** -20))
            c3 = float(2 * math.pi - c1 - c2)
            rnd = float(1.5 * 2 ** 23)
            own.done(V.tensor_copy(rott[:], posb[:]))
            own.done(V.tensor_scalar(rott[:], rott[:], const[:, C_INVF:C_INVF + 1], None, ALU.mult))
            own.done(V.tensor_scalar(rotk[:], rott[:], float(1 / (2 * math.pi)), const[:, C_TURN:C_TURN + 1], ALU.mult, ALU.add))
            own.done(V.tensor_scalar(rotk[:], rotk[:], rnd, None, ALU.add))
            own.done(V.tensor_scalar(rotk[:], rotk[:], -rnd, None, ALU.add))
            for c in (c1, c2, c3):
                own.done(V.scalar_tensor_tensor(rott[:], rotk[:], -c, rott[:], ALU.mult, ALU.add))
            own.done(V.tensor_scalar(rott[:], rott[:], const[:, C_PHASE:C_PHASE + 1], 3.1415925, ALU.add, ALU.min))
            own.done(V.memset(CS[0:NOPE, :], 1.0))
            V.tensor_scalar(rott[:], rott[:], -3.1415925, None, ALU.max).then_inc(S("rot_angle"), 1)
            dve.wait_ge(S("rot_ready"), 1)
            copies(gLat, 2, (QT + KVT) // 2, lambda i, j: lat[:, ds(2 * i + j, 1), :].rearrange("p a t -> p (a t)"))
            copies(gLat, 1, 1, lambda i, j: lat[:, QT + KVT - 1, :], first=QT + KVT - 1)
            dve.wait_ge(*N("nq", "root", 1))
            own.done(V.reciprocal(rstd[:], rstd[:]))
            for k in range(QT):
                norm_scaled("nq", k, lambda k: lat[:, k, :], lambda k: vcol("q_norm_g_2", k), rstd[:])
            dve.wait_ge(*N("nkv", "root", 1))
            own.done(V.reciprocal(Vf[:], Vf[:]))
            for k in range(QT):
                low("nq", k, lambda k: actL[:, k, :], lambda k: actH[:, k, :], None)
            dve.wait_ge(*N("nq", "low", QT))
            for k in range(KVT):
                norm_scaled("nkv", k, lambda k: lat[:, QT + k, :], lambda k: vcol("kv_norm_g_2", k), Vf[:])
            dve.wait_ge(s_mm, gRope.n0 + 1)
            V.tensor_tensor(T[4][NOPE:P, :], ps[NOPE:P, gRope.bank(0), :], CS[NOPE:P, :], ALU.mult).then_inc(s_ev, 1)
            dve.wait_ge(s_ev, gRope.b0 + 1)
            own.done(V.tensor_copy(T[5][NOPE:QKD, :], T[4][QKD:P, :]))
            for par in range(2):
                own.done(V.tensor_tensor(Kp[NOPE:QKD, par, :], T[4][NOPE:QKD, :], T[5][NOPE:QKD, :], ALU.add))
                V.tensor_copy(Kp[QKD:P, par, :], Kp[NOPE:QKD, par, :]).then_inc(S("krot_ready"), 1)
            dve.wait_ge(S("krot_ready"), 2)
            for k in range(KVT):
                low("nkv", k, lambda k: actL[:, QT + k, :], lambda k: actH[:, QT + k, :], None)
            dve.wait_ge(S("gate_evacuated"), 2 * KT)
            repeat(dve, KT // 2, pr_round)

            def value_rows(s):
                dve.wait_ge(S("m_kv_made"), s + 1)
                if not isinstance(s, int) or s > 0:
                    dve.wait_ge(S("m_v_turned"), s)
                V.tensor_copy(Vf[NOPE:P, :], ps[NOPE:P, 1, :]).then_inc(S("m_v_rows"), 1)

            def query_evac(s, par):
                dve.wait_ge(s_mm, s + (gHead.n0 + 1))
                V.tensor_tensor(Qp[:, par, :], ps[:, 0, :], CS[:], ALU.mult).then_inc(S("m_q_ready"), 1)

            SC_M = QKD ** -0.5
            z_m = lambda at: strip[:, at:SEQ]
            value_rows(0)
            query_evac(0, 0)

            def ahead(s, par):
                return lambda: (value_rows(s), query_evac(s, par))
            head("m", LP2, 0, 0, z_m, SC_M, ahead(1, 1))

            def m_low(p):
                return dict(between=lambda: pair_low("m", p, UL, UH), at=1)

            def head_pair(p, low):
                head("m", LP2, 2 * p + 1, 1, z_m, SC_M, ahead(2 * p + 2, 0), **low)
                head("m", LP2, 2 * p + 2, 0, z_m, SC_M, ahead(2 * p + 3, 1))

            def later_pair(p):
                own.enter(p, 2 * TB)
                head_pair(p + 1, m_low(p))
            head_pair(0, {})
            repeat(dve, N_MLA // 2 - 2, later_pair)
            own.leave(N_MLA // 2 - 2)
            head("m", LP2, N_MLA - 1, 1, z_m, SC_M, **m_low(N_MLA // 2 - 2))
            pair_low("m", N_MLA // 2 - 1, UL, UH)

            def pm_round(i):
                for j in range(2):
                    dve.wait_ge(s_mm, 2 * i + (gPM.n0 + j + 1))
                    m = lambda t: t[:, ds(2 * i + j, 1), :].rearrange("p a t -> p (a t)")
                    if not isinstance(i, int) or i > 0:
                        dve.wait_ge(S("merged_low"), 2 * i + (j - 1))
                    V.tensor_tensor(T[j][:], ps[:, gPM.bank(j), :], m(gM), ALU.mult).then_inc(s_ev, 1)
                    dve.wait_ge(s_ev, 2 * i + (gPM.b0 + j + 1))
                    V.tensor_tensor(T[j][:], T[j][:], m(gR), ALU.add).then_inc(S("merged"), 1)
                for j in range(2):
                    m = lambda t: t[:, ds(2 * i + j, 1), :].rearrange("p a t -> p (a t)")
                    dve.wait_ge(S("merged_high"), 2 * i + (j + 1))
                    V.tensor_tensor(m(actL), T[j][:], m(actH).bitcast(F32), ALU.subtract).then_inc(S("merged_low"), 1)
            peeled(dve, KT // 2, pm_round)

            peeled(dve, KT // 2, adds(gOut2, "n5", 2 * KT))
            dve.wait_ge(s_ev, gOut2.b0 + KT)
            mean("n5")
            norm_parts("n5", KT, lambda k: xT[:, k, :], lambda k: gainA[:, 1, k:k + 1], lambda k: actL[:, k, :],
                       lambda k: actH[:, k, :], shift=lambda k: mod[:, 3 * KT + k:3 * KT + k + 1])

            def ffn_conv(t, j, h, dst, sem):
                dve.wait_ge(s_mm, 2 * t + (gUp.n0 + h + 1))
                w = lambda k: vec[:, ds(t + (VEC[f"ffn_conv_w{k}"] + FT * h), 1)]
                own.done(V.tensor_scalar(dst[:, j, :], ps[:, gUp.bank(h), :], w(FFN_CONV - 1),
                                         vec[:, ds(t + (VEC["ffn_conv_b_2"] + FT * h), 1)], ALU.mult, ALU.add))
                own.done(V.scalar_tensor_tensor(dst[:, j, 1:SEQ], ps[:, gUp.bank(h), 0:SEQ - 1], w(FFN_CONV - 2),
                                                dst[:, j, 1:SEQ], ALU.mult, ALU.add))
                V.scalar_tensor_tensor(dst[:, j, 2:SEQ], ps[:, gUp.bank(h), 0:SEQ - 2], w(FFN_CONV - 3),
                                       dst[:, j, 2:SEQ], ALU.mult, ALU.add).then_inc(S(sem), 1)

            def up_pair(t, j):
                ffn_conv(t, j, 0, cg, "up_gate")
                ffn_conv(t, j, 1, cv, "up_value")
                dve.wait_ge(S("up_value"), t + 1)
                dve.wait_ge(S("up_silu"), t + 1)
                V.tensor_tensor(act2[:, j, :], act2[:, j, :], cv[:, j, :], ALU.mult).then_inc(S("up_product"), 1)
                dve.wait_ge(S("up_high"), t + 1)
                u = lambda b: b[:, ds(t, 1), :].rearrange("p a t -> p (a t)")
                V.tensor_tensor(u(UL), act2[:, j, :], u(UH).bitcast(F32), ALU.subtract).then_inc(S("up_low"), 1)

            def up_round(p):
                own.enter(p, 8)
                up_pair(2 * p, 0)
                up_pair(2 * p + 1, 1)
            repeat(dve, FT // 2, up_round)
            own.leave(FT // 2)

            def down_round(i):
                for j in range(2):
                    k = 2 * i + j
                    dve.wait_ge(s_mm, 2 * len(DOWN_KS) * i + (gDown.n0 + len(DOWN_KS) * (j + 1)))
                    x = xT[:, ds(k, 1), :].rearrange("p a t -> p (a t)")
                    V.scalar_tensor_tensor(x, ps[:, gDown.bank(j), :], mod[:, ds(2 * i + (5 * KT + j), 1)], x,
                                           ALU.mult, ALU.add).then_inc(s_ev, 1)
                    dve.wait_ge(s_ev, 2 * i + (gDown.b0 + j + 1))
                    if not isinstance(i, int) or i > 0:
                        dve.wait_ge(S("y_turned"), k - 1)
                    V.tensor_scalar(yout[:, j, :], x, vec[:, ds(2 * i + (VEC["final_g_2"] + j), 1)], None, ALU.mult
                                    ).then_inc(S("y_scaled"), 1)
                    add_square("n6", k, j)
            peeled(dve, KT // 2, down_round)
            mean("n6")
            dve.wait_ge(S("rows_turned"), KT)
            dve.wait_ge(*N("n6", "power", 1))
            for t in range(0, TB, 2):
                V.tensor_scalar(yrow[:, t, :], yrow[:, t, :], rtok[:, 1, t:t + 1], None, ALU.mult
                                ).then_inc(S("rows_scaled0"), 1)

        @block.tensor
        def _(pe):
            MM = nc.tensor.matmul

            def three(o, wh, wl, ah, al, first, last):
                MM(o, wh, ah, start=first, stop=False)
                MM(o, wh, al, start=False, stop=False)
                return MM(o, wl, ah, start=False, stop=last)

            def block_product(ph, n, j, q, actin, k0, ready, evac, after=None):
                kts, last = ph.ks[q], q == len(ph.ks) - 1
                slot, bank = ph.slot(len(ph.ks) * j + q), ph.bank(j)
                pe.wait_ge(s_lo, n + 1)
                if q == 0:
                    for sem, v in evac:
                        pe.wait_ge(sem, v)
                for k in range(kts):
                    if ready is not None:
                        pe.wait_ge(*ready(k0 + k))
                    mm = three(ps[:, bank, :], WH[slot][:, k, :], WL[slot][:, k, :], actin(0, k0 + k), actin(1, k0 + k),
                               q == 0 and k == 0, last and k == kts - 1)
                    if k == kts - 1:
                        mm.then_inc(s_mm, 1)
                    if after is not None:
                        after(k)

            def free(b):
                return [(s_ev, b - 1)] if not isinstance(b, int) or b >= 2 else []

            def products(ph, per, rounds, actin, ready=None, first=0, evac=free):
                nk = len(ph.ks)

                def body(i):
                    for j in range(per):
                        k0 = 0
                        for q in range(nk):
                            block_product(ph, per * nk * i + (ph.n0 + nk * (first + j) + q), first + j, q, actin, k0,
                                          ready if j == 0 else None, evac(per * i + (ph.b0 + first + j)))
                            k0 += ph.ks[q]
                repeat(pe, rounds, body)

            x_in = lambda part, k: (actH, actL)[part][:, k, :]

            def mean_square(name, tiles, bank=2):
                for k in range(tiles):
                    pe.wait_ge(*N(name, "squared", k + 1))
                    MM(ps[:, bank, :], ones[:], T[k % 2][:], start=(k == 0), stop=(k == tiles - 1)
                       ).then_inc(S("norm_summed"), 1)

            def norm_sum(name, acc=5, bank=2):
                pe.wait_ge(*N(name, "added", KT - 1))
                for t in range(TB):
                    mm = MM(ps[:, bank, t:t + 1], T[acc][:, t * P:(t + 1) * P], ones[:, 0:1], start=True, stop=True)
                mm.then_inc(S("norm_summed"), 1)

            def spread(name, ready, bank=2, at=1):
                pe.wait_ge(*ready)
                for t in range(TB):
                    mm = MM(ps[:, bank, t * P:(t + 1) * P], rtok[:, at, t:t + 1].to_broadcast([P, P]), ident,
                            start=True, stop=True)
                mm.then_inc(S("norm_spread"), 1)

            def keep_clock(n, bank=7):
                for _ in range(n):
                    MM(ps[:, bank, 0:P], ident, ones[:], start=True, stop=True)

            def norm_factors(name):
                keep_clock(13)
                norm_sum(name)
                keep_clock(5)
                spread(name, N(name, "power", 1))
                keep_clock(7)

            def pair_product(ph, n, actin, ready, evac, order=range(KT), lag=KT):
                for step in range(KT + lag):
                    for j, at in ((0, step), (1, step - lag)):
                        if not 0 <= at < KT:
                            continue
                        if at == 0:
                            pe.wait_ge(s_lo, n + j + 1)
                            for sem, v in evac(j):
                                pe.wait_ge(sem, v)
                        k = order[at]
                        if j == 0:
                            pe.wait_ge(*ready(k))
                        mm = three(ps[:, ph.bank(j), :], WH[ph.slot(j)][:, k, :], WL[ph.slot(j)][:, k, :], actin(0, k),
                                   actin(1, k), at == 0, at == KT - 1)
                        if at == KT - 1:
                            mm.then_inc(s_mm, 1)

            pe.wait_ge(S("const_loaded"), 16)
            for k in range(KT):
                pe.wait_ge(S(f"x_loaded{k // (KT // 2)}"), 16)
                if k >= 2:
                    pe.wait_ge(S(f"x_turned{k % 2}"), k // 2)
                for t in range(TB):
                    mm = nc.tensor.transpose(ps[:, 6 + k % 2, t * P:(t + 1) * P], xn[:, t, k * P:(k + 1) * P], ident)
                mm.then_inc(S("x_transposed"), 1)
            pe.wait_ge(S("vec_loaded"), 16 * sum(len(g) for g in VEC_GROUPS))
            for g, (at, n) in enumerate(VEC_ROWS):
                nc.tensor.transpose(ps[:, 2 + g, 0:n], vrows[0:n, g, :], ident[0:n, 0:n]).then_inc(S("vec_transposed"), 1)
            pe.wait_ge(S("ones_set"), 1)
            norm_sum("n1", bank=1)
            pe.wait_ge(S("tables_loaded"), 64)
            pe.wait_ge(S("vecs_turned"), len(VEC_GROUPS))
            for h in range(2):
                mm = MM(ps[0:2 * PAIRS, 3 + h, 0:TAB // 2], relb[:], onehot[:, h * TAB // 2:(h + 1) * TAB // 2],
                        start=True, stop=True)
            mm.then_inc(S("tabs_made"), 1)
            spread("n1", N("n1", "power", 1))
            n1 = lambda k: N("n1", "low", k + 1)
            pair_product(gB, gB.n0, x_in, n1, lambda j: [], lag=LAG)
            products(gB, 2, NB_B // 2 - 1, x_in, first=2)
            products(gB, 1, 1, x_in, first=NB_B - 1)
            pe.wait_ge(s_ev, gB.b0 + NB_B)
            MM(ps[:, 2, :], wa2[:], bT[0:B_RANK, NB_B - 1, :], start=True, stop=True).then_inc(S("gla_z"), 1)

            def gla_sums(g, par):
                bank, u = 2 + g // SUM_GROUPS, g % SUM_GROUPS

                def after(k):
                    if k != KT // 2:
                        return
                    for j in range(GLA_GROUP):
                        pe.wait_ge(S("gla_read"), GLA_GROUP * g + (j + 1))
                        mm = MM(ps[SUM_ROWS * j:SUM_ROWS * (j + 1), bank, :], headsum(u), qs[:, par, j, :],
                                start=(u == 0), stop=(u == SUM_GROUPS - 1))
                    mm.then_inc(S("gla_summed"), GLA_GROUP)
                return after

            def turn_sums(b):
                pe.wait_ge(S("gla_out_of_psum"), b + 1)
                for t in range(TB):
                    mm = nc.tensor.transpose(ps[:, 2 + b, t * P:(t + 1) * P], T[b][:, t * P:(t + 1) * P], ident)
                mm.then_inc(S("gla_tokens"), 1)

            products(gQK, 2, 1, x_in)

            def qk_round(i):
                for j in range(2):
                    block_product(gQK, 2 * i + (gQK.n0 + 2 + j), j, 0, x_in, 0, None, free(2 * i + (gQK.b0 + 2 + j)),
                                  gla_sums(2 * i + j, j))
            for i in range(PAIRS - 1):
                qk_round(i)

            def turn_values(v):
                pe.wait_ge(s_ev, gV.b0 + v + 1)
                if v >= 2:
                    pe.wait_ge(S("values_turned"), v - 1)
                for t in range(TB):
                    q = slice(t * P, (t + 1) * P)
                    mm = nc.tensor.transpose(ps[:, 5 + v % 2, q], T[2 + v % 2][:, q], ident)
                mm.then_inc(S("v_turned"), 1)

            for v in range(PAIRS):
                block_product(gV, gV.n0 + v, v, 0, x_in, 0, None, free(gV.b0 + v), gla_sums(2 * PAIRS - 2 + v, v % 2))
                if v:
                    turn_values(v - 1)
                if v == 1:
                    turn_sums(0)
            turn_values(PAIRS - 1)
            turn_sums(1)
            pe.wait_ge(S("gla_normed"), 1)
            for e in range(2):
                for t in range(TB):
                    mm = nc.tensor.transpose(ps[:, 5 + e, t * P:(t + 1) * P], oTok[:, t, e * P:(e + 1) * P], ident)
                mm.then_inc(S("gla_turned"), 1)

            S_BANK = (3, 4, 2, 3)

            def scores(pre, s, i, q, k):
                n = (i + 1) * P
                if i == TB - 1:
                    pe.wait_ge(S(pre + "_logits"), 4 * s + 1)
                elif not isinstance(s, int) or s > 0:
                    pe.wait_ge(S(pre + "_logits"), 4 * s)
                MM(ps[:, S_BANK[i], 0:n], q(i), k(n), start=True, stop=True).then_inc(S(pre + "_scored"), 1)

            def turn(pre, lp, s, par, i, weighed):
                off = i * (i + 1) // 2 * P
                pe.wait_ge(S(pre + "_normed"), 4 * s + (i + 1))
                if i >= 2 or not weighed and not (isinstance(s, int) and s == 0):
                    pe.wait_ge(S(pre + "_pt"), 4 * s + (i - 1))
                for k in range(i + 1):
                    mm = nc.tensor.transpose(ps[:, 5 + i % 2, k * P:(k + 1) * P],
                                             lp[:, par, off + k * P:off + (k + 1) * P], ident)
                mm.then_inc(S(pre + "_turned"), 1)

            def weigh(pre, pt, s, par, p, v):
                pe.wait_ge(S(pre + "_pt"), 4 * s + 4)
                if par == 0 and not (isinstance(p, int) and p == 0):
                    pe.wait_ge(S(pre + "_low"), p)
                for k in range(TB):
                    mm = MM(ps[HEAD_DIM * par:HEAD_DIM * (par + 1), 7, k * P:SEQ], v(k), pt[:, k, k * P:SEQ],
                            start=(k == 0), stop=(k == TB - 1))
                mm.then_inc(S(pre + "_weighted"), 1)

            def a_weigh(s, par, p):
                pe.wait_ge(S("a_v_staged"), s + 1)
                weigh("a", PT[:, par], s, par, p, lambda k: Vs[:, k, HEAD_DIM * par:HEAD_DIM * (par + 1)])

            def a_step(s, par, p=None):
                q = slice(HEAD_DIM * par, HEAD_DIM * (par + 1))
                pe.wait_ge(S("a_qk_staged"), 2 * s + 2)
                for i in range(TB):
                    scores("a", s, i, lambda i: Qs[q, i * P:(i + 1) * P], lambda n: Ks[q, 0:n])
                    if not (isinstance(s, int) and s == 0):
                        turn("a", LP, s - 1, 1 - par, i, False)
                    if i == 1 and p is not None:
                        a_weigh(s - 2, par, p)

            a_step(0, 0)
            a_step(1, 1)

            def a_pair(p):
                a_step(2 * p + 2, 0, p)
                a_step(2 * p + 3, 1, p)
            repeat(pe, PAIRS - 1, a_pair)
            for i in range(TB):
                turn("a", LP, 2 * PAIRS - 1, 1, i, False)
                if i == 1:
                    a_weigh(2 * PAIRS - 2, 0, PAIRS - 1)
            a_weigh(2 * PAIRS - 1, 1, PAIRS - 1)
            pair_product(gOut, gOut.n0, x_in, lambda k: (S("a_low"), k + 1) if k < PAIRS else (S("gla_low"), k + 1 - PAIRS),
                         lambda j: free(gOut.b0 + j), [*range(PAIRS, KT), *range(PAIRS)])
            products(gOut, 2, KT // 2 - 1, x_in, first=2)
            norm_factors("n2")
            n2 = lambda k: N("n2", "low", k + 1)

            def ada_sums(f):
                pe.wait_ge(S("ada_used"), 1 + KT * (f + 1))
                for m in range(f * ADA_COLS // P, (f + 1) * ADA_COLS // P):
                    mm = MM(ps[:, 3, m:m + 1], adaacc[:, m * P:(m + 1) * P], ones[:, 0:1], start=True, stop=True)
                mm.then_inc(S("ada_summed"), 1)

            def ff_group(o):
                for gi in range(2):
                    one, two = gFF[gi]
                    hid = lambda part, k, gi=gi: (UH, UL)[part][:, KT * gi + k, :]

                    blocks = KT * (2 * o + gi)
                    n = 2 * FF_SLOTS * o

                    def first(p, one=one, blocks=blocks, n=n):
                        for j in range(2):
                            block_product(one, 2 * p + (n + one.n0 + j), j, 0, x_in, 0, None,
                                          [(S("hid_relu"), 2 * p + (blocks + j - 1))])
                    pair_product(one, n + one.n0, x_in, n2, lambda j: [(S("x_added"), blocks - 1 + j) if blocks
                                                                       else (s_ev, gOut.b0 + KT - 1 + j)],
                                 lag=KT if blocks else LAG)
                    if blocks:
                        ada_sums(blocks // KT * 2 - 1)
                    repeat(pe, KT // 2 - 1, lambda p: first(p + 1))

                    def second(p, two=two, hid=hid, blocks=blocks, n=n):
                        for j in range(2):
                            block_product(two, 2 * p + (n + two.n0 + j), j, 0, hid, 0, None,
                                          [(S("x_added"), 2 * p + (blocks + j - 1))])
                    pair_product(two, n + two.n0, hid, lambda k: (S("hid_low"), blocks + k + 1),
                                 lambda j: [(S("hid_relu"), blocks + KT - 1 + j)])
                    ada_sums(blocks // KT * 2)
                    repeat(pe, KT // 2 - 1, lambda p: second(p + 1))
            ff_group(0)
            ff_group(1)
            keep_clock(13)
            norm_sum("n3")
            norm_sum("n4", 4, 4)
            ada_sums(2 * FF_GROUPS - 1)
            spread("n4", (S("n4_scale"), 1), 4, 3)
            spread("n3", N("n3", "power", 1))
            keep_clock(7)
            n4 = lambda k: N("n4", "low", k + 1)
            pair_product(gX, gX.n0, x_in, n4, lambda j: [(S("x_added"), KT * FF_GROUPS - 1 + j)], lag=LAG)
            products(gX, 2, RT // 2 - 1, x_in, first=2)

            def rnn_gate(t, j):
                pe.wait_ge(S(f"rnn_weights{j}"), t * 32 + 64)
                pe.wait_ge(s_ev, t + (gX.b0 + j + 1))
                if not isinstance(t, int) or t > 0:
                    pe.wait_ge(S("rnn_sig"), 2 * t + (2 * j - 2))
                x = xc[:, ds(t + j, 1), :].rearrange("p a t -> p (a t)")
                MM(ps[:, 2 + 2 * j, :], BDa[:, j, :], x, start=True, stop=True)
                MM(ps[:, 3 + 2 * j, :], BDx[:, j, :], x, start=True, stop=True).then_inc(S("rnn_gated"), 1)

            def gate_round(i, rnn):
                for j in range(2):
                    if isinstance(i, int) and i == 0:
                        prev = [(s_ev, gX.b0 + RT - 1 + j)]
                    else:
                        prev = [(S("gate_evacuated"), 2 * i + (j - 1))]
                    block_product(gGate, 2 * i + (gGate.n0 + j), j, 0, x_in, 0, None, prev)
                    if rnn:
                        rnn_gate(2 * i, j)
            pairs = RT // 2
            peeled(pe, pairs, lambda i: gate_round(i, True))
            repeat(pe, KT - pairs, lambda i: gate_round(i + pairs, False))
            y_in = lambda part, k: (UH, UL)[part][:, k, :]
            pe.wait_ge(S("gate_evacuated"), 2 * KT)
            seen = lambda b: [(s_ev, b - 1)]
            products(gLat, 2, (QT + KVT) // 2, x_in, evac=seen)
            products(gLat, 1, 1, x_in, first=QT + KVT - 1, evac=seen)
            mean_square("nq", QT)
            products(gRope, 1, 1, x_in, evac=seen)
            mean_square("nkv", KVT, 3)
            pe.wait_ge(S("rnn_low"), RT)
            products(gPR, 2, KT // 2, y_in, evac=seen)
            pe.wait_ge(*N("nkv", "low", KVT))
            pe.wait_ge(s_ev, gPR.b0 + KT)

            def head_products(s, par):
                pe.wait_ge(s_lo, s + (gHead.n0 + 1))
                slot = gHead.slot(par)
                if not isinstance(s, int) or s > 0:
                    pe.wait_ge(S("m_v_ready"), s)
                for k in range(KVT):
                    mm = three(ps[:, 1, :], WH[slot][:, QT + k, :], WL[slot][:, QT + k, :], actH[:, QT + k, :], actL[:, QT + k, :],
                               k == 0, k == KVT - 1)
                mm.then_inc(S("m_kv_made"), 1)
                if not isinstance(s, int) or s > 0:
                    pe.wait_ge(S("m_q_ready"), s)
                for k in range(QT):
                    mm = three(ps[:, 0, :], WH[slot][:, k, :], WL[slot][:, k, :], actH[:, k, :], actL[:, k, :],
                               k == 0, k == QT - 1)
                mm.then_inc(s_mm, 1)

            def head_values(s):
                pe.wait_ge(S("m_k_ready"), s + 1)
                pe.wait_ge(S("m_v_rows"), s + 1)
                for t in range(TB):
                    mm = MM(ps[:, 1, t * VH:(t + 1) * VH], Vf[NOPE:P, t * P:(t + 1) * P], ident[NOPE:P, NOPE:P],
                            start=True, stop=True)
                mm.then_inc(S("m_v_turned"), 1)

            def m_weigh(s, par, p):
                pe.wait_ge(S("m_v_ready"), s + 1)
                weigh("m", PT2, s, par, p, lambda k: Vp[:, par, k, :])

            def m_head(s, par, p=None, more=True):
                pe.wait_ge(S("m_q_ready"), s + 1)
                pe.wait_ge(S("m_k_ready"), s + 1)
                for i in range(TB):
                    scores("m", s, i, lambda i: Qp[:, par, i * P:(i + 1) * P], lambda n: Kp[:, par, 0:n])
                    if p is not None:
                        turn("m", LP2, s - 1, 1 - par, i, True)
                if more:
                    head_products(s + 1, 1 - par)
                if p is not None:
                    m_weigh(s - 1, 1 - par, p)
                if more:
                    head_values(s + 1)

            pe.wait_ge(S("krot_ready"), 2)
            head_products(0, 0)
            head_values(0)
            m_head(0, 0)

            def m_pair(p):
                m_head(2 * p + 1, 1, p)
                m_head(2 * p + 2, 0, p)
            repeat(pe, N_MLA // 2 - 1, m_pair)
            m_head(N_MLA - 1, 1, N_MLA // 2 - 1, more=False)
            for i in range(TB):
                turn("m", LP2, N_MLA - 1, 1, i, True)
            m_weigh(N_MLA - 1, 1, N_MLA // 2 - 1)
            keep_clock(11, 3)
            pair_product(gPM, gPM.n0, y_in, lambda k: (S("m_low"), k + 1),
                         lambda j: [(S("m_q_ready"), N_MLA), (S("m_v_ready"), N_MLA)])
            products(gPM, 2, KT // 2 - 1, y_in, first=2, evac=seen)
            pair_product(gOut2, gOut2.n0, x_in, lambda k: (S("merged_low"), k + 1), lambda j: seen(gOut2.b0 + j))
            products(gOut2, 2, KT // 2 - 1, x_in, first=2, evac=seen)
            norm_factors("n5")

            def up_round(p):
                for h in range(2):
                    block_product(gUp, 2 * p + (gUp.n0 + h), h, 0, x_in, 0, None, [(S(("up_gate", "up_value")[h]), p)])
            pair_product(gUp, gUp.n0, x_in, lambda k: N("n5", "low", k + 1), lambda j: [(s_ev, gOut2.b0 + KT - 1 + j)],
                         lag=LAG)
            repeat(pe, FT - 1, lambda p: up_round(p + 1))

            def turn_rows(k, par):
                pe.wait_ge(S("y_scaled"), k + 1)
                if not isinstance(k, int) or k >= 2:
                    pe.wait_ge(S("rows_turned"), k - 1)
                for t in range(TB):
                    mm = nc.tensor.transpose(ps[:, 4 + par, t * P:(t + 1) * P], yout[:, par, t * P:(t + 1) * P], ident)
                mm.then_inc(S("y_turned"), 1)

            def down_round(i):
                n = len(DOWN_KS)
                for j in range(2):
                    b = 2 * i + (gDown.b0 + j)
                    for q in range(n):
                        block_product(gDown, 2 * n * i + (gDown.n0 + n * j + q), j, q, y_in, sum(DOWN_KS[:q]),
                                      (lambda k: (S("up_low"), k + 1)) if j == 0 and isinstance(i, int) else None,
                                      [(s_ev, b - 1), (S(("up_gate", "up_value")[j]), FT)])
                        if q == 0 and (j or not isinstance(i, int)):
                            turn_rows(2 * i + j - 1, 1 - j)
            peeled(pe, KT // 2, down_round)
            turn_rows(KT - 1, 1)
            norm_sum("n6")


INPUTS = ["x", "norm1_w", "w_in", "gla_w_a2", "gla_b_a", "gla_norm_w", "w_out", "norm2_w", "w_ff1", "w_ff2", "rel_bias",
          "final_norm_w", "c_2", "positions_2", "w_ada_2", "b_ada_2", "norm1_g_2", "w_in_2", "conv_w_2", "conv_b_2",
          "w_gate_a_2", "b_gate_a_2", "w_gate_x_2", "b_gate_x_2", "lru_param_2", "q_norm_g_2", "w_uq_2", "kv_norm_g_2",
          "w_ukv_2", "w_proj_rnn_2", "w_proj_mla_2", "w_out_2", "norm2_g_2", "w_up_2", "ffn_conv_w_2", "ffn_conv_b_2",
          "w_down_2", "final_g_2"]
WITHOUT_LAYERS = {"x", "rel_bias", "final_norm_w", "positions_2", "final_g_2"}


def kernel(**inputs):
    import concourse.bacc as bacc
    from concourse.bass_utils import run_bass_kernel_spmd

    nc = bacc.Bacc("TRN2", target_bir_lowering=False, num_devices=1)
    arrays, io = {}, {}

    def give(name, a):
        a = np.ascontiguousarray(a)
        arrays[f"in_{name}"] = a
        ap = nc.dram_tensor(f"in_{name}", a.shape, mybir.dt.from_np(a.dtype), kind="ExternalInput").ap()
        io[name] = ap if name in WITHOUT_LAYERS or name.startswith("const") else ap[0]

    for name in INPUTS:
        give(name, inputs[name])
    for name, a in shape_constants().items():
        give(name, a)
    out = nc.dram_tensor("out", (1, SEQ, D_MODEL), F32, kind="ExternalOutput").ap()
    hybrid_stack(nc, io, out)
    r = run_bass_kernel_spmd(nc, [arrays], core_ids=[0])
    return r.results[0]["out"]
```
